# Optimizing a Trainium2 kernel written in Bass

```python
import jax, jax.numpy as jnp
from jax import lax
import numpy as np

D_MODEL = 1024
BATCH = 1
SEQ = 256
DEPTH = 1
DEC_BATCH = 8
DEC_SEQ = 1
PAST_LEN = 1024
PAGE_SIZE = 128

D_MIX = D_MODEL
HEAD_DIM = 64
POOL_WIDTH = D_MIX // 4
POOL_WINDOWS = (2, 4, 8, 16)
POOL_GROUP = POOL_WIDTH // len(POOL_WINDOWS)
POOL_BUF = max(POOL_WINDOWS) - 1
MOBA_WIDTH = D_MIX // 2
MOBA_HEADS = MOBA_WIDTH // HEAD_DIM
MOBA_BLOCK = 256
MOBA_TOPK = 3
MOBA_Q_CHUNK = 32
MEM_WIDTH = D_MIX - POOL_WIDTH - MOBA_WIDTH
MEM_HEADS = MEM_WIDTH // HEAD_DIM
MEM_LEN = 256
ROT_DIM = HEAD_DIM // 4
ROPE_THETA = 500000.0
D_FF = 2816
RMS_EPS = 1e-6
IN_COLS = POOL_WIDTH + 3 * MOBA_WIDTH + MEM_WIDTH

kernel_name = "hymba_pool_moba_memxattn_macaron_step"

def rmsnorm(x, g):
    xf = x.astype(jnp.float32)
    y = xf * lax.rsqrt(jnp.mean(xf * xf, axis=-1, keepdims=True) + RMS_EPS)
    return (y * g.astype(jnp.float32)).astype(x.dtype)

def rotary(x, pos):
    half = ROT_DIM // 2
    inv = jnp.power(jnp.float32(ROPE_THETA), -jnp.arange(half, dtype=jnp.float32) * (2.0 / ROT_DIM))
    ang = pos.astype(jnp.float32)[:, None] * inv[None, :]
    cos = jnp.cos(ang)[None, :, None, :]
    sin = jnp.sin(ang)[None, :, None, :]
    xr = x[..., :ROT_DIM].astype(jnp.float32)
    x1, x2 = xr[..., :half], xr[..., half:]
    rot = jnp.concatenate([x1 * cos - x2 * sin, x2 * cos + x1 * sin], axis=-1).astype(x.dtype)
    return jnp.concatenate([rot, x[..., ROT_DIM:]], axis=-1)

def swiglu_ffn(x, g, w_in, w_out):
    gate, up = jnp.split(rmsnorm(x, g) @ w_in, 2, axis=-1)
    return (jax.nn.silu(gate) * up) @ w_out

def pool_mixer(u, buf, pos, pool_w, pool_scale):
    B, T, C = u.shape
    ext = jnp.concatenate([buf, u], axis=1).astype(jnp.float32)
    cs = jnp.concatenate([jnp.zeros((B, 1, C), jnp.float32), jnp.cumsum(ext, axis=1)], axis=1)
    end = cs[:, POOL_BUF + 1:]
    means = []
    for gi, w in enumerate(POOL_WINDOWS):
        sl = slice(gi * POOL_GROUP, (gi + 1) * POOL_GROUP)
        start = cs[:, POOL_BUF + 1 - w: POOL_BUF + 1 - w + T, sl]
        cnt = jnp.minimum(w, pos + 1).astype(jnp.float32)[None, :, None]
        means.append((end[..., sl] - start) / cnt)
    pooled = (jnp.concatenate(means, axis=-1) - ext[:, POOL_BUF:]).astype(u.dtype)
    pg = pooled.reshape(B, T, len(POOL_WINDOWS), POOL_GROUP)
    y = jnp.einsum("btgc,gcd->btgd", pg, pool_w).reshape(B, T, C) * pool_scale
    new_buf = ext[:, -POOL_BUF:].astype(u.dtype)
    return y, new_buf

def moba_attention(q, k, v, q_pos):
    B, Q, H, Dh = q.shape
    L = k.shape[1]
    nb = max(-(-L // MOBA_BLOCK), MOBA_TOPK)
    pad = nb * MOBA_BLOCK - L
    kb = jnp.pad(k, ((0, 0), (0, pad), (0, 0), (0, 0))).reshape(B, nb, MOBA_BLOCK, H, Dh)
    vb = jnp.pad(v, ((0, 0), (0, pad), (0, 0), (0, 0))).reshape(B, nb, MOBA_BLOCK, H, Dh)
    kmean = jnp.mean(kb.astype(jnp.float32), axis=2)
    qc = min(MOBA_Q_CHUNK, Q)
    n_ch = -(-Q // qc)
    qpad = n_ch * qc - Q
    qs = jnp.pad(q, ((0, 0), (0, qpad), (0, 0), (0, 0))).reshape(B, n_ch, qc, H, Dh).transpose(1, 0, 2, 3, 4)
    ps = jnp.pad(q_pos, (0, qpad), mode="edge").reshape(n_ch, qc)
    bi = jnp.arange(B)[:, None, None]
    hi = jnp.arange(H)[None, :, None]
    blk_pos = jnp.arange(MOBA_BLOCK, dtype=jnp.int32)
    scale = Dh ** -0.5

    def one_chunk(args):
        qch, pch = args
        qf = qch.astype(jnp.float32)
        own = pch // MOBA_BLOCK
        s = jnp.einsum("bqhd,bnhd->bhqn", qf, kmean)
        fully_past = jnp.arange(nb)[None, :] < own[:, None]
        s = jnp.where(fully_past[None, None], s, -jnp.inf)
        top_s, top_i = lax.top_k(s, MOBA_TOPK)
        idx = jnp.concatenate([top_i, jnp.broadcast_to(own[None, None, :, None], (B, H, qc, 1))], axis=-1)
        masks = [jnp.isfinite(top_s[..., i])[..., None] for i in range(MOBA_TOPK)]
        own_pos = own[:, None] * MOBA_BLOCK + blk_pos[None, :]
        masks.append((own_pos <= pch[:, None])[None, None])
        logits = []
        for i in range(MOBA_TOPK + 1):
            ks = kb[bi, idx[..., i], :, hi].astype(jnp.float32)
            lg = jnp.einsum("bqhd,bhqkd->bhqk", qf, ks) * scale
            logits.append(jnp.where(masks[i], lg, -jnp.inf))
        p = jax.nn.softmax(jnp.concatenate(logits, axis=-1), axis=-1)
        p = p.reshape(B, H, qc, MOBA_TOPK + 1, MOBA_BLOCK)
        out = sum(jnp.einsum("bhqk,bhqkd->bqhd", p[:, :, :, i], vb[bi, idx[..., i], :, hi].astype(jnp.float32))
                  for i in range(MOBA_TOPK + 1))
        return out.astype(q.dtype)

    out = lax.map(one_chunk, (qs, ps))
    return out.transpose(1, 0, 2, 3, 4).reshape(B, n_ch * qc, H, Dh)[:, :Q]

def mem_attention(q, mk, mv):
    lg = jnp.einsum("bthd,bmhd->bhtm", q.astype(jnp.float32), mk.astype(jnp.float32)) * (HEAD_DIM ** -0.5)
    p = jax.nn.softmax(lg, axis=-1)
    return jnp.einsum("bhtm,bmhd->bthd", p, mv.astype(jnp.float32)).astype(q.dtype)

def mem_kv(mem, mem_norm, mem_w_kv, mem_k_norm):
    B, M, _ = mem.shape
    mk, mv = jnp.split(rmsnorm(mem, mem_norm) @ mem_w_kv, 2, axis=-1)
    mk = rmsnorm(mk.reshape(B, M, MEM_HEADS, HEAD_DIM), mem_k_norm)
    return mk, mv.reshape(B, M, MEM_HEADS, HEAD_DIM)

def trunk_layer(x, pos, k_past, v_past, pool_buf, mk, mv,
                ffn1_norm, ffn1_w_in, ffn1_w_out, mix_norm, w_in, pool_w, pool_scale,
                q_norm, k_norm, mem_q_norm, w_out, ffn2_norm, ffn2_w_in, ffn2_w_out):
    B, T, _ = x.shape
    x = x + 0.5 * swiglu_ffn(x, ffn1_norm, ffn1_w_in, ffn1_w_out)
    h = rmsnorm(x, mix_norm)
    proj = h @ w_in
    c1 = POOL_WIDTH
    c2 = c1 + MOBA_WIDTH
    c3 = c2 + MOBA_WIDTH
    c4 = c3 + MOBA_WIDTH
    u, q, k, v, qm = proj[..., :c1], proj[..., c1:c2], proj[..., c2:c3], proj[..., c3:c4], proj[..., c4:]
    y_pool, new_buf = pool_mixer(u, pool_buf, pos, pool_w, pool_scale)
    q = rotary(rmsnorm(q.reshape(B, T, MOBA_HEADS, HEAD_DIM), q_norm), pos)
    k = rotary(rmsnorm(k.reshape(B, T, MOBA_HEADS, HEAD_DIM), k_norm), pos)
    v = v.reshape(B, T, MOBA_HEADS, HEAD_DIM)
    k_all = jnp.concatenate([k_past, k], axis=1)
    v_all = jnp.concatenate([v_past, v], axis=1)
    y_moba = moba_attention(q, k_all, v_all, pos).reshape(B, T, MOBA_WIDTH)
    qm = rmsnorm(qm.reshape(B, T, MEM_HEADS, HEAD_DIM), mem_q_norm)
    y_mem = mem_attention(qm, mk, mv).reshape(B, T, MEM_WIDTH)
    x = x + jnp.concatenate([y_pool, y_moba, y_mem], axis=-1) @ w_out
    x = x + 0.5 * swiglu_ffn(x, ffn2_norm, ffn2_w_in, ffn2_w_out)
    return x, k, v, new_buf

def setup_inputs(seed: int = 0) -> dict:
    key = jax.random.key(seed)
    ks = jax.random.split(key, 32)
    n_pages = PAST_LEN // PAGE_SIZE
    n_used = DEC_BATCH * n_pages
    n_phys = n_used + n_used // 4
    f32 = jnp.float32

    def nrm(k, shape, scale=1.0):
        return jax.random.normal(k, shape, f32) * scale

    def gain(k, shape):
        return 1.0 + 0.05 * jax.random.normal(k, shape, f32)

    page_table = jax.random.permutation(ks[8], n_phys)[:n_used].reshape(DEC_BATCH, n_pages).astype(jnp.int32)
    return {
        "x_prompt": nrm(ks[0], (BATCH, SEQ, D_MODEL)),
        "x_sample": nrm(ks[1], (DEC_BATCH, DEC_SEQ, D_MODEL)),
        "mem_prompt": nrm(ks[2], (BATCH, MEM_LEN, D_MODEL)),
        "cache_k": nrm(ks[3], (DEPTH, n_phys, PAGE_SIZE, MOBA_HEADS, HEAD_DIM)),
        "cache_v": nrm(ks[4], (DEPTH, n_phys, PAGE_SIZE, MOBA_HEADS, HEAD_DIM)),
        "cache_mem_k": nrm(ks[5], (DEPTH, DEC_BATCH, MEM_LEN, MEM_HEADS, HEAD_DIM)),
        "cache_mem_v": nrm(ks[6], (DEPTH, DEC_BATCH, MEM_LEN, MEM_HEADS, HEAD_DIM)),
        "state_pool": nrm(ks[7], (DEPTH, DEC_BATCH, POOL_BUF, POOL_WIDTH)),
        "page_table": page_table,
        "ffn1_norm": gain(ks[9], (DEPTH, D_MODEL)),
        "ffn1_w_in": nrm(ks[10], (DEPTH, D_MODEL, 2 * D_FF), D_MODEL ** -0.5),
        "ffn1_w_out": nrm(ks[11], (DEPTH, D_FF, D_MODEL), D_FF ** -0.5),
        "mix_norm": gain(ks[12], (DEPTH, D_MODEL)),
        "w_in": nrm(ks[13], (DEPTH, D_MODEL, IN_COLS), D_MODEL ** -0.5),
        "pool_w": nrm(ks[14], (DEPTH, len(POOL_WINDOWS), POOL_GROUP, POOL_GROUP), POOL_GROUP ** -0.5),
        "pool_scale": 1.0 + 0.1 * jax.random.normal(ks[15], (DEPTH, POOL_WIDTH), f32),
        "q_norm": gain(ks[16], (DEPTH, HEAD_DIM)),
        "k_norm": gain(ks[17], (DEPTH, HEAD_DIM)),
        "mem_norm": gain(ks[18], (DEPTH, D_MODEL)),
        "mem_w_kv": nrm(ks[19], (DEPTH, D_MODEL, 2 * MEM_WIDTH), D_MODEL ** -0.5),
        "mem_q_norm": gain(ks[20], (DEPTH, HEAD_DIM)),
        "mem_k_norm": gain(ks[21], (DEPTH, HEAD_DIM)),
        "w_out": nrm(ks[22], (DEPTH, D_MIX, D_MODEL), D_MIX ** -0.5),
        "ffn2_norm": gain(ks[23], (DEPTH, D_MODEL)),
        "ffn2_w_in": nrm(ks[24], (DEPTH, D_MODEL, 2 * D_FF), D_MODEL ** -0.5),
        "ffn2_w_out": nrm(ks[25], (DEPTH, D_FF, D_MODEL), D_FF ** -0.5),
    }

def reference(x_prompt, x_sample, mem_prompt, cache_k, cache_v, cache_mem_k, cache_mem_v, state_pool, page_table,
              ffn1_norm, ffn1_w_in, ffn1_w_out, mix_norm, w_in, pool_w, pool_scale, q_norm, k_norm,
              mem_norm, mem_w_kv, mem_q_norm, mem_k_norm, w_out, ffn2_norm, ffn2_w_in, ffn2_w_out):
    n_p, t_p, _ = x_prompt.shape
    n_s, t_s, _ = x_sample.shape
    past_len = page_table.shape[1] * PAGE_SIZE
    pos_p = jnp.arange(t_p, dtype=jnp.int32)
    pos_s = past_len + jnp.arange(t_s, dtype=jnp.int32)
    empty_kv = jnp.zeros((n_p, 0, MOBA_HEADS, HEAD_DIM), x_prompt.dtype)
    empty_buf = jnp.zeros((n_p, POOL_BUF, POOL_WIDTH), x_prompt.dtype)
    hp, hs = x_prompt, x_sample
    kp_l, vp_l, mkp_l, mvp_l, bp_l, ks_l, vs_l, bs_l = [], [], [], [], [], [], [], []
    for l in range(DEPTH):
        lw = (ffn1_norm[l], ffn1_w_in[l], ffn1_w_out[l], mix_norm[l], w_in[l], pool_w[l], pool_scale[l],
              q_norm[l], k_norm[l], mem_q_norm[l], w_out[l], ffn2_norm[l], ffn2_w_in[l], ffn2_w_out[l])
        mk_p, mv_p = mem_kv(mem_prompt, mem_norm[l], mem_w_kv[l], mem_k_norm[l])
        hp, kp, vp, bp = trunk_layer(hp, pos_p, empty_kv, empty_kv, empty_buf, mk_p, mv_p, *lw)
        k_past = cache_k[l][page_table].reshape(n_s, past_len, MOBA_HEADS, HEAD_DIM)
        v_past = cache_v[l][page_table].reshape(n_s, past_len, MOBA_HEADS, HEAD_DIM)
        hs, ksn, vsn, bs = trunk_layer(hs, pos_s, k_past, v_past, state_pool[l], cache_mem_k[l], cache_mem_v[l], *lw)
        kp_l.append(kp); vp_l.append(vp); mkp_l.append(mk_p); mvp_l.append(mv_p); bp_l.append(bp)
        ks_l.append(ksn); vs_l.append(vsn); bs_l.append(bs)
    return (hp, hs, jnp.stack(kp_l), jnp.stack(vp_l), jnp.stack(mkp_l), jnp.stack(mvp_l), jnp.stack(bp_l),
            jnp.stack(ks_l), jnp.stack(vs_l), jnp.stack(bs_l))


_drawn_inputs = setup_inputs


def setup_inputs(seed=0):
    import zlib

    import numpy as np

    out = dict(_drawn_inputs(seed))
    spreads = {}
    factors = {'q_norm': 8.0, 'mem_q_norm': 8.0, 'ffn2_norm': 3.218}
    for name, (base, spread) in spreads.items():
        noise = np.random.default_rng([zlib.crc32(name.encode()), seed]).standard_normal(out[name].shape)
        drawn = base * np.exp(spread * noise) if base else spread * noise
        out[name] = __import__('jax').numpy.asarray(drawn.astype(out[name].dtype))
    for name, factor in factors.items():
        out[name] = (out[name] * factor).astype(out[name].dtype)
    return out
```

```python
from contextlib import ExitStack

import concourse.bass as bass
from concourse import mybir
import numpy as np

F32 = mybir.dt.float32
F32R = mybir.dt.float32r
I32 = mybir.dt.int32
ALU = mybir.AluOpType
ACT = mybir.ActivationFunctionType
AX = mybir.AxisListType
ds = bass.ds

P = 128
D = 1024
KT = D // P
DFF = 2816
HT = DFF // P
NS = 8
NP = 256
N = NS + NP
POOL, MOBA, MEM = 256, 512, 256
HD = 64
MH, CH = MOBA // HD, MEM // HD
PAST, PAGE, BLOCK = 1024, 128, 256
PAGES = PAST // PAGE
BLOCKS = PAST // BLOCK
EPS = 1e-6
SCALE = HD ** -0.5
NEG = -1e30
WINDOWS = (2, 4, 8, 16)
BUF = 15
ROT, HALF_ROT, THETA = 16, 8, 500000.0

RING = 4
U_MEM = 0
U_FFN1 = U_MEM + 4
U_WIN = U_FFN1 + 3 * HT
U_MIX = U_WIN + 16
U_FFN2 = U_MIX + KT
U_END = U_FFN2 + 3 * HT
LEAD = 2
X_BANKS = (5, 6, 7, 0, 1, 2, 3, 4)
M_ORDER = (4, 5, 6, 7, 0, 1, 2, 3)
KV_SLOTS = 4
KV_STREAM = ([("k", b) for b in range(5)] + [("v", 0), ("k", 5), ("v", 1), ("k", 6), ("v", 2), ("k", 7), ("v", 3),
             ("mk", 0), ("mv", 0)] + [("v", b) for b in range(4, 8)])
KV_AT = {kb: n for n, kb in enumerate(KV_STREAM)}
GP_PAGES = 4


def shape_constants():
    c = {}
    c["ident"] = np.eye(P, dtype=np.float32)
    q = np.arange(NP).reshape(2, P).T[:, :, None]
    c["causal"] = np.where(np.arange(NP)[None, None, :] <= q, 0.0, NEG).astype(np.float32)
    inv = np.power(np.float32(THETA), -np.arange(HALF_ROT, dtype=np.float32) * np.float32(2.0 / ROT)).astype(np.float32)
    pos = np.concatenate([np.arange(NP), np.full(P, PAST)]).astype(np.float32).reshape(3, P)
    ang = (pos.T[:, :, None] * inv[None, None, :]).astype(np.float32)
    c["rope"] = np.stack([np.cos(ang), np.sin(ang)], axis=1).astype(np.float32)
    band = np.zeros((P, 2, 4, NP), np.float32)
    samp = np.zeros((P, 4, NS), np.float32)
    for g, w in enumerate(WINDOWS):
        for t in range(NP):
            for s in range(max(0, t - w + 1), t + 1):
                band[s % P, s // P, g, t] += 1.0 / min(w, t + 1)
            band[t % P, t // P, g, t] -= 1.0
        for b in range(NS):
            samp[b, g, b] = 1.0 / w - 1.0
            for j in range(BUF - (w - 1), BUF):
                samp[NS + BUF * b + j, g, b] = 1.0 / w
    c["band"], c["samp"] = band, samp
    delta = np.zeros((NS, NS, MH), np.float32)
    for b in range(NS):
        delta[b, b, :] = 1.0
    c["delta"] = delta
    back = np.zeros((32, 2, NS), np.float32)
    for r in range(32):
        for hf in range(2):
            back[r, hf, 4 * hf + r // MH] = 1.0
    c["back"] = back
    c["rank"] = np.tile(np.arange(1, BLOCKS + 1, dtype=np.float32), (32, 1))
    return c


def layer(nc, a):
    ctx = ExitStack()
    with ctx:
        cursor = [1152]

        def place(name, shape, dt=F32, at=None):
            size = 4 * int(np.prod(shape[1:]))
            if at is None:
                at = cursor[0]
                cursor[0] += -(-size // 64) * 64
            return nc.alloc_sbuf_tensor_at(name, list(shape), dt, offset=at)

        def sem(name):
            return ctx.enter_context(nc.semaphore(name))

        raw = place("raw", [P, RING, 1024])
        w_hi = place("w_hi", [P, RING, 1024], F32R)
        w_lo = place("w_lo", [P, RING, 1024], F32R)
        xT = place("xT", [P, KT, N])
        x_hi = place("x_hi", [P, KT, N], F32R)
        x_lo_at = cursor[0]
        x_lo = place("x_lo", [P, KT, N], F32R)
        band = place("band", [P, 2, 4, NP], at=x_lo_at)
        tmp = place("tmp", [P, KT, N])
        mem_kv = place("mem_kv", [P, 2, 512])
        kv = place("kv", [P, KV_SLOTS, PAGES * 512])
        root = place("root", [P, N])
        rstd = place("rstd", [P, N])
        sg = place("sg", [P, 2, N])
        h_tmp = place("h_tmp", [P, 2, N])
        ident = place("ident", [P, P])
        ones = place("ones", [P, P])
        gains = place("gains", [P, 34])
        rope = place("rope", [P, 2, 3, HALF_ROT])
        head_gain = place("head_gain", [P, 4, HD])
        eps_col = place("eps_col", [P, 1])
        dummy = place("dummy", [P, 4])
        page_ids = place("page_ids", [1, NS * PAGES], I32)
        samp = place("samp", [P, 4, NS])
        delta = place("delta", [NS, NS, MH])
        back = place("back", [32, 2, NS])
        rank = place("rank", [32, BLOCKS])
        own8 = place("own8", [NS, MH])
        own_e = place("own_e", [NS, 4, MH])
        logits = place("logits", [P, PAGES, 4, MH])
        logits_m = place("logits_m", [P, 2, NS, CH])
        rows = place("rows", [32, PAST + 8])
        p_cols = place("p_cols", [P, 2, PAGES, 32])
        p_own = place("p_own", [32, 32])
        p_own8 = place("p_own8", [NS, 2, 32])
        stats = place("stats", [32, 24])
        qb = place("qb", [P, 2, 512])
        ss_h = place("ss_h", [P, 16])
        var_h = place("var_h", [P, 16])
        sd_h = place("sd_h", [P, 16])
        rs_h = place("rs_h", [P, 16])
        rot = place("rot", [P, 4, 2, MH * HALF_ROT])
        mx = place("mx", [P, 2, 2])
        nb = place("nb", [P, 2, 2])
        sm = place("sm", [P, 2, 2])
        rc = place("rc", [P, 2, 2])
        ext = place("ext", [P, POOL])
        pool_wd = place("pool_wd", [P, 2, P])
        region = cursor[0]
        h_hi = place("h_hi", [P, HT, N], F32R)
        h_lo = place("h_lo", [P, HT, N], F32R)
        end = cursor[0]
        at = [region]

        def over(name, shape, dt=F32):
            t = place(name, shape, dt, at=at[0])
            at[0] += -(-4 * int(np.prod(shape[1:])) // 64) * 64
            assert at[0] <= end, name
            return t

        x_rows = over("x_rows", [P, 3, D])
        m_rows = over("m_rows", [P, 2, D])
        memT = over("memT", [P, KT, NP])
        m_hi = over("m_hi", [P, KT, NP], F32R)
        m_lo = over("m_lo", [P, KT, NP], F32R)
        g_rows = over("g_rows", [34, P])
        at[0] = region
        qp = over("qp", [P, 2, 512])
        kp = over("kp", [P, 2, 512])
        vp = over("vp", [P, 2, 512])
        up = over("up", [P, 2, 512])
        qs = over("qs", [NS, 512])
        ks = over("ks", [NS, 512])
        vs = over("vs", [NS, 512])
        us = over("us", [NS, 512])
        qT = over("qT", [P, 4, NP])
        kT = over("kT", [P, 4, NP])
        qmT = over("qmT", [P, 2, NP])
        mkT = over("mkT", [P, 2, NP])
        prob = over("prob", [P, 2, NP])
        probT = over("probT", [P, 2, NP])
        sq_h = over("sq_h", [P, 2, 512])
        causal = place("causal", [P, 2, NP])

        bank = [ctx.enter_context(nc.psum_tensor(f"bank{i}", [P, 512], F32)) for i in range(8)]

        x_loaded, m_loaded, g_loaded = sem("x_loaded"), sem("m_loaded"), sem("g_loaded")
        id_loaded, c_loaded, band_loaded = sem("id_loaded"), sem("c_loaded"), sem("band_loaded")
        pg_loaded, poolw_loaded = sem("pg_loaded"), sem("poolw_loaded")
        raw_loaded = [sem(f"raw_loaded{i}") for i in range(RING)]
        kv_loaded = [sem(f"kv_loaded{i}") for i in range(KV_SLOTS)]
        hi_ready, lo_ready, w_used = sem("hi_ready"), sem("lo_ready"), sem("w_used")
        const_set = sem("const_set")
        g_turned, gains_ready = sem("g_turned"), sem("gains_ready")
        m_turned, memT_ready = sem("m_turned"), sem("memT_ready")
        x_turned, res_ready = sem("x_turned"), sem("res_ready")
        sq_ready, ss_ready, root_ready, rstd_ready = sem("sq_ready"), sem("ss_ready"), sem("root_ready"), sem("rstd_ready")
        xn_ready, xhi_ready, xlo_ready = sem("xn_ready"), sem("xhi_ready"), sem("xlo_ready")
        kvm_done, gu_free = sem("kvm_done"), sem("gu_free")
        silu_ready, hhi_ready, h_ready = sem("silu_ready"), sem("hhi_ready"), sem("h_ready")
        out_done = sem("out_done")
        proj_done, proj_evac = sem("proj_done"), sem("proj_evac")
        vec_step = sem("vec_step")
        var_ready, sd_ready, nrm_ready = sem("var_ready"), sem("sd_ready"), sem("nrm_ready")
        qb_psum, qb_ready, gp_done, k_used, v_used = sem("qb_psum"), sem("qb_ready"), sem("gp_done"), sem("k_used"), sem("v_used")
        qk_turned, qkT_ready = sem("qk_turned"), sem("qkT_ready")
        pooled_psum, pooled_ready, pool_psum, pool_ready = sem("pooled_psum"), sem("pooled_ready"), sem("pool_psum"), sem("pool_ready")
        ext_ready = sem("ext_ready")
        sc_ready, nb_ready, exp_done, prob_ready = sem("sc_ready"), sem("nb_ready"), sem("exp_done"), sem("prob_ready")
        pT_psum, probT_ready, pv_done, head_ready = sem("pT_psum"), sem("probT_ready"), sem("pv_done"), sem("head_ready")
        own_ready, lt_psum, rows_ready = sem("own_ready"), sem("lt_psum"), sem("rows_ready")
        smn_ready, sme_ready, p_ready, p_psum, pcols_ready = (sem("smn_ready"), sem("sme_ready"), sem("p_ready"),
                                                              sem("p_psum"), sem("pcols_ready"))
        ys_ready = sem("ys_ready")
        cat_hi, cat_lo = sem("cat_hi"), sem("cat_lo")
        y_turned, y_ready = sem("y_turned"), sem("y_ready")
        mid_stored, stored = sem("mid_stored"), sem("stored")
        MID_STORES = 8

        def cols_view(w, k):
            return w[0].rearrange("(k p) c -> p k c", p=P)

        ffn_in = [cols_view(a["ffn1_w_in"], KT), cols_view(a["ffn2_w_in"], KT)]
        ffn_out = [cols_view(a["ffn1_w_out"], HT), cols_view(a["ffn2_w_out"], HT)]
        w_in, w_mix, w_mem = cols_view(a["w_in"], KT), cols_view(a["w_out"], KT), cols_view(a["mem_w_kv"], KT)

        def kv_level(n):
            total = 0
            for i in range(n % KV_SLOTS, n + 1, KV_SLOTS):
                total += 16 * (PAGES if KV_STREAM[i][0] in "kv" else 1)
            return total

        def kv_wait(eng, kind, b):
            n = KV_AT[(kind, b)]
            eng.wait_ge(kv_loaded[n % KV_SLOTS], kv_level(n))
            return n % KV_SLOTS

        V_ORDER = [0, 1, 2, 3, "mem", 4, 5, 6, 7]

        def raw_level(n, i):
            return 16 * (n // RING + 1) + 16 * i + (16 if n >= U_WIN + 12 else 0)

        def y_rows(eng, g):
            eng.wait_ge(y_turned, g + 1)
            if g < 2:
                dst, src = kv[0:NS, 0, g * 512:(g + 1) * 512], bank[g][0:NS, :]
            else:
                dst, src = kv[:, 1, (g - 2) * 512:(g - 1) * 512], bank[g][:, :]
            if eng is act_engine[0]:
                eng.activation(dst, src, ACT.Copy).then_inc(y_ready, 1)
            else:
                eng.tensor_copy(dst, src).then_inc(y_ready, 1)

        act_engine = [None]

        def steps(eng):
            yield from [("X", 0), ("POOL", 0), ("HA", 0), ("SA", 0), ("HB", 0), ("HA", 1), ("SB", 0), ("L", 4), ("SC", 0),
                        ("HB", 1), ("SD", 0), ("HA", 2), ("L", 5), ("PV", 0), ("HB", 2), ("HA", 3), ("L", 6), ("HB", 3),
                        ("HA", 4), ("L", 7), ("HB", 4), ("HA", 5), ("SA", 1), ("HB", 5), ("HA", 6), ("SB", 1), ("L", 8),
                        ("L", 9), ("SC", 1), ("HB", 6), ("SD", 1), ("HA", 7), ("L", 10), ("L", 11), ("HB", 7), ("SA", 2),
                        ("HA", 8), ("SB", 2), ("HB", 8), ("HA", 9), ("SC", 2), ("HB", 9), ("SD", 2), ("HA", 10),
                        ("PV", 2), ("HB", 10), ("HA", 11), ("PV", 1), ("HB", 11)]

        block = ctx.enter_context(nc.Block())

        @block.sync
        def _(sp):
            def load_unit(n0, j, i, src):
                n = n0 + j
                if not (isinstance(i, int) and n + 4 * i < RING):
                    sp.wait_ge(lo_ready, 4 * i + n - RING + 1)
                sp.dma_start(raw[:, n % RING, :].rearrange("p (k c) -> p k c", k=src.shape[1]), src)\
                    .then_inc(raw_loaded[n % RING], 16)

            def ffn_in_units(f, lo, hi):
                n0 = (U_FFN1, U_FFN2)[f]
                with sp.Fori(lo, hi) as i:
                    for j in range(4):
                        col = (j // 2) * P + (j % 2) * DFF
                        load_unit(n0, j, i, ffn_in[f][:, :, ds(i * (2 * P) + col, P)])

            def ffn_out_units(f):
                n0 = (U_FFN1, U_FFN2)[f] + 2 * HT
                for j in range(2):
                    load_unit(n0, j, 0, ffn_out[f][:, j:j + 1, :])
                with sp.Fori(0, 5) as i:
                    for j in range(4):
                        load_unit(n0 + 2, j, i, ffn_out[f][:, ds(i * 4 + (2 + j), 1), :])

            def load_kv(n):
                kind, b = KV_STREAM[n]
                if n >= KV_SLOTS:
                    was, wb = KV_STREAM[n - KV_SLOTS]
                    if was in ("k", "mk"):
                        sp.wait_ge(k_used, wb + 1 if was == "k" else 12)
                    else:
                        sp.wait_ge(v_used, V_ORDER.index(wb if was == "v" else "mem") + 1)
                slot = n % KV_SLOTS
                if kind in "kv":
                    cache = a["cache_k"] if kind == "k" else a["cache_v"]
                    for t in range(PAGES):
                        page = sp.value_load(page_ids[0:1, b * PAGES + t:b * PAGES + t + 1], min_val=0,
                                             max_val=cache.shape[1] - 1)
                        sp.dma_start(kv[:, slot, t * 512:(t + 1) * 512],
                                     cache[0, ds(page, 1)].rearrange("o p h d -> p (o h d)"))\
                            .then_inc(kv_loaded[slot], 16)
                else:
                    cache = a["cache_mem_k"] if kind == "mk" else a["cache_mem_v"]
                    sp.dma_start(kv[:, slot, :].rearrange("p (b t c) -> p b t c", b=NS, t=2),
                                 cache[0].rearrange("b (t p) h d -> p b t (h d)", p=P)).then_inc(kv_loaded[slot], 16)

            sp.dma_start(ident[:], a["ident"]).then_inc(id_loaded, 16)
            sp.dma_start(m_rows[:], a["mem_prompt"][0].rearrange("(t p) d -> p t d", p=P)).then_inc(m_loaded, 16)
            for j, name in enumerate(("ffn1_norm", "mix_norm", "mem_norm", "ffn2_norm")):
                sp.dma_start(g_rows[8 * j:8 * j + 8, :], a[name][0].rearrange("(k p) -> k p", p=P)).then_inc(g_loaded, 16)
            sp.dma_start(g_rows[32:34, :], a["pool_scale"][0].rearrange("(k p) -> k p", p=P)).then_inc(g_loaded, 16)
            sp.dma_start(x_rows[0:NS, 0, :], a["x_sample"][:, 0, :]).then_inc(x_loaded, 16)
            sp.dma_start(x_rows[:, 1:3, :], a["x_prompt"][0].rearrange("(t p) d -> p t d", p=P)).then_inc(x_loaded, 16)
            for j in range(4):
                load_unit(U_MEM, j, 0, w_mem[:, 2 * j:2 * j + 2, :])
            sp.dma_start(page_ids[:], a["page_table"].rearrange("b g -> (b g)").unsqueeze(0)).then_inc(pg_loaded, 16)
            for j, name in enumerate(("q_norm", "k_norm", "mem_q_norm", "mem_k_norm")):
                sp.dma_start(head_gain[:, j, :], a[name][0].partition_broadcast(P)).then_inc(c_loaded, 16)
            for dst, name in ((rope, "rope"), (samp, "samp"), (delta, "delta"), (back, "back"), (rank, "rank"),
                              (causal, "causal")):
                sp.dma_start(dst[:], a[name]).then_inc(c_loaded, 16)
            sp.dma_start(ext[NS:P, :], a["state_pool"][0].rearrange("b j c -> (b j) c")).then_inc(c_loaded, 16)
            sp.wait_ge(const_set, 1)
            for g in range(4):
                lo = HD * (g % 2)
                sp.dma_start(pool_wd[lo:lo + HD, g // 2, lo:lo + HD], a["pool_w"][0, g]).then_inc(poolw_loaded, 16)
            sp.dma_start(a["state_out"][0, :, 0:BUF - 1, :], a["state_pool"][0, :, 1:BUF, :]).then_inc(stored, 16)
            sp.wait_ge(pg_loaded, 16)
            for s, (lo, hi) in enumerate(((0, 5), (5, 8), (8, 11))):
                ffn_in_units(0, lo, hi)
                load_kv(s)
            ffn_out_units(0)
            load_kv(3)
            for nb_ in range(4):
                for j in range(4):
                    n = 4 * nb_ + j
                    if nb_ < 3:
                        c0 = POOL + MOBA * nb_
                        load_unit(U_WIN, n, 0, w_in[:, 2 * j:2 * j + 2, c0:c0 + 512])
                    else:
                        sp.wait_ge(lo_ready, U_WIN + n - RING + 1)
                        dst = raw[:, (U_WIN + n) % RING, :].rearrange("p (k c) -> p k c", k=2)
                        last = POOL + 3 * MOBA
                        sp.dma_start(dst[:, :, 0:256], w_in[:, 2 * j:2 * j + 2, 0:256])\
                            .then_inc(raw_loaded[(U_WIN + n) % RING], 16)
                        sp.dma_start(dst[:, :, 256:512], w_in[:, 2 * j:2 * j + 2, last:last + 256])\
                            .then_inc(raw_loaded[(U_WIN + n) % RING], 16)
                if nb_ in (1, 2):
                    load_kv(3 + nb_)
            for j in range(2):
                load_unit(U_MIX, j, 0, w_mix[:, j:j + 1, :])
            sp.wait_ge(w_used, U_WIN + 16)
            sp.dma_start(band[:], a["band"]).then_inc(band_loaded, 16)
            for n in range(6, len(KV_STREAM)):
                load_kv(n)
            sp.wait_ge(nrm_ready, 7)
            sp.wait_ge(proj_evac, 12)
            sp.dma_start(a["k_out"][0, 0].rearrange("(t p) h d -> p t (h d)", p=P), kp[:]).then_inc(mid_stored, 16)
            sp.dma_start(a["v_out"][0, 0].rearrange("(t p) h d -> p t (h d)", p=P), vp[:]).then_inc(mid_stored, 16)
            sp.dma_start(a["mk_out"][0, 0].rearrange("(t p) h d -> p t (h d)", p=P), mem_kv[:, :, 0:256])\
                .then_inc(mid_stored, 16)
            sp.dma_start(a["mv_out"][0, 0].rearrange("(t p) h d -> p t (h d)", p=P), mem_kv[:, :, 256:512])\
                .then_inc(mid_stored, 16)
            sp.dma_start(a["buf_out"][0, 0], up[P - BUF:P, 1, 0:POOL]).then_inc(mid_stored, 16)
            sp.dma_start(a["ks_out"][0, :, 0].rearrange("b h d -> b (h d)"), ks[:]).then_inc(mid_stored, 16)
            sp.dma_start(a["vs_out"][0, :, 0].rearrange("b h d -> b (h d)"), vs[:]).then_inc(mid_stored, 16)
            sp.dma_start(a["state_out"][0, :, BUF - 1, :], us[:, 0:POOL]).then_inc(mid_stored, 16)
            for j in range(2, KT):
                load_unit(U_MIX, j, 0, w_mix[:, j:j + 1, :])
            ffn_in_units(1, 0, 11)
            ffn_out_units(1)
            sp.wait_ge(y_ready, 6)
            sp.dma_start(a["y_sample"][:, 0, :], kv[0:NS, 0, 0:D]).then_inc(stored, 16)
            sp.dma_start(a["y_prompt"][0].rearrange("(t p) d -> p t d", p=P),
                         kv[:, 1, 0:2 * D].rearrange("p (t d) -> p t d", t=2)).then_inc(stored, 16)
            sp.wait_ge(mid_stored, 16 * MID_STORES)
            sp.wait_ge(stored, 16 * 3)

        @block.gpsimd
        def _(pool):
            pool.memset(pool_wd[:], 0.0).then_inc(const_set, 1)
            pool.memset(ones[:], 1.0).then_inc(const_set, 1)
            pool.memset(eps_col[:], EPS).then_inc(const_set, 1)
            pool.memset(dummy[:], 1.0).then_inc(const_set, 1)
            for b in range(NS + 4):
                pool.wait_ge(qb_ready, b + 1)
                if b < NS:
                    slot = kv_wait(pool, "k", b)
                    k_rows = kv[:, slot, 0:GP_PAGES * 512].rearrange("p (t c) -> p t c", c=512)
                    pool.tensor_tensor(k_rows, k_rows, qb[:, b % 2, :].unsqueeze(1).to_broadcast([P, GP_PAGES, 512]),
                                       ALU.mult).then_inc(gp_done, 1)
                else:
                    g = b - NS
                    slot = kv_wait(pool, "mk", 0)
                    m_keys = kv[:, slot, g * 1024:(g + 1) * 1024].rearrange("p (b t c) -> p b t c", b=2, t=2)
                    q_two = qb[:, b % 2, :].rearrange("p (b c) -> p b c", b=2).unsqueeze(2).to_broadcast([P, 2, 2, 256])
                    pool.tensor_tensor(m_keys, m_keys, q_two, ALU.mult).then_inc(gp_done, 1)

        @block.scalar
        def _(act):
            def split(n0, j=0, i=0):
                n = n0 + j
                act.wait_ge(raw_loaded[n % RING], raw_level(n, i))
                if not (isinstance(i, int) and n + 4 * i < RING):
                    act.wait_ge(w_used, 4 * i + n - RING + 1)
                act.activation(w_hi[:, n % RING, :], raw[:, n % RING, :], ACT.Copy).then_inc(hi_ready, 1)

            def norm_squares(inst, src, cols, order, ready, base):
                if inst:
                    act.wait_ge(xlo_ready, KT * inst)
                for idx, m in enumerate(order):
                    act.wait_ge(ready, base + idx + 1)
                    act.activation(tmp[:, m, 0:cols], src[:, m, :], ACT.Square).then_inc(sq_ready, 1)

            def norm_root(inst, cols, bk):
                act.wait_ge(ss_ready, inst + 1)
                act.activation(root[:, 0:cols], bank[bk][:, 0:cols], ACT.Sqrt, bias=eps_col[:, 0:1],
                               scale=1.0 / D).then_inc(root_ready, 1)

            def norm_hi(inst, dst, cols, order):
                for idx, m in enumerate(order):
                    act.wait_ge(xn_ready, KT * inst + idx + 1)
                    act.activation(dst[:, m, :], tmp[:, m, 0:cols], ACT.Copy).then_inc(xhi_ready, 1)

            def silu(f, c, s):
                act.wait_ge(w_used, (U_FFN1, U_FFN2)[f] + 2 * c + 2)
                act.activation(sg[:, s, :], bank[2 * s][:, 0:N], ACT.Silu).then_inc(silu_ready, 1)

            def table(func, k):
                act.activation(dummy[:, k:k + 1], dummy[:, 3:4], func)

            def ffn(f):
                n0 = (U_FFN1, U_FFN2)[f]
                table(ACT.Silu, 0)
                with act.Fori(0, HT // 2) as i:
                    for s in range(2):
                        split(n0 + 2 + 2 * s, 0, i)
                        split(n0 + 3 + 2 * s, 0, i)
                        silu(f, i * 2 + s, s)
                with act.Fori(0, 5) as i:
                    for j in range(4):
                        split(n0 + 2 * HT + LEAD, j, i)

            def head_sd(inst, nrows, width):
                act.wait_ge(var_ready, inst + 1)
                act.activation(sd_h[0:nrows, 0:width], var_h[0:nrows, 0:width], ACT.Sqrt).then_inc(sd_ready, 1)

            def evac(nb_):
                for tt in range(3):
                    if tt < 2:
                        act.wait_ge(proj_done, 2 * nb_ + tt + 1)
                    else:
                        act.wait_ge(w_used, U_WIN + 4 * nb_ + 4)
                    src = bank[3 * (nb_ % 2) + tt]
                    if tt == 0:
                        act.activation((qs, ks, vs, us)[nb_][:], src[0:NS, :], ACT.Copy).then_inc(proj_evac, 1)
                    else:
                        act.activation((qp, kp, vp, up)[nb_][:, tt - 1, :], src[:, :], ACT.Copy).then_inc(proj_evac, 1)

            def queries(b):
                act.wait_ge(qb_psum, b + 1)
                if b >= 2:
                    act.wait_ge(k_used, b - 1)
                act.activation(qb[:, b % 2, :], bank[6][:, :], ACT.Copy).then_inc(qb_ready, 1)

            act_engine[0] = act
            act.wait_ge(const_set, 4)
            table(ACT.Sqrt, 1)
            for g in range(4):
                act.wait_ge(m_turned, g + 1)
                act.activation(memT[:, 2 * g:2 * g + 2, :].rearrange("p k c -> p (k c)"), bank[g][:, :], ACT.Copy)\
                    .then_inc(memT_ready, 1)
            for k in range(KT):
                act.wait_ge(memT_ready, k // 2 + 1)
                act.activation(tmp[:, k, 0:NP], memT[:, k, :], ACT.Square).then_inc(sq_ready, 1)
            split(0)
            split(1)
            norm_root(0, NP, 6)
            norm_hi(0, m_hi, NP, range(KT))
            split(2)
            split(3)
            norm_squares(1, xT, N, range(KT), res_ready, 0)
            norm_root(1, N, 7)
            norm_hi(1, x_hi, N, range(KT))
            split(4)
            split(5)
            ffn(0)
            table(ACT.Sqrt, 1)
            split(U_WIN)
            split(U_WIN + 1)
            norm_squares(2, xT, N, M_ORDER, res_ready, KT)
            norm_root(2, N, 4)
            norm_hi(2, x_hi, N, M_ORDER)
            for r in range(2, 6):
                split(U_WIN + r)
            evac(0)
            split(U_WIN + 6)
            split(U_WIN + 7)
            head_sd(0, NS, MH)
            queries(0)
            split(U_WIN + 8)
            split(U_WIN + 9)
            head_sd(1, P, 2 * MH)
            split(U_WIN + 10)
            split(U_WIN + 11)
            evac(1)
            queries(1)
            split(U_WIN + 12)
            split(U_WIN + 13)
            head_sd(2, NS, MH)
            head_sd(3, P, 2 * MH)
            queries(2)
            split(U_WIN + 14)
            split(U_WIN + 15)
            evac(2)
            queries(3)
            evac(3)
            act.wait_ge(proj_evac, 10)
            act.activation(ext[0:NS, :], us[:, 0:POOL], ACT.Copy).then_inc(ext_ready, 1)
            split(U_MIX)
            split(U_MIX + 1)
            head_sd(4, NS, CH)
            head_sd(5, P, 2 * CH)
            head_sd(6, P, 2 * CH)
            queries(4)
            table(ACT.Exp, 2)
            for what, k in steps(act):
                if what == "X":
                    for g, dst in enumerate((qT, qT, kT, kT, qmT, mkT)):
                        act.wait_ge(qk_turned, g + 1)
                        half = 2 * (g % 2) if g < 4 else 0
                        act.activation(dst[:, half:half + 2, :].rearrange("p k c -> p (k c)"), bank[(g if g < 4 else g - 4)][:, :],
                                       ACT.Copy).then_inc(qkT_ready, 1)
                elif what == "POOL":
                    for pr in range(2):
                        act.wait_ge(pooled_psum, pr + 1)
                        act.activation(sg[:, pr, :], bank[4 + pr][:, 0:N], ACT.Copy).then_inc(pooled_ready, 1)
                    for pr in range(2):
                        act.wait_ge(pool_psum, pr + 1)
                        act.activation(tmp[:, pr, :], bank[4 + pr][:, 0:N], ACT.Copy, scale=gains[:, 32 + pr:33 + pr])\
                            .then_inc(pool_ready, 1)
                elif what == "HA":
                    act.wait_ge(nb_ready, k + 1)
                    if k >= 1:
                        act.wait_ge(pT_psum, k)
                    for t in range(2):
                        act.activation(prob[:, t, :], bank[k % 2][:, t * NP:(t + 1) * NP], ACT.Exp, scale=SCALE,
                                       bias=nb[:, k % 2, t:t + 1], accum_out=sm[:, k % 2, t:t + 1]).then_inc(exp_done, 1)
                elif what == "HB":
                    act.wait_ge(pT_psum, k + 1)
                    if k >= 1:
                        act.wait_ge(pv_done, k)
                    act.activation(probT[:].rearrange("p k c -> p (k c)"), bank[2][:, :], ACT.Copy).then_inc(probT_ready, 1)
                    if k % 2 == 1:
                        act.wait_ge(pv_done, k + 1)
                        act.activation(tmp[:, 2 + k // 2, NS:N], bank[3][:, 0:NP], ACT.Copy).then_inc(head_ready, 1)
                elif what == "L":
                    if k + 1 < NS + 4:
                        queries(k + 1)
                elif what == "SA":
                    act.wait_ge(lt_psum, k + 1)
                    if k:
                        act.wait_ge(p_psum, k)
                    if k < 2:
                        act.activation(rows[:, 0:512], bank[4][0:32, :], ACT.Copy).then_inc(rows_ready, 1)
                        act.activation(rows[:, 512:1024], bank[5][0:32, :], ACT.Copy).then_inc(rows_ready, 1)
                        act.activation(rows[:, 1024:1025], bank[7][0:32, 0:1], ACT.Copy).then_inc(rows_ready, 1)
                    else:
                        act.activation(rows[:, 0:NP], bank[4][0:32, 0:NP], ACT.Copy).then_inc(rows_ready, 1)
                elif what == "SC":
                    width = PAST + 1 if k < 2 else NP
                    act.wait_ge(smn_ready, k + 1)
                    act.activation(rows[:, 0:width], rows[:, 0:width], ACT.Exp, scale=SCALE, bias=stats[:, 15:16],
                                   accum_out=stats[:, 16:17]).then_inc(sme_ready, 1)
                elif what == "SD":
                    act.wait_ge(p_psum, k + 1)
                    if k < 2:
                        act.activation(p_cols[:, k % 2, :, :].rearrange("p t c -> p (t c)"), bank[4][:, 0:256], ACT.Copy)\
                            .then_inc(pcols_ready, 1)
                        act.activation(p_own8[:, k, :], bank[7][0:NS, 64:96], ACT.Copy).then_inc(pcols_ready, 1)
                    else:
                        act.wait_ge(v_used, 4)
                        act.activation(p_cols[:, 0, 0:2, :].rearrange("p t c -> p (t c)"), bank[4][:, 0:64], ACT.Copy)\
                            .then_inc(pcols_ready, 1)
            act.wait_ge(ys_ready, 6)
            act.wait_ge(head_ready, 6)
            act.wait_ge(pool_ready, 2)
            for m in range(KT):
                act.activation(x_hi[:, m, :], tmp[:, m, :], ACT.Copy).then_inc(cat_hi, 1)
            table(ACT.Sqrt, 1)
            for r in range(2, KT + 2):
                split(U_MIX + r)
            norm_squares(3, xT, N, M_ORDER, res_ready, 2 * KT)
            norm_root(3, N, 4)
            norm_hi(3, x_hi, N, M_ORDER)
            ffn(1)
            for g in range(1, 6, 2):
                y_rows(act, g)


        @block.vector
        def _(vec):
            chained = [0]

            def chain(ins):
                chained[0] += 1
                ins.then_inc(vec_step, 1)
                vec.wait_ge(vec_step, chained[0])

            def split(n0, j=0, i=0):
                n = n0 + j
                vec.wait_ge(hi_ready, 4 * i + n + 1)
                vec.tensor_tensor(w_lo[:, n % RING, :], raw[:, n % RING, :], w_hi[:, n % RING, :].bitcast(F32),
                                  ALU.subtract).then_inc(lo_ready, 1)

            def norm(inst, src, g0, hi, lo, cols, order):
                vec.wait_ge(root_ready, inst + 1)
                vec.reciprocal(rstd[:, 0:cols], root[:, 0:cols]).then_inc(rstd_ready, 1)
                vec.wait_ge(rstd_ready, inst + 1)
                order = list(order)
                for idx in range(KT + 1):
                    if idx < KT:
                        m = order[idx]
                        vec.scalar_tensor_tensor(out=tmp[:, m, 0:cols], in0=src[:, m, :], scalar=gains[:, g0 + m:g0 + m + 1],
                                                 in1=rstd[:, 0:cols], op0=ALU.mult, op1=ALU.mult).then_inc(xn_ready, 1)
                    if idx >= 1:
                        m = order[idx - 1]
                        vec.wait_ge(xhi_ready, KT * inst + idx)
                        vec.tensor_tensor(lo[:, m, :], tmp[:, m, 0:cols], hi[:, m, :].bitcast(F32), ALU.subtract)\
                            .then_inc(xlo_ready, 1)

            def residual(inst, last, weight):
                for idx, m in enumerate(M_ORDER):
                    if idx < KT - 1:
                        vec.wait_ge(out_done, (KT - 1) * inst + idx + 1)
                    else:
                        vec.wait_ge(w_used, last + 1)
                    vec.scalar_tensor_tensor(out=xT[:, m, :], in0=bank[m][:, 0:N], scalar=weight, in1=xT[:, m, :],
                                             op0=ALU.mult, op1=ALU.add).then_inc(res_ready, 1)

            def ffn(f):
                n0 = (U_FFN1, U_FFN2)[f]
                with vec.Fori(0, HT // 2) as i:
                    for s in range(2):
                        split(n0 + 2 + 2 * s, 0, i)
                        split(n0 + 3 + 2 * s, 0, i)
                        c = i * 2 + s
                        vec.wait_ge(silu_ready, c + (HT * f + 1))
                        vec.tensor_tensor(h_tmp[:, s, :], sg[:, s, :], bank[2 * s + 1][:, 0:N], ALU.mult)\
                            .then_inc(gu_free, 1)
                        vec.wait_ge(gu_free, c + (HT * f + 3))
                        vec.tensor_copy(h_hi[:, ds(c, 1), :].rearrange("p a n -> p (a n)"), h_tmp[:, s, :]).then_inc(hhi_ready, 1)
                        vec.wait_ge(hhi_ready, c + (HT * f + 1))
                        vec.tensor_tensor(h_lo[:, ds(c, 1), :].rearrange("p a n -> p (a n)"), h_tmp[:, s, :],
                                          h_hi[:, ds(c, 1), :].rearrange("p a n -> p (a n)").bitcast(F32), ALU.subtract)\
                            .then_inc(h_ready, 1)
                with vec.Fori(0, 5) as i:
                    for j in range(4):
                        split(n0 + 2 * HT + LEAD, j, i)

            def head_norm(inst, buf, nt, nh, gain, rope_at, evacuated):
                nrows = buf.shape[0]
                vec.wait_ge(proj_evac, evacuated)
                sq = sq_h[0:nrows, 0:nt, 0:nh * HD]
                chain(vec.tensor_tensor(sq, buf, buf, ALU.mult))
                chain(vec.tensor_reduce(ss_h[0:nrows, 0:nt * nh].rearrange("p (t h) -> p t h", t=nt),
                                        sq.rearrange("p t (h d) -> p t h d", d=HD), AX.X, ALU.add))
                vec.tensor_scalar(var_h[0:nrows, 0:nt * nh], ss_h[0:nrows, 0:nt * nh], 1.0 / HD, EPS, ALU.mult, ALU.add)\
                    .then_inc(var_ready, 1)
                vec.wait_ge(sd_ready, inst + 1)
                chain(vec.reciprocal(rs_h[0:nrows, 0:nt * nh], sd_h[0:nrows, 0:nt * nh]))
                heads = buf.rearrange("p t (h d) -> p t h d", d=HD)
                for t in range(nt):
                    r = rs_h[0:nrows, t * nh:(t + 1) * nh].unsqueeze(2).to_broadcast([nrows, nh, HD])
                    one = vec.tensor_tensor(heads[:, t], heads[:, t], r, ALU.mult)
                    if t < nt - 1:
                        one.then_inc(vec_step, 1)
                        chained[0] += 1
                chain(one)
                g = head_gain[0:nrows, gain, :].unsqueeze(1).to_broadcast([nrows, nt * nh, HD])
                flat = buf.rearrange("p t (h d) -> p (t h) d", d=HD) if nh * HD == 512 else None
                for t in range(nt):
                    g = head_gain[0:nrows, gain, :].unsqueeze(1).to_broadcast([nrows, nh, HD])
                    one = vec.tensor_tensor(heads[:, t], heads[:, t], g, ALU.mult)
                    if rope_at is None and t == nt - 1:
                        one.then_inc(nrm_ready, 1)
                    elif t < nt - 1:
                        one.then_inc(vec_step, 1)
                        chained[0] += 1
                    else:
                        chain(one)
                if rope_at is None:
                    return
                x1, x2 = heads[:, :, :, 0:HALF_ROT], heads[:, :, :, HALF_ROT:ROT]
                cs = [rope[0:nrows, q, rope_at:rope_at + nt, :].unsqueeze(2).to_broadcast([nrows, nt, nh, HALF_ROT])
                      for q in range(2)]
                r = [rot[0:nrows, q, 0:nt, :].rearrange("p t (h d) -> p t h d", h=nh) for q in range(4)]
                for q, (x, cos_sin) in enumerate(((x1, cs[0]), (x2, cs[1]), (x2, cs[0]), (x1, cs[1]))):
                    one = vec.tensor_tensor(r[q], x, cos_sin, ALU.mult)
                    if q < 3:
                        one.then_inc(vec_step, 1)
                        chained[0] += 1
                chain(one)
                vec.tensor_tensor(x1, r[0], r[1], ALU.subtract)
                vec.tensor_tensor(x2, r[2], r[3], ALU.add).then_inc(nrm_ready, 1)

            def own_keys(hf):
                if hf == 0:
                    chain(vec.tensor_tensor(sq_h[0:NS, 0, :], qs[:], ks[:], ALU.mult))
                    chain(vec.tensor_reduce(own8[:], sq_h[0:NS, 0, :].rearrange("p (h d) -> p h d", d=HD), AX.X, ALU.add))
                else:
                    vec.wait_ge(lt_psum, 1)
                vec.tensor_tensor(own_e[:], delta[:, 4 * hf:4 * hf + 4, :], own8[:].unsqueeze(1).to_broadcast([NS, 4, MH]),
                                  ALU.mult).then_inc(own_ready, 1)

            def key_logits(b):
                if b < NS:
                    slot = kv_wait(vec, "k", b)
                    vec.wait_ge(qb_ready, b + 1)
                    if b == 4:
                        vec.wait_ge(lt_psum, 1)
                    part = kv[:, slot, GP_PAGES * 512:PAGES * 512].rearrange("p (t c) -> p t c", c=512)
                    chain(vec.tensor_tensor(part, part, qb[:, b % 2, :].unsqueeze(1)
                                            .to_broadcast([P, PAGES - GP_PAGES, 512]), ALU.mult))
                    vec.tensor_reduce(logits[:, GP_PAGES:PAGES, b % 4, :],
                                      part.rearrange("p t (h d) -> p t h d", d=HD), AX.X, ALU.add)
                    vec.wait_ge(gp_done, b + 1)
                    part = kv[:, slot, 0:GP_PAGES * 512].rearrange("p (t h d) -> p t h d", d=HD, h=MH)
                    vec.tensor_reduce(logits[:, 0:GP_PAGES, b % 4, :], part, AX.X, ALU.add).then_inc(k_used, 1)
                else:
                    g = b - NS
                    slot = KV_AT[("mk", 0)] % KV_SLOTS
                    vec.wait_ge(gp_done, b + 1)
                    m_keys = kv[:, slot, g * 1024:(g + 1) * 1024].rearrange("p (b t h d) -> p t b h d", b=2, t=2, h=CH)
                    for t in range(2):
                        red = vec.tensor_reduce(logits_m[:, t, 2 * g:2 * g + 2, :], m_keys[:, t], AX.X, ALU.add)
                    red.then_inc(k_used, 1)

            vec.wait_ge(g_turned, 1)
            vec.tensor_copy(gains[:], bank[4][:, 0:34]).then_inc(gains_ready, 1)
            for m in range(KT):
                vec.wait_ge(x_turned, m + 1)
                vec.tensor_copy(xT[:, m, :], bank[X_BANKS[m]][:, 0:N]).then_inc(res_ready, 1)
            split(0)
            split(1)
            vec.wait_ge(gains_ready, 1)
            norm(0, memT, 16, m_hi, m_lo, NP, range(KT))
            split(2)
            split(3)
            norm(1, xT, 0, x_hi, x_lo, N, range(KT))
            split(4)
            split(5)
            vec.wait_ge(kvm_done, 1)
            vec.tensor_copy(mem_kv[:, 0, :], bank[4][:, :]).then_inc(gu_free, 1)
            vec.wait_ge(w_used, 4)
            vec.tensor_copy(mem_kv[:, 1, :], bank[5][:, :]).then_inc(gu_free, 1)
            ffn(0)
            split(U_WIN)
            split(U_WIN + 1)
            residual(0, U_WIN - 1, 0.5)
            norm(2, xT, 8, x_hi, x_lo, N, M_ORDER)
            for r in range(2, 6):
                split(U_WIN + r)
            vec.wait_ge(c_loaded, 16 * 11)
            head_norm(0, qs[:].unsqueeze(1), 1, MH, 0, 2, 1)
            split(U_WIN + 6)
            split(U_WIN + 7)
            key_logits(0)
            split(U_WIN + 8)
            split(U_WIN + 9)
            head_norm(1, qp[:], 2, MH, 0, 0, 3)
            split(U_WIN + 10)
            split(U_WIN + 11)
            key_logits(1)
            head_norm(2, ks[:].unsqueeze(1), 1, MH, 1, 2, 4)
            head_norm(3, kp[:], 2, MH, 1, 0, 6)
            split(U_WIN + 12)
            split(U_WIN + 13)
            own_keys(0)
            split(U_WIN + 14)
            split(U_WIN + 15)
            key_logits(2)
            head_norm(4, us[:, 256:512].unsqueeze(1), 1, CH, 2, None, 10)
            head_norm(5, up[:, :, 256:512], 2, CH, 2, None, 12)
            head_norm(6, mem_kv[:, :, 0:256], 2, CH, 3, None, 12)
            split(U_MIX)
            split(U_MIX + 1)
            key_logits(3)
            for what, k in steps(vec):
                if what == "L":
                    key_logits(k)
                elif what == "HA":
                    vec.wait_ge(sc_ready, k + 1)
                    chain(vec.tensor_reduce(mx[:, k % 2, :], bank[k % 2][:, :].rearrange("p (t c) -> p t c", t=2), AX.X, ALU.max))
                    vec.tensor_scalar(nb[:, k % 2, :], mx[:, k % 2, :], -SCALE, None, ALU.mult).then_inc(nb_ready, 1)
                elif what == "HB":
                    vec.wait_ge(exp_done, 2 * k + 2)
                    chain(vec.reciprocal(rc[:, k % 2, :], sm[:, k % 2, :]))
                    vec.tensor_scalar(prob[:, 0, :], prob[:, 0, :], rc[:, k % 2, 0:1], None, ALU.mult)
                    vec.tensor_scalar(prob[:, 1, :], prob[:, 1, :], rc[:, k % 2, 1:2], None, ALU.mult).then_inc(prob_ready, 1)
                elif what == "SA" and k == 1:
                    own_keys(1)
                elif what == "SB":
                    vec.wait_ge(rows_ready, (3, 6, 7)[k])
                    if k:
                        vec.wait_ge(sme_ready, k)
                    if k < 2:
                        blocks = rows[:, 0:PAST].rearrange("p (b c) -> p b c", b=BLOCKS)
                        chain(vec.tensor_reduce(stats[:, 0:4], blocks, AX.X, ALU.add))
                        chain(vec.tensor_reduce(stats[:, 4:5], stats[:, 0:4], AX.X, ALU.min))
                        chain(vec.scalar_tensor_tensor(out=stats[:, 5:9], in0=stats[:, 0:4], scalar=stats[:, 4:5],
                                                       in1=rank[:], op0=ALU.is_equal, op1=ALU.mult))
                        chain(vec.tensor_reduce(stats[:, 9:10], stats[:, 5:9], AX.X, ALU.max))
                        chain(vec.tensor_scalar(stats[:, 10:14], stats[:, 5:9], stats[:, 9:10], NEG, ALU.is_equal, ALU.mult))
                        chain(vec.tensor_tensor(blocks, blocks, stats[:, 10:14].unsqueeze(2).to_broadcast([32, BLOCKS, BLOCK]),
                                                ALU.add))
                    width = PAST + 1 if k < 2 else NP
                    chain(vec.tensor_reduce(stats[:, 14:15], rows[:, 0:width], AX.X, ALU.max))
                    vec.tensor_scalar(stats[:, 15:16], stats[:, 14:15], -SCALE, None, ALU.mult).then_inc(smn_ready, 1)
                elif what == "SC":
                    width = PAST + 1 if k < 2 else NP
                    vec.wait_ge(sme_ready, k + 1)
                    chain(vec.reciprocal(stats[:, 17:18], stats[:, 16:17]))
                    scaled = vec.tensor_scalar(rows[:, 0:width], rows[:, 0:width], stats[:, 17:18], None, ALU.mult)
                    if k < 2:
                        chain(scaled)
                        if k:
                            vec.wait_ge(p_psum, 1)
                        vec.tensor_scalar(p_own[:], ident[0:32, 0:32], rows[:, PAST:PAST + 1], None, ALU.mult)\
                            .then_inc(p_ready, 1)
                    else:
                        scaled.then_inc(p_ready, 1)
                elif what == "PV":
                    vec.wait_ge(v_used, {0: 4, 2: 5, 1: 9}[k])
                    hp = 4 if k < 2 else 2
                    tiles = slice(2, 6) if k < 2 else slice(6, 8)
                    toks = slice(4 * k, 4 * k + 4) if k < 2 else slice(0, NS)
                    for two in range(2):
                        r = slice(HD * two, HD * two + HD)
                        vec.tensor_copy(tmp[r, tiles, toks],
                                        bank[5][r, 0:32].rearrange("p (b h two) -> p h b two", h=hp, two=2)[:, :, :, two])\
                            .then_inc(ys_ready, 1)
            for m in range(KT):
                vec.wait_ge(cat_hi, m + 1)
                vec.tensor_tensor(x_lo[:, m, :], tmp[:, m, :], x_hi[:, m, :].bitcast(F32), ALU.subtract).then_inc(cat_lo, 1)
            for r in range(2, KT + 2):
                split(U_MIX + r)
            residual(1, U_FFN2 - 1, 1.0)
            norm(3, xT, 24, x_hi, x_lo, N, M_ORDER)
            vec.wait_ge(mid_stored, 16 * MID_STORES)
            ffn(1)
            residual(2, U_END - 1, 0.5)
            for g in range(0, 6, 2):
                y_rows(vec, g)

        @block.tensor
        def _(pe):
            def three(out, lhs, rhs, start, stop):
                pe.matmul(out, lhs[0], rhs[0], start=start, stop=False)
                pe.matmul(out, lhs[0], rhs[1], start=False, stop=False)
                return pe.matmul(out, lhs[1], rhs[0], start=False, stop=stop)

            def weights(slot, c0, c1):
                return w_hi[:, slot, c0:c1], w_lo[:, slot, c0:c1]

            def sum_squares(inst, cols, order, bk):
                for idx, m in enumerate(order):
                    pe.wait_ge(sq_ready, KT * inst + idx + 1)
                    mm = pe.matmul(bank[bk][:, 0:cols], ones[:], tmp[:, m, 0:cols], start=(idx == 0), stop=(idx == KT - 1))
                mm.then_inc(ss_ready, 1)

            def turn(out, in_, k=P):
                return pe.transpose(out, in_, ident[0:k, 0:k])

            def ffn(f):
                n0, inst = (U_FFN1, U_FFN2)[f], (1, 3)[f]
                pe.wait_ge(xlo_ready, KT * (inst + 1))
                with pe.Fori(0, HT // 2) as i:
                    for s in range(2):
                        pe.wait_ge(gu_free, i * 2 + (s + HT * f + 1))
                        for half in range(2):
                            j = 2 * s + half
                            pe.wait_ge(lo_ready, i * 4 + (n0 + j + 1))
                            for k in range(KT):
                                mm = three(bank[j][:, 0:N], weights((n0 + j) % RING, k * P, (k + 1) * P),
                                           (x_hi[:, k, :], x_lo[:, k, :]), k == 0, k == KT - 1)
                            mm.then_inc(w_used, 1)
                n0 += 2 * HT
                hidden = lambda k: tuple(h[:, ds(k, 1), :].rearrange("p a n -> p (a n)") for h in (h_hi, h_lo))
                for k in range(2):
                    outer(n0 + k, n0 + k, hidden(k), k == 0, False, f if k == 0 else None,
                          lambda k=k: pe.wait_ge(h_ready, HT * f + k + 1))
                with pe.Fori(0, 4) as i:
                    for j in range(4):
                        outer(n0 + 2 + j, i * 4 + (n0 + 2 + j), hidden(i * 4 + (2 + j)), False, False, None,
                              lambda j=j: pe.wait_ge(h_ready, i * 4 + (HT * f + 3 + j)))
                for k in range(HT - 4, HT):
                    outer(n0 + k, n0 + k, hidden(k), False, k == HT - 1, None, lambda k=k: pe.wait_ge(h_ready, HT * f + k + 1))

            def outer(n, unit, x, start, stop, first_of, ready):
                pe.wait_ge(lo_ready, unit + 1)
                ready()
                for idx, m in enumerate(M_ORDER):
                    if first_of is not None and m == 0:
                        pe.wait_ge(gu_free, 2 + HT * (first_of + 1))
                    mm = three(bank[m][:, 0:N], weights(n % RING, m * P, (m + 1) * P), x, start, stop)
                    if stop and idx < KT - 1:
                        mm.then_inc(out_done, 1)
                mm.then_inc(w_used, 1)

            def project(nb_, j):
                r = 4 * nb_ + j
                if j == 0 and nb_ >= 2:
                    pe.wait_ge(proj_evac, 3 * (nb_ - 1))
                pe.wait_ge(lo_ready, U_WIN + r + 1)
                for tt, c0 in enumerate((0, NS, NS + P)):
                    for kk in range(2):
                        k = 2 * j + kk
                        mm = three(bank[3 * (nb_ % 2) + tt][:, :], (x_hi[:, k, c0:c0 + P], x_lo[:, k, c0:c0 + P]),
                                   weights((U_WIN + r) % RING, kk * 512, kk * 512 + 512), k == 0, k == KT - 1)
                    if j == 3 and tt < 2:
                        mm.then_inc(proj_done, 1)
                mm.then_inc(w_used, 1)

            def queries(b):
                pe.wait_ge(nrm_ready, 1 if b < NS else 5)
                if b:
                    pe.wait_ge(qb_ready, b)
                if b < NS:
                    pe.matmul(bank[6][:, :], delta[:, b, 0:1].to_broadcast([NS, P]), qs[:], start=True, stop=True)\
                        .then_inc(qb_psum, 1)
                else:
                    for two in range(2):
                        mm = pe.matmul(bank[6][:, two * 256:two * 256 + 256],
                                       delta[:, 2 * (b - NS) + two, 0:1].to_broadcast([NS, P]), us[:, 256:512],
                                       start=True, stop=True)
                    mm.then_inc(qb_psum, 1)

            pe.wait_ge(id_loaded, 16)
            pe.wait_ge(g_loaded, 16 * 5)
            turn(bank[4][:, 0:34], g_rows[:], 34).then_inc(g_turned, 1)
            pe.wait_ge(m_loaded, 16)
            for g in range(4):
                for k in range(2):
                    for t in range(2):
                        mm = turn(bank[g][:, k * NP + t * P:k * NP + (t + 1) * P], m_rows[:, t, (2 * g + k) * P:(2 * g + k + 1) * P])
                mm.then_inc(m_turned, 1)
            pe.wait_ge(x_loaded, 32)
            for m in range(KT):
                bk = X_BANKS[m]
                if bk < 4:
                    pe.wait_ge(memT_ready, bk + 1)
                if bk == 4:
                    pe.wait_ge(gains_ready, 1)
                turn(bank[bk][:, 0:NS], x_rows[0:NS, 0, m * P:(m + 1) * P], NS)
                for t in range(2):
                    mm = turn(bank[bk][:, NS + t * P:NS + (t + 1) * P], x_rows[:, 1 + t, m * P:(m + 1) * P])
                mm.then_inc(x_turned, 1)
            pe.wait_ge(const_set, 4)
            pe.wait_ge(res_ready, KT)
            sum_squares(0, NP, range(KT), 6)
            pe.wait_ge(xlo_ready, KT)
            for j in range(4):
                pe.wait_ge(lo_ready, j + 1)
                for t in range(2):
                    for kk in range(2):
                        k = 2 * j + kk
                        mm = three(bank[4 + t][:, :], (m_hi[:, k, t * P:(t + 1) * P], m_lo[:, k, t * P:(t + 1) * P]),
                                   weights(j, kk * 512, kk * 512 + 512), k == 0, k == KT - 1)
                    if j == 3 and t == 0:
                        mm.then_inc(kvm_done, 1)
                mm.then_inc(w_used, 1)
                if j == 1:
                    sum_squares(1, N, range(KT), 7)
            ffn(0)
            sum_squares(2, N, M_ORDER, 4)
            pe.wait_ge(xlo_ready, 3 * KT)
            pe.wait_ge(c_loaded, 16 * 11)
            for nb_ in range(4):
                for j in range(4):
                    project(nb_, j)
                    if nb_ in (1, 2) and j in (1, 3):
                        queries(2 * (nb_ - 1) + j // 2)
            queries(4)
            for what, k in steps(pe):
                if what == "X":
                    pe.wait_ge(nrm_ready, 7)
                    pe.wait_ge(proj_evac, 12)
                    for g in range(6):
                        src, c0 = ((qp, 0), (qp, 256), (kp, 0), (kp, 256), (up, 256), (mem_kv, 0))[g]
                        if g >= 4:
                            pe.wait_ge(qkT_ready, g - 3)
                        for hh in range(2):
                            for t in range(2):
                                mm = turn(bank[g % 4][:, hh * NP + t * P:hh * NP + (t + 1) * P],
                                          src[:, t, c0 + hh * P:c0 + (hh + 1) * P])
                        mm.then_inc(qk_turned, 1)
                elif what == "POOL":
                    pe.wait_ge(band_loaded, 16)
                    pe.wait_ge(ext_ready, 1)
                    for g in range(4):
                        out, r = bank[4 + g // 2], slice(HD * (g % 2), HD * (g % 2) + HD)
                        for t in range(2):
                            pe.matmul(out[r, NS:N], up[:, t, g * HD:(g + 1) * HD], band[:, t, g, :], start=(t == 0), stop=(t == 1))
                        mm = pe.matmul(out[r, 0:NS], ext[:, g * HD:(g + 1) * HD], samp[:, g, :], start=True, stop=True)
                        if g % 2:
                            mm.then_inc(pooled_psum, 1)
                    pe.wait_ge(poolw_loaded, 16 * 4)
                    for pr in range(2):
                        pe.wait_ge(pooled_ready, pr + 1)
                        pe.matmul(bank[4 + pr][:, 0:N], pool_wd[:, pr, :], sg[:, pr, :], start=True, stop=True).then_inc(pool_psum, 1)
                elif what == "HA":
                    if k < 2:
                        pe.wait_ge(qkT_ready, 6)
                    else:
                        pe.wait_ge(exp_done, 2 * (k - 1))
                    r = slice(HD * (k % 2), HD * (k % 2) + HD)
                    q_, k_, hp = (qT, kT, k // 2) if k < MH else (qmT, mkT, (k - MH) // 2)
                    for t in range(2):
                        out = bank[k % 2][:, t * NP:(t + 1) * NP]
                        mm = pe.matmul(out, q_[r, hp, t * P:(t + 1) * P], k_[r, hp, :], start=True, stop=(k >= MH))
                        if k < MH:
                            mm = pe.matmul(out, ident[:], causal[:, t, :], start=False, stop=True)
                    mm.then_inc(sc_ready, 1)
                elif what == "HB":
                    pe.wait_ge(prob_ready, k + 1)
                    if k:
                        pe.wait_ge(probT_ready, k)
                    for kt in range(2):
                        for t in range(2):
                            mm = turn(bank[2][:, (2 * kt + t) * P:(2 * kt + t + 1) * P], prob[:, t, kt * P:(kt + 1) * P])
                    mm.then_inc(pT_psum, 1)
                    pe.wait_ge(probT_ready, k + 1)
                    if k % 2 == 0 and k:
                        pe.wait_ge(head_ready, k // 2)
                    r = slice(HD * (k % 2), HD * (k % 2) + HD)
                    for kt in range(2):
                        v_ = vp[:, kt, k * HD:(k + 1) * HD] if k < MH else \
                            mem_kv[:, kt, 256 + (k - MH) * HD:256 + (k - MH + 1) * HD]
                        mm = pe.matmul(bank[3][r, 0:NP], v_, probT[:, kt, :], start=(kt == 0), stop=(kt == 1))
                    mm.then_inc(pv_done, 1)
                elif what == "L":
                    if k + 1 < NS + 4:
                        queries(k + 1)
                elif what == "SA":
                    if k < 2:
                        pe.wait_ge(own_ready, k + 1)
                        if k:
                            pe.wait_ge(pcols_ready, 2)
                            pe.wait_ge(ys_ready, 2)
                        else:
                            pe.wait_ge(pool_ready, 2)
                        pe.matmul(bank[7][0:32, 0:1], own_e[:].rearrange("p b h -> p (b h)"), ones[0:NS, 0:1], start=True, stop=True)
                        pe.wait_ge(k_used, 4 * k + 4)
                        for t in range(PAGES):
                            mm = turn(bank[4 + t // 4][0:32, (t % 4) * P:(t % 4 + 1) * P],
                                      logits[:, t, :, :].rearrange("p b h -> p (b h)"))
                    else:
                        pe.wait_ge(k_used, NS + 4)
                        pe.wait_ge(pcols_ready, 4)
                        for t in range(2):
                            mm = turn(bank[4][0:32, t * P:(t + 1) * P], logits_m[:, t].rearrange("p b h -> p (b h)"))
                    mm.then_inc(lt_psum, 1)
                elif what == "SD":
                    pe.wait_ge(p_ready, k + 1)
                    for t in range(PAGES if k < 2 else 2):
                        mm = turn(bank[4][:, t * 32:(t + 1) * 32], rows[:, t * P:(t + 1) * P], 32)
                    if k < 2:
                        mm = pe.matmul(bank[7][0:NS, 64:96], back[:, k, :], p_own[:], start=True, stop=True)
                    mm.then_inc(p_psum, 1)
                elif what == "PV":
                    pe.wait_ge(pcols_ready, (2, 4, 5)[k])
                    if k:
                        pe.wait_ge(ys_ready, {2: 2, 1: 4}[k])
                        pe.wait_ge(rows_ready, 6)
                    if k < 2:
                        for b4 in range(4):
                            slot = kv_wait(pe, "v", 4 * k + b4)
                            for hp in range(4):
                                col, q = (4 * b4 + hp) * 2, b4 * MH + 2 * hp
                                for t in range(PAGES):
                                    pe.matmul(bank[5][:, col:col + 2], kv[:, slot, t * 512 + hp * P:t * 512 + (hp + 1) * P],
                                              p_cols[:, k, t, q:q + 2], start=(t == 0), stop=False)
                                mm = pe.matmul(bank[5][:, col:col + 2], vs[:, hp * P:(hp + 1) * P], p_own8[:, k, q:q + 2],
                                               start=False, stop=True)
                            mm.then_inc(v_used, 1)
                    else:
                        slot = kv_wait(pe, "mv", 0)
                        for b in range(NS):
                            for hp in range(2):
                                col = (2 * b + hp) * 2
                                for t in range(2):
                                    c0 = b * 512 + t * 256 + hp * P
                                    mm = pe.matmul(bank[5][:, col:col + 2], kv[:, slot, c0:c0 + P],
                                                   p_cols[:, 0, t, b * CH + 2 * hp:b * CH + 2 * hp + 2], start=(t == 0), stop=(t == 1))
                        mm.then_inc(v_used, 1)
            for k in range(KT):
                outer(U_MIX + k, U_MIX + k, (x_hi[:, k, :], x_lo[:, k, :]), k == 0, k == KT - 1, None,
                      lambda k=k: pe.wait_ge(cat_lo, k + 1))
            sum_squares(3, N, M_ORDER, 4)
            ffn(1)
            pe.wait_ge(res_ready, 4 * KT)
            for g in range(6):
                for q in range(4):
                    if g < 2:
                        mm = turn(bank[g][0:NS, q * P:(q + 1) * P], xT[:, 4 * g + q, 0:NS])
                    else:
                        t, m = (g - 2) // 2, 4 * ((g - 2) % 2) + q
                        mm = turn(bank[g][:, q * P:(q + 1) * P], xT[:, m, NS + t * P:NS + (t + 1) * P])
                mm.then_inc(y_turned, 1)


_INS = ["x_prompt", "x_sample", "mem_prompt", "cache_k", "cache_v", "cache_mem_k", "cache_mem_v", "state_pool", "page_table",
        "ffn1_norm", "ffn1_w_in", "ffn1_w_out", "mix_norm", "w_in", "pool_w", "pool_scale", "q_norm", "k_norm",
        "mem_norm", "mem_w_kv", "mem_q_norm", "mem_k_norm", "w_out", "ffn2_norm", "ffn2_w_in", "ffn2_w_out"]
_OUTS = [("y_prompt", (1, NP, D)), ("y_sample", (NS, 1, D)), ("k_out", (1, 1, NP, MH, HD)), ("v_out", (1, 1, NP, MH, HD)),
         ("mk_out", (1, 1, NP, CH, HD)), ("mv_out", (1, 1, NP, CH, HD)), ("buf_out", (1, 1, BUF, POOL)),
         ("ks_out", (1, NS, 1, MH, HD)), ("vs_out", (1, NS, 1, MH, HD)), ("state_out", (1, NS, BUF, POOL))]


def kernel(**inputs):
    import concourse.bacc as bacc
    from concourse.bass_utils import run_bass_kernel_spmd

    nc = bacc.Bacc("TRN2", target_bir_lowering=False, num_devices=1, dynamic_dma_scratch_size=1024)
    arrays, views = {}, {}
    given = {name: np.ascontiguousarray(inputs[name]) for name in _INS}
    for name, arr in list(given.items()) + list(shape_constants().items()):
        arrays[f"in_{name}"] = arr
        views[name] = nc.dram_tensor(f"in_{name}", arr.shape, mybir.dt.from_np(arr.dtype), kind="ExternalInput").ap()
    for name, shape in _OUTS:
        views[name] = nc.dram_tensor(f"out_{name}", shape, F32, kind="ExternalOutput").ap()
    layer(nc, views)
    r = run_bass_kernel_spmd(nc, [arrays], core_ids=[0])
    return tuple(r.results[0][f"out_{name}"] for name, _ in _OUTS)
```

```python
from contextlib import ExitStack

import concourse.bass as bass
from concourse import mybir
import numpy as np

F32 = mybir.dt.float32
F32R = mybir.dt.float32r
BF16 = mybir.dt.bfloat16
I32 = mybir.dt.int32
ALU = mybir.AluOpType
ACT = mybir.ActivationFunctionType
AX = mybir.AxisListType
ds = bass.ds

P = 128
D = 1024
KT = D // P
DFF = 2816
HT = DFF // P
NS = 8
NP = 256
N = NS + NP
POOL, MOBA, MEM = 256, 512, 256
HD = 64
MH, CH = MOBA // HD, MEM // HD
PAST, PAGE, BLOCK = 1024, 128, 256
PAGES = PAST // PAGE
BLOCKS = PAST // BLOCK
EPS = 1e-6
SCALE = HD ** -0.5
NEG = -1e30
WINDOWS = (2, 4, 8, 16)
BUF = 15
EDGE = 16
ROT, HALF_ROT, THETA = 16, 8, 500000.0

RING = 4
U_MEM = 0
U_FFN1 = U_MEM + 4
U_WIN = U_FFN1 + 3 * HT
U_MIX = U_WIN + 16
U_FFN2 = U_MIX + KT
U_END = U_FFN2 + 3 * HT
LEAD = 2
X_BANKS = (5, 6, 7, 0, 1, 2, 3, 4)
M_ORDER = (4, 5, 6, 7, 0, 1, 2, 3)
KV_SLOTS = 4
HELD = 6
KV_STREAM = ([("k", b) for b in range(NS)] + [("mk", 0)] + [("v", b) for b in range(4)] + [("mv", 0)] +
             [("v", b) for b in range(4, NS)])
KV_AT = {kb: n for n, kb in enumerate(KV_STREAM)}
GP_PAGES = 6


def shape_constants():
    c = {}
    c["ident"] = np.eye(P, dtype=np.float32)
    c["causal"] = np.where(np.arange(P)[None, :] <= np.arange(P)[:, None], 0.0, NEG).astype(np.float32)
    inv = np.power(np.float32(THETA), -np.arange(HALF_ROT, dtype=np.float32) * np.float32(2.0 / ROT)).astype(np.float32)
    pos = np.concatenate([np.arange(NP), np.full(P, PAST)]).astype(np.float32).reshape(3, P)
    ang = (pos.T[:, :, None] * inv[None, None, :]).astype(np.float32)
    c["rope"] = np.stack([np.cos(ang), np.sin(ang)], axis=1).astype(np.float32)
    band = np.zeros((P, 2, 4, NP), np.float32)
    samp = np.zeros((P, 4, NS), np.float32)
    for g, w in enumerate(WINDOWS):
        for t in range(NP):
            for s in range(max(0, t - w + 1), t + 1):
                band[s % P, s // P, g, t] += 1.0 / min(w, t + 1)
            band[t % P, t // P, g, t] -= 1.0
        for b in range(NS):
            samp[b, g, b] = 1.0 / w - 1.0
            for j in range(BUF - (w - 1), BUF):
                samp[NS + BUF * b + j, g, b] = 1.0 / w
    c["band"] = np.concatenate([band[:, 0, :, 0:P + EDGE], band[:, 1, :, P:NP]], axis=2)
    c["samp"] = samp
    delta = np.zeros((NS, NS, MH), np.float32)
    for b in range(NS):
        delta[b, b, :] = 1.0
    c["delta"] = delta
    back = np.zeros((32, 2, NS), np.float32)
    for r in range(32):
        for hf in range(2):
            back[r, hf, 4 * hf + r // MH] = 1.0
    c["back"] = back
    c["rank"] = np.tile(np.arange(1, BLOCKS + 1, dtype=np.float32), (32, 1))
    return c


def layer(nc, a):
    ctx = ExitStack()
    with ctx:
        cursor = [1152]

        def place(name, shape, dt=F32, at=None):
            size = 4 * int(np.prod(shape[1:]))
            if at is None:
                at = cursor[0]
                cursor[0] += -(-size // 64) * 64
            return nc.alloc_sbuf_tensor_at(name, list(shape), dt, offset=at)

        def sem(name):
            return ctx.enter_context(nc.semaphore(name))

        raw = place("raw", [P, RING, 1024])
        w_hi = place("w_hi", [P, RING, 1024], F32R)
        w_lo = place("w_lo", [P, RING, 1024], F32R)
        xT = place("xT", [P, KT, N])
        x_hi = place("x_hi", [P, KT, N], F32R)
        x_lo_at = cursor[0]
        x_lo = place("x_lo", [P, KT, N], F32R)
        rows = place("rows", [32, PAST + 8], at=x_lo_at)
        probT = place("probT", [P, 2, 2 * NP], at=x_lo_at + 4160)
        band = place("band", [P, 4, 2 * P + EDGE])
        tmp = place("tmp", [P, KT, N])
        mem_kv = place("mem_kv", [P, 2, 512])
        kv = place("kv", [P, KV_SLOTS, PAGES * 512])
        y_rows_s = place("y_rows_s", [P, 512], at=cursor[0])
        root = place("root", [P, N])
        rstd = place("rstd", [P, N])
        sg = place("sg", [P, 2, N])
        h_tmp = place("h_tmp", [P, 2, N])
        ident = place("ident", [P, P])
        causal = place("causal", [P, P])
        ident_b = place("ident_b", [P, P], BF16)
        causal_b = place("causal_b", [P, P], BF16)
        ones = place("ones", [P, P])
        gains = place("gains", [P, 34])
        rope = place("rope", [P, 2, 3, HALF_ROT])
        head_gain = place("head_gain", [P, 4, HD])
        eps_col = place("eps_col", [P, 1])
        dummy = place("dummy", [P, 4])
        page_ids = place("page_ids", [1, NS * PAGES], I32)
        samp = place("samp", [P, 4, NS])
        delta = place("delta", [NS, NS, MH])
        back = place("back", [32, 2, NS])
        rank = place("rank", [32, BLOCKS])
        own8 = place("own8", [NS, MH])
        own_e = place("own_e", [NS, 4, MH])
        logits = place("logits", [P, PAGES, 4, MH])
        logits_m = place("logits_m", [P, 2, NS, CH])
        p_cols = place("p_cols", [P, 2, PAGES, 32])
        pm_cols = place("pm_cols", [P, 2, 32])
        p_own = place("p_own", [32, 32])
        p_own8 = place("p_own8", [NS, 2, 32])
        stats = place("stats", [32, 24])
        qb = place("qb", [P, 2, 512])
        ss_h = place("ss_h", [P, 16])
        var_h = place("var_h", [P, 16])
        sd_h = place("sd_h", [P, 16])
        rs_h = place("rs_h", [P, 16])
        rot = place("rot", [P, 4, 2, MH * HALF_ROT])
        mx = place("mx", [P, 2, 2])
        nb = place("nb", [P, 2, 2])
        sm = place("sm", [P, 2, 2])
        rc = place("rc", [P, 2, 2])
        ext = place("ext", [P, POOL])
        pool_wd = place("pool_wd", [P, 2, P])
        region = cursor[0]
        h_hi = place("h_hi", [P, HT, N], F32R)
        h_lo = place("h_lo", [P, HT, N], F32R)
        end = cursor[0]
        at = [region]

        def over(name, shape, dt=F32):
            t = place(name, shape, dt, at=at[0])
            at[0] += -(-4 * int(np.prod(shape[1:])) // 64) * 64
            assert at[0] <= end, name
            return t

        x_rows = over("x_rows", [P, 3, D])
        m_rows = over("m_rows", [P, 2, D])
        memT = over("memT", [P, KT, NP])
        m_hi = over("m_hi", [P, KT, NP], F32R)
        m_lo = over("m_lo", [P, KT, NP], F32R)
        g_rows = over("g_rows", [34, P])
        at[0] = region
        qp = over("qp", [P, 2, 512])
        kp = over("kp", [P, 2, 512])
        vp = over("vp", [P, 2, 512])
        up = over("up", [P, 2, 512])
        qs = over("qs", [NS, 512])
        ks = over("ks", [NS, 512])
        vs = over("vs", [NS, 512])
        us = over("us", [NS, 512])
        qT = over("qT", [P, 4, NP])
        kT = over("kT", [P, 4, NP])
        qmT = over("qmT", [P, 2, NP])
        mkT = over("mkT", [P, 2, NP])
        prob = over("prob", [P, 2, 2, NP])
        sq_h = over("sq_h", [P, 2, 512])

        banks = ctx.enter_context(nc.psum_tensor("banks", [P, 8, 512], F32))
        bank = [banks[:, i, :] for i in range(8)]

        x_loaded, m_loaded, g_loaded = sem("x_loaded"), sem("m_loaded"), sem("g_loaded")
        id_loaded, c_loaded = sem("id_loaded"), sem("c_loaded")
        pg_loaded, poolw_loaded = sem("pg_loaded"), sem("poolw_loaded")
        raw_loaded = [sem(f"raw_loaded{i}") for i in range(RING)]
        kv_loaded = [sem(f"kv_loaded{i}") for i in range(KV_SLOTS)]
        hi_ready, lo_ready, w_used = sem("hi_ready"), sem("lo_ready"), sem("w_used")
        const_set = sem("const_set")
        g_turned, gains_ready = sem("g_turned"), sem("gains_ready")
        m_turned, memT_ready = sem("m_turned"), sem("memT_ready")
        x_turned, res_ready = sem("x_turned"), sem("res_ready")
        sq_ready, ss_ready, root_ready, rstd_ready = sem("sq_ready"), sem("ss_ready"), sem("root_ready"), sem("rstd_ready")
        xn_ready, xhi_ready, xlo_ready = sem("xn_ready"), sem("xhi_ready"), sem("xlo_ready")
        kvm_done, gu_free = sem("kvm_done"), sem("gu_free")
        silu_ready, hhi_ready, h_ready = sem("silu_ready"), sem("hhi_ready"), sem("h_ready")
        out_done = sem("out_done")
        proj_done, proj_evac = sem("proj_done"), sem("proj_evac")
        vec_step = sem("vec_step")
        var_ready, sd_ready, nrm_ready = sem("var_ready"), sem("sd_ready"), sem("nrm_ready")
        qb_psum, qb_ready, gp_done, k_used, v_used = sem("qb_psum"), sem("qb_ready"), sem("gp_done"), sem("k_used"), sem("v_used")
        qk_turned, qkT_ready = sem("qk_turned"), sem("qkT_ready")
        pooled_psum, pooled_ready, pool_psum, pool_ready = sem("pooled_psum"), sem("pooled_ready"), sem("pool_psum"), sem("pool_ready")
        ext_ready = sem("ext_ready")
        sc_ready, nb_ready, exp_done, prob_ready = sem("sc_ready"), sem("nb_ready"), sem("exp_done"), sem("prob_ready")
        pT_psum, probT_ready, pv_done, head_ready = sem("pT_psum"), sem("probT_ready"), sem("pv_done"), sem("head_ready")
        own_ready, lt_psum, rows_ready = sem("own_ready"), sem("lt_psum"), sem("rows_ready")
        yr_psum, yr_ready, mask_ready = sem("yr_psum"), sem("yr_ready"), sem("mask_ready")
        smn_ready, sme_ready, p_ready, p_psum, pcols_ready = (sem("smn_ready"), sem("sme_ready"), sem("p_ready"),
                                                              sem("p_psum"), sem("pcols_ready"))
        ys_ready = sem("ys_ready")
        cat_hi, cat_lo = sem("cat_hi"), sem("cat_lo")
        y_turned, y_ready = sem("y_turned"), sem("y_ready")
        mid_stored, stored = sem("mid_stored"), sem("stored")
        MID_STORES = 8

        def cols_view(w, k):
            return w[0].rearrange("(k p) c -> p k c", p=P)

        ffn_in = [cols_view(a["ffn1_w_in"], KT), cols_view(a["ffn2_w_in"], KT)]
        ffn_out = [cols_view(a["ffn1_w_out"], HT), cols_view(a["ffn2_w_out"], HT)]
        w_in, w_mix, w_mem = cols_view(a["w_in"], KT), cols_view(a["w_out"], KT), cols_view(a["mem_w_kv"], KT)

        def kv_level(n):
            total = 0
            for i in range(n % KV_SLOTS, n + 1, KV_SLOTS):
                total += 16 * (PAGES if KV_STREAM[i][0] in "kv" else 1)
            return total

        def kv_wait(eng, kind, b):
            n = KV_AT[(kind, b)]
            eng.wait_ge(kv_loaded[n % KV_SLOTS], kv_level(n))
            return n % KV_SLOTS

        V_ORDER = [0, 1, 2, 3, "mem", 4, 5, 6, 7]

        def raw_level(n, i):
            return 16 * (n // RING + 1) + 16 * i + (16 if n >= U_WIN + 12 else 0)

        def y_rows(eng, g):
            eng.wait_ge(y_turned, g + 1)
            if g < 2:
                dst, src = kv[0:NS, 0, g * 512:(g + 1) * 512], bank[g][0:NS, :]
            else:
                dst, src = kv[:, 1, (g - 2) * 512:(g - 1) * 512], bank[g][:, :]
            if eng is act_engine[0]:
                eng.activation(dst, src, ACT.Copy).then_inc(y_ready, 1)
            else:
                eng.tensor_copy(dst, src).then_inc(y_ready, 1)

        act_engine = [None]
        PV_ORDER = (0, 2, 1)
        PV_USED = {0: 4, 2: 5, 1: 9}

        def keys_of(pair, t):
            return P if pair < MH // 2 and t == 0 else NP

        def steps(eng):
            yield from [("X", 0), ("HA", 0), ("POOL", 0), ("SA", 0), ("L", 4), ("HB", 0), ("SB", 0), ("HA", 1), ("SC", 0),
                        ("L", 5), ("HB", 1), ("SD", 0), ("HA", 2), ("L", 6), ("HB", 2), ("HA", 3), ("L", 7), ("SA", 1),
                        ("HB", 3), ("SB", 1), ("HA", 4), ("L", 8), ("L", 9), ("SC", 1), ("HB", 4), ("HA", 5), ("L", 10),
                        ("L", 11), ("SD", 1), ("SA", 2), ("SB", 2), ("HB", 5), ("SC", 2), ("SD", 2), ("PV", 0), ("PV", 2),
                        ("PV", 1)]

        block = ctx.enter_context(nc.Block())

        @block.sync
        def _(sp):
            def load_unit(n0, j, i, src):
                n = n0 + j
                if not (isinstance(i, int) and n + 4 * i < RING):
                    sp.wait_ge(lo_ready, 4 * i + n - RING + 1)
                sp.dma_start(raw[:, n % RING, :].rearrange("p (k c) -> p k c", k=src.shape[1]), src)\
                    .then_inc(raw_loaded[n % RING], 16)

            def ffn_in_units(f, lo, hi):
                n0 = (U_FFN1, U_FFN2)[f]
                with sp.Fori(lo, hi) as i:
                    for j in range(4):
                        col = (j // 2) * P + (j % 2) * DFF
                        load_unit(n0, j, i, ffn_in[f][:, :, ds(i * (2 * P) + col, P)])

            def ffn_out_units(f):
                n0 = (U_FFN1, U_FFN2)[f] + 2 * HT
                for j in range(2):
                    load_unit(n0, j, 0, ffn_out[f][:, j:j + 1, :])
                with sp.Fori(0, 5) as i:
                    for j in range(4):
                        load_unit(n0 + 2, j, i, ffn_out[f][:, ds(i * 4 + (2 + j), 1), :])

            def page_of(b, t):
                return sp.value_load(page_ids[0:1, b * PAGES + t:b * PAGES + t + 1], min_val=0,
                                     max_val=a["cache_k"].shape[1] - 1)

            def load_kv(n):
                kind, b = KV_STREAM[n]
                if n >= KV_SLOTS:
                    was, wb = KV_STREAM[n - KV_SLOTS]
                    if was in ("k", "mk"):
                        sp.wait_ge(k_used, wb + 1 if was == "k" else 12)
                    else:
                        sp.wait_ge(v_used, V_ORDER.index(wb if was == "v" else "mem") + 1)
                slot = n % KV_SLOTS
                if kind in "kv":
                    cache = a["cache_k"] if kind == "k" else a["cache_v"]
                    for t in range(PAGES):
                        page = pages[b][t] if b < HELD else page_of(b, t)
                        sp.dma_start(kv[:, slot, t * 512:(t + 1) * 512],
                                     cache[0, ds(page, 1)].rearrange("o p h d -> p (o h d)"))\
                            .then_inc(kv_loaded[slot], 16)
                else:
                    cache = a["cache_mem_k"] if kind == "mk" else a["cache_mem_v"]
                    sp.dma_start(kv[:, slot, :].rearrange("p (b t c) -> p b t c", b=NS, t=2),
                                 cache[0].rearrange("b (t p) h d -> p b t (h d)", p=P)).then_inc(kv_loaded[slot], 16)

            sp.dma_start(ident[:], a["ident"]).then_inc(id_loaded, 16)
            sp.dma_start(m_rows[:], a["mem_prompt"][0].rearrange("(t p) d -> p t d", p=P)).then_inc(m_loaded, 16)
            for j, name in enumerate(("ffn1_norm", "mix_norm", "mem_norm", "ffn2_norm")):
                sp.dma_start(g_rows[8 * j:8 * j + 8, :], a[name][0].rearrange("(k p) -> k p", p=P)).then_inc(g_loaded, 16)
            sp.dma_start(g_rows[32:34, :], a["pool_scale"][0].rearrange("(k p) -> k p", p=P)).then_inc(g_loaded, 16)
            sp.dma_start(x_rows[0:NS, 0, :], a["x_sample"][:, 0, :]).then_inc(x_loaded, 16)
            sp.dma_start(x_rows[:, 1:3, :], a["x_prompt"][0].rearrange("(t p) d -> p t d", p=P)).then_inc(x_loaded, 16)
            for j in range(4):
                load_unit(U_MEM, j, 0, w_mem[:, 2 * j:2 * j + 2, :])
            sp.dma_start(page_ids[:], a["page_table"].rearrange("b g -> (b g)").unsqueeze(0)).then_inc(pg_loaded, 16)
            for j, name in enumerate(("q_norm", "k_norm", "mem_q_norm", "mem_k_norm")):
                sp.dma_start(head_gain[:, j, :], a[name][0].partition_broadcast(P)).then_inc(c_loaded, 16)
            for dst, name in ((rope, "rope"), (samp, "samp"), (delta, "delta"), (back, "back"), (rank, "rank"),
                              (causal, "causal"), (band, "band")):
                sp.dma_start(dst[:], a[name]).then_inc(c_loaded, 16)
            sp.dma_start(ext[NS:P, :], a["state_pool"][0].rearrange("b j c -> (b j) c")).then_inc(c_loaded, 16)
            sp.wait_ge(const_set, 1)
            for g in range(4):
                lo = HD * (g % 2)
                sp.dma_start(pool_wd[lo:lo + HD, g // 2, lo:lo + HD], a["pool_w"][0, g]).then_inc(poolw_loaded, 16)
            sp.dma_start(a["state_out"][0, :, 0:BUF - 1, :], a["state_pool"][0, :, 1:BUF, :]).then_inc(stored, 16)
            sp.wait_ge(pg_loaded, 16)
            pages = [[page_of(b, t) for t in range(PAGES)] for b in range(HELD)]
            for s, (lo, hi) in enumerate(((0, 5), (5, 8), (8, 11))):
                ffn_in_units(0, lo, hi)
                load_kv(s)
            ffn_out_units(0)
            load_kv(3)
            def load_projection(r):
                j = r % 4
                if r < 12:
                    c0 = POOL + MOBA * (r // 4)
                    load_unit(U_WIN, r, 0, w_in[:, 2 * j:2 * j + 2, c0:c0 + 512])
                    return
                sp.wait_ge(lo_ready, U_WIN + r - RING + 1)
                dst = raw[:, (U_WIN + r) % RING, :].rearrange("p (k c) -> p k c", k=2)
                last = POOL + 3 * MOBA
                sp.dma_start(dst[:, :, 0:256], w_in[:, 2 * j:2 * j + 2, 0:256]).then_inc(raw_loaded[(U_WIN + r) % RING], 16)
                sp.dma_start(dst[:, :, 256:512], w_in[:, 2 * j:2 * j + 2, last:last + 256])\
                    .then_inc(raw_loaded[(U_WIN + r) % RING], 16)

            for r in range(12):
                load_projection(r)
            load_kv(4)
            load_projection(12)
            load_projection(13)
            load_kv(5)
            load_projection(14)
            load_projection(15)
            for j in range(2):
                load_unit(U_MIX, j, 0, w_mix[:, j:j + 1, :])
            load_kv(6)
            for j in range(2, 4):
                load_unit(U_MIX, j, 0, w_mix[:, j:j + 1, :])
            for n in range(7, len(KV_STREAM)):
                load_kv(n)
            sp.wait_ge(nrm_ready, 7)
            sp.wait_ge(proj_evac, 12)
            sp.dma_start(a["k_out"][0, 0].rearrange("(t p) h d -> p t (h d)", p=P), kp[:]).then_inc(mid_stored, 16)
            sp.dma_start(a["v_out"][0, 0].rearrange("(t p) h d -> p t (h d)", p=P), vp[:]).then_inc(mid_stored, 16)
            sp.dma_start(a["mk_out"][0, 0].rearrange("(t p) h d -> p t (h d)", p=P), mem_kv[:, :, 0:256])\
                .then_inc(mid_stored, 16)
            sp.dma_start(a["mv_out"][0, 0].rearrange("(t p) h d -> p t (h d)", p=P), mem_kv[:, :, 256:512])\
                .then_inc(mid_stored, 16)
            sp.dma_start(a["buf_out"][0, 0], up[P - BUF:P, 1, 0:POOL]).then_inc(mid_stored, 16)
            sp.dma_start(a["ks_out"][0, :, 0].rearrange("b h d -> b (h d)"), ks[:]).then_inc(mid_stored, 16)
            sp.dma_start(a["vs_out"][0, :, 0].rearrange("b h d -> b (h d)"), vs[:]).then_inc(mid_stored, 16)
            sp.dma_start(a["state_out"][0, :, BUF - 1, :], us[:, 0:POOL]).then_inc(mid_stored, 16)
            for j in range(4, KT):
                load_unit(U_MIX, j, 0, w_mix[:, j:j + 1, :])
            ffn_in_units(1, 0, 11)
            ffn_out_units(1)
            sp.wait_ge(y_ready, 6)
            sp.dma_start(a["y_sample"][:, 0, :], kv[0:NS, 0, 0:D]).then_inc(stored, 16)
            sp.dma_start(a["y_prompt"][0].rearrange("(t p) d -> p t d", p=P),
                         kv[:, 1, 0:2 * D].rearrange("p (t d) -> p t d", t=2)).then_inc(stored, 16)
            sp.wait_ge(mid_stored, 16 * MID_STORES)
            sp.wait_ge(stored, 16 * 3)

        @block.gpsimd
        def _(pool):
            pool.memset(pool_wd[:], 0.0).then_inc(const_set, 1)
            pool.memset(ones[:], 1.0).then_inc(const_set, 1)
            pool.memset(eps_col[:], EPS).then_inc(const_set, 1)
            pool.memset(dummy[:], 1.0).then_inc(const_set, 1)
            for b in range(NS + 4):
                pool.wait_ge(qb_ready, b + 1)
                if b < NS:
                    slot = kv_wait(pool, "k", b)
                    k_rows = kv[:, slot, 0:GP_PAGES * 512].rearrange("p (t c) -> p t c", c=512)
                    pool.tensor_tensor(k_rows, k_rows, qb[:, b % 2, :].unsqueeze(1).to_broadcast([P, GP_PAGES, 512]),
                                       ALU.mult).then_inc(gp_done, 1)
                else:
                    g = b - NS
                    slot = kv_wait(pool, "mk", 0)
                    m_keys = kv[:, slot, g * 1024:(g + 1) * 1024].rearrange("p (b t c) -> p b t c", b=2, t=2)
                    q_two = qb[:, b % 2, :].rearrange("p (b c) -> p b c", b=2).unsqueeze(2).to_broadcast([P, 2, 2, 256])
                    pool.tensor_tensor(m_keys, m_keys, q_two, ALU.mult).then_inc(gp_done, 1)

        @block.scalar
        def _(act):
            def split(n0, j=0, i=0):
                n = n0 + j
                act.wait_ge(raw_loaded[n % RING], raw_level(n, i))
                if not (isinstance(i, int) and n + 4 * i < RING):
                    act.wait_ge(w_used, 4 * i + n - RING + 1)
                act.activation(w_hi[:, n % RING, :], raw[:, n % RING, :], ACT.Copy).then_inc(hi_ready, 1)

            def norm_squares(inst, src, cols, order, ready, base):
                if inst:
                    act.wait_ge(xlo_ready, KT * inst)
                for idx, m in enumerate(order):
                    act.wait_ge(ready, base + idx + 1)
                    act.activation(tmp[:, m, 0:cols], src[:, m, :], ACT.Square).then_inc(sq_ready, 1)

            def norm_root(inst, cols, bk):
                act.wait_ge(ss_ready, inst + 1)
                act.activation(root[:, 0:cols], bank[bk][:, 0:cols], ACT.Sqrt, bias=eps_col[:, 0:1],
                               scale=1.0 / D).then_inc(root_ready, 1)

            def norm_hi(inst, dst, cols, order):
                for idx, m in enumerate(order):
                    act.wait_ge(xn_ready, KT * inst + idx + 1)
                    act.activation(dst[:, m, :], tmp[:, m, 0:cols], ACT.Copy).then_inc(xhi_ready, 1)

            def silu(f, c, s):
                act.wait_ge(w_used, (U_FFN1, U_FFN2)[f] + 2 * c + 2)
                act.activation(sg[:, s, :], bank[2 * s][:, 0:N], ACT.Silu).then_inc(silu_ready, 1)

            def table(func, k):
                act.activation(dummy[:, k:k + 1], dummy[:, 3:4], func)

            def ffn(f):
                n0 = (U_FFN1, U_FFN2)[f]
                table(ACT.Silu, 0)
                with act.Fori(0, HT // 2) as i:
                    for s in range(2):
                        split(n0 + 2 + 2 * s, 0, i)
                        split(n0 + 3 + 2 * s, 0, i)
                        silu(f, i * 2 + s, s)
                with act.Fori(0, 5) as i:
                    for j in range(4):
                        split(n0 + 2 * HT + LEAD, j, i)

            def head_sd(inst, nrows, width):
                act.wait_ge(var_ready, inst + 1)
                act.activation(sd_h[0:nrows, 0:width], var_h[0:nrows, 0:width], ACT.Sqrt).then_inc(sd_ready, 1)

            def evac(nb_):
                for tt in range(3):
                    if tt < 2:
                        act.wait_ge(proj_done, 2 * nb_ + tt + 1)
                    else:
                        act.wait_ge(w_used, U_WIN + 4 * nb_ + 4)
                    src = bank[3 * (nb_ % 2) + tt]
                    if tt == 0:
                        act.activation((qs, ks, vs, us)[nb_][:], src[0:NS, :], ACT.Copy).then_inc(proj_evac, 1)
                    else:
                        act.activation((qp, kp, vp, up)[nb_][:, tt - 1, :], src[:, :], ACT.Copy).then_inc(proj_evac, 1)

            def queries(b):
                act.wait_ge(qb_psum, b + 1)
                if b >= 2:
                    act.wait_ge(k_used, b - 1)
                act.activation(qb[:, b % 2, :], bank[6][:, :], ACT.Copy).then_inc(qb_ready, 1)

            act_engine[0] = act
            act.wait_ge(const_set, 4)
            table(ACT.Sqrt, 1)
            for g in range(4):
                act.wait_ge(m_turned, g + 1)
                act.activation(memT[:, 2 * g:2 * g + 2, :].rearrange("p k c -> p (k c)"), bank[g][:, :], ACT.Copy)\
                    .then_inc(memT_ready, 1)
            for k in range(KT):
                act.wait_ge(memT_ready, k // 2 + 1)
                act.activation(tmp[:, k, 0:NP], memT[:, k, :], ACT.Square).then_inc(sq_ready, 1)
            split(0)
            split(1)
            norm_root(0, NP, 6)
            norm_hi(0, m_hi, NP, range(KT))
            split(2)
            split(3)
            norm_squares(1, xT, N, range(KT), res_ready, 0)
            norm_root(1, N, 7)
            norm_hi(1, x_hi, N, range(KT))
            split(4)
            split(5)
            ffn(0)
            table(ACT.Sqrt, 1)
            split(U_WIN)
            split(U_WIN + 1)
            norm_squares(2, xT, N, M_ORDER, res_ready, KT)
            norm_root(2, N, 4)
            norm_hi(2, x_hi, N, M_ORDER)
            for r in range(2, 6):
                split(U_WIN + r)
            evac(0)
            split(U_WIN + 6)
            split(U_WIN + 7)
            head_sd(0, NS, MH)
            queries(0)
            split(U_WIN + 8)
            split(U_WIN + 9)
            head_sd(1, P, 2 * MH)
            split(U_WIN + 10)
            split(U_WIN + 11)
            evac(1)
            queries(1)
            split(U_WIN + 12)
            split(U_WIN + 13)
            head_sd(2, NS, MH)
            head_sd(3, P, 2 * MH)
            queries(2)
            split(U_WIN + 14)
            split(U_WIN + 15)
            evac(2)
            queries(3)
            evac(3)
            act.wait_ge(proj_evac, 10)
            act.activation(ext[0:NS, :], us[:, 0:POOL], ACT.Copy).then_inc(ext_ready, 1)
            split(U_MIX)
            split(U_MIX + 1)
            head_sd(4, NS, CH)
            head_sd(5, P, 2 * CH)
            head_sd(6, P, 2 * CH)
            queries(4)
            table(ACT.Exp, 2)
            for what, k in steps(act):
                if what == "X":
                    for g, dst in enumerate((qT, qT, kT, kT, qmT, mkT)):
                        act.wait_ge(qk_turned, g + 1)
                        half = 2 * (g % 2) if g < 4 else 0
                        act.activation(dst[:, half:half + 2, :].rearrange("p k c -> p (k c)"), bank[(g if g < 4 else g - 4)][:, :],
                                       ACT.Copy).then_inc(qkT_ready, 1)
                elif what == "POOL":
                    for pr in range(2):
                        act.wait_ge(pooled_psum, pr + 1)
                        act.activation(sg[:, pr, :], bank[4 + pr][:, 0:N], ACT.Copy).then_inc(pooled_ready, 1)
                    for pr in range(2):
                        act.wait_ge(pool_psum, pr + 1)
                        act.activation(tmp[:, pr, :], bank[4 + pr][:, 0:N], ACT.Copy, scale=gains[:, 32 + pr:33 + pr])\
                            .then_inc(pool_ready, 1)
                elif what == "HA":
                    act.wait_ge(nb_ready, k + 1)
                    if k:
                        act.wait_ge(pT_psum, k)
                    for h in range(2):
                        for t in range(2):
                            n = keys_of(k, t)
                            act.activation(prob[:, h, t, 0:n], bank[h][:, t * NP:t * NP + n], ACT.Exp, scale=SCALE,
                                           bias=nb[:, h, t:t + 1], accum_out=sm[:, h, t:t + 1]).then_inc(exp_done, 1)
                elif what == "HB":
                    act.wait_ge(pT_psum, k + 1)
                    if k:
                        act.wait_ge(pv_done, k)
                    n = 3 * P if k < MH // 2 else 4 * P
                    act.activation(probT[:, :, 0:n], banks[:, 2:4, 0:n], ACT.Copy).then_inc(probT_ready, 1)
                    act.wait_ge(pv_done, k + 1)
                    act.activation(tmp[:, 2 + k, NS:N], bank[7][:, 0:NP], ACT.Copy).then_inc(head_ready, 1)
                elif what == "L":
                    if k + 1 < NS + 4:
                        queries(k + 1)
                elif what == "SA":
                    act.wait_ge(lt_psum, k + 1)
                    if k:
                        act.wait_ge(p_psum, k)
                    if k < 2:
                        act.activation(rows[:, 0:512], bank[4][0:32, :], ACT.Copy).then_inc(rows_ready, 1)
                        act.activation(rows[:, 512:1024], bank[5][0:32, :], ACT.Copy).then_inc(rows_ready, 1)
                        act.activation(rows[:, 1024:1025], bank[7][0:32, 256:257], ACT.Copy).then_inc(rows_ready, 1)
                    else:
                        act.activation(rows[:, 0:NP], bank[4][0:32, 0:NP], ACT.Copy).then_inc(rows_ready, 1)
                elif what == "SC":
                    width = PAST + 1 if k < 2 else NP
                    act.wait_ge(smn_ready, k + 1)
                    act.activation(rows[:, 0:width], rows[:, 0:width], ACT.Exp, scale=SCALE, bias=stats[:, 15:16],
                                   accum_out=stats[:, 16:17]).then_inc(sme_ready, 1)
                elif what == "SD":
                    act.wait_ge(p_psum, k + 1)
                    if k < 2:
                        act.activation(p_cols[:, k % 2, :, :].rearrange("p t c -> p (t c)"), bank[4][:, 0:256], ACT.Copy)\
                            .then_inc(pcols_ready, 1)
                        act.activation(p_own8[:, k, :], bank[7][0:NS, 320:352], ACT.Copy).then_inc(pcols_ready, 1)
                    else:
                        act.activation(pm_cols[:].rearrange("p t c -> p (t c)"), bank[4][:, 0:64], ACT.Copy)\
                            .then_inc(pcols_ready, 1)
                elif what == "PV":
                    act.wait_ge(v_used, PV_USED[k])
                    act.activation(y_rows_s[:], bank[5][:, :], ACT.Copy).then_inc(yr_ready, 1)
            act.wait_ge(ys_ready, 6)
            act.wait_ge(head_ready, 6)
            act.wait_ge(pool_ready, 2)
            for m in range(KT):
                act.activation(x_hi[:, m, :], tmp[:, m, :], ACT.Copy).then_inc(cat_hi, 1)
            table(ACT.Sqrt, 1)
            for r in range(2, KT + 2):
                split(U_MIX + r)
            norm_squares(3, xT, N, M_ORDER, res_ready, 2 * KT)
            norm_root(3, N, 4)
            norm_hi(3, x_hi, N, M_ORDER)
            ffn(1)
            for g in range(1, 6, 2):
                y_rows(act, g)


        @block.vector
        def _(vec):
            chained = [0]

            def chain(ins):
                chained[0] += 1
                ins.then_inc(vec_step, 1)
                vec.wait_ge(vec_step, chained[0])

            def split(n0, j=0, i=0):
                n = n0 + j
                vec.wait_ge(hi_ready, 4 * i + n + 1)
                vec.tensor_tensor(w_lo[:, n % RING, :], raw[:, n % RING, :], w_hi[:, n % RING, :].bitcast(F32),
                                  ALU.subtract).then_inc(lo_ready, 1)

            def norm(inst, src, g0, hi, lo, cols, order):
                vec.wait_ge(root_ready, inst + 1)
                vec.reciprocal(rstd[:, 0:cols], root[:, 0:cols]).then_inc(rstd_ready, 1)
                vec.wait_ge(rstd_ready, inst + 1)
                order = list(order)
                for idx in range(KT + 1):
                    if idx < KT:
                        m = order[idx]
                        vec.scalar_tensor_tensor(out=tmp[:, m, 0:cols], in0=src[:, m, :], scalar=gains[:, g0 + m:g0 + m + 1],
                                                 in1=rstd[:, 0:cols], op0=ALU.mult, op1=ALU.mult).then_inc(xn_ready, 1)
                    if idx >= 1:
                        m = order[idx - 1]
                        vec.wait_ge(xhi_ready, KT * inst + idx)
                        vec.tensor_tensor(lo[:, m, :], tmp[:, m, 0:cols], hi[:, m, :].bitcast(F32), ALU.subtract)\
                            .then_inc(xlo_ready, 1)

            def residual(inst, last, weight):
                for idx, m in enumerate(M_ORDER):
                    if idx < KT - 1:
                        vec.wait_ge(out_done, (KT - 1) * inst + idx + 1)
                    else:
                        vec.wait_ge(w_used, last + 1)
                    vec.scalar_tensor_tensor(out=xT[:, m, :], in0=bank[m][:, 0:N], scalar=weight, in1=xT[:, m, :],
                                             op0=ALU.mult, op1=ALU.add).then_inc(res_ready, 1)

            def ffn(f):
                n0 = (U_FFN1, U_FFN2)[f]
                with vec.Fori(0, HT // 2) as i:
                    for s in range(2):
                        split(n0 + 2 + 2 * s, 0, i)
                        split(n0 + 3 + 2 * s, 0, i)
                        c = i * 2 + s
                        vec.wait_ge(silu_ready, c + (HT * f + 1))
                        vec.tensor_tensor(h_tmp[:, s, :], sg[:, s, :], bank[2 * s + 1][:, 0:N], ALU.mult)\
                            .then_inc(gu_free, 1)
                        vec.wait_ge(gu_free, c + (HT * f + 3))
                        vec.tensor_copy(h_hi[:, ds(c, 1), :].rearrange("p a n -> p (a n)"), h_tmp[:, s, :]).then_inc(hhi_ready, 1)
                        vec.wait_ge(hhi_ready, c + (HT * f + 1))
                        vec.tensor_tensor(h_lo[:, ds(c, 1), :].rearrange("p a n -> p (a n)"), h_tmp[:, s, :],
                                          h_hi[:, ds(c, 1), :].rearrange("p a n -> p (a n)").bitcast(F32), ALU.subtract)\
                            .then_inc(h_ready, 1)
                with vec.Fori(0, 5) as i:
                    for j in range(4):
                        split(n0 + 2 * HT + LEAD, j, i)

            def head_norm(inst, buf, nt, nh, gain, rope_at, evacuated):
                nrows = buf.shape[0]
                vec.wait_ge(proj_evac, evacuated)
                sq = sq_h[0:nrows, 0:nt, 0:nh * HD]
                chain(vec.tensor_tensor(sq, buf, buf, ALU.mult))
                chain(vec.tensor_reduce(ss_h[0:nrows, 0:nt * nh].rearrange("p (t h) -> p t h", t=nt),
                                        sq.rearrange("p t (h d) -> p t h d", d=HD), AX.X, ALU.add))
                vec.tensor_scalar(var_h[0:nrows, 0:nt * nh], ss_h[0:nrows, 0:nt * nh], 1.0 / HD, EPS, ALU.mult, ALU.add)\
                    .then_inc(var_ready, 1)
                vec.wait_ge(sd_ready, inst + 1)
                chain(vec.reciprocal(rs_h[0:nrows, 0:nt * nh], sd_h[0:nrows, 0:nt * nh]))
                heads = buf.rearrange("p t (h d) -> p t h d", d=HD)
                for t in range(nt):
                    r = rs_h[0:nrows, t * nh:(t + 1) * nh].unsqueeze(2).to_broadcast([nrows, nh, HD])
                    one = vec.tensor_tensor(heads[:, t], heads[:, t], r, ALU.mult)
                    if t < nt - 1:
                        one.then_inc(vec_step, 1)
                        chained[0] += 1
                chain(one)
                g = head_gain[0:nrows, gain, :].unsqueeze(1).to_broadcast([nrows, nt * nh, HD])
                flat = buf.rearrange("p t (h d) -> p (t h) d", d=HD) if nh * HD == 512 else None
                for t in range(nt):
                    g = head_gain[0:nrows, gain, :].unsqueeze(1).to_broadcast([nrows, nh, HD])
                    one = vec.tensor_tensor(heads[:, t], heads[:, t], g, ALU.mult)
                    if rope_at is None and t == nt - 1:
                        one.then_inc(nrm_ready, 1)
                    elif t < nt - 1:
                        one.then_inc(vec_step, 1)
                        chained[0] += 1
                    else:
                        chain(one)
                if rope_at is None:
                    return
                x1, x2 = heads[:, :, :, 0:HALF_ROT], heads[:, :, :, HALF_ROT:ROT]
                cs = [rope[0:nrows, q, rope_at:rope_at + nt, :].unsqueeze(2).to_broadcast([nrows, nt, nh, HALF_ROT])
                      for q in range(2)]
                r = [rot[0:nrows, q, 0:nt, :].rearrange("p t (h d) -> p t h d", h=nh) for q in range(4)]
                for q, (x, cos_sin) in enumerate(((x1, cs[0]), (x2, cs[1]), (x2, cs[0]), (x1, cs[1]))):
                    one = vec.tensor_tensor(r[q], x, cos_sin, ALU.mult)
                    if q < 3:
                        one.then_inc(vec_step, 1)
                        chained[0] += 1
                chain(one)
                vec.tensor_tensor(x1, r[0], r[1], ALU.subtract)
                vec.tensor_tensor(x2, r[2], r[3], ALU.add).then_inc(nrm_ready, 1)

            def own_keys(hf):
                if hf == 0:
                    chain(vec.tensor_tensor(sq_h[0:NS, 0, :], qs[:], ks[:], ALU.mult))
                    chain(vec.tensor_reduce(own8[:], sq_h[0:NS, 0, :].rearrange("p (h d) -> p h d", d=HD), AX.X, ALU.add))
                else:
                    vec.wait_ge(lt_psum, 1)
                vec.tensor_tensor(own_e[:], delta[:, 4 * hf:4 * hf + 4, :], own8[:].unsqueeze(1).to_broadcast([NS, 4, MH]),
                                  ALU.mult).then_inc(own_ready, 1)

            def key_logits(b):
                if b < NS:
                    slot = kv_wait(vec, "k", b)
                    vec.wait_ge(qb_ready, b + 1)
                    if b == 4:
                        vec.wait_ge(lt_psum, 1)
                    part = kv[:, slot, GP_PAGES * 512:PAGES * 512].rearrange("p (t c) -> p t c", c=512)
                    chain(vec.tensor_tensor(part, part, qb[:, b % 2, :].unsqueeze(1)
                                            .to_broadcast([P, PAGES - GP_PAGES, 512]), ALU.mult))
                    vec.tensor_reduce(logits[:, GP_PAGES:PAGES, b % 4, :],
                                      part.rearrange("p t (h d) -> p t h d", d=HD), AX.X, ALU.add)
                    vec.wait_ge(gp_done, b + 1)
                    part = kv[:, slot, 0:GP_PAGES * 512].rearrange("p (t h d) -> p t h d", d=HD, h=MH)
                    vec.tensor_reduce(logits[:, 0:GP_PAGES, b % 4, :], part, AX.X, ALU.add).then_inc(k_used, 1)
                else:
                    g = b - NS
                    slot = KV_AT[("mk", 0)] % KV_SLOTS
                    vec.wait_ge(gp_done, b + 1)
                    m_keys = kv[:, slot, g * 1024:(g + 1) * 1024].rearrange("p (b t h d) -> p t b h d", b=2, t=2, h=CH)
                    for t in range(2):
                        red = vec.tensor_reduce(logits_m[:, t, 2 * g:2 * g + 2, :], m_keys[:, t], AX.X, ALU.add)
                    red.then_inc(k_used, 1)

            vec.wait_ge(g_turned, 1)
            vec.tensor_copy(gains[:], bank[4][:, 0:34]).then_inc(gains_ready, 1)
            for m in range(KT):
                vec.wait_ge(x_turned, m + 1)
                vec.tensor_copy(xT[:, m, :], bank[X_BANKS[m]][:, 0:N]).then_inc(res_ready, 1)
            split(0)
            split(1)
            vec.wait_ge(gains_ready, 1)
            norm(0, memT, 16, m_hi, m_lo, NP, range(KT))
            split(2)
            split(3)
            norm(1, xT, 0, x_hi, x_lo, N, range(KT))
            split(4)
            split(5)
            vec.wait_ge(kvm_done, 1)
            vec.tensor_copy(mem_kv[:, 0, :], bank[4][:, :]).then_inc(gu_free, 1)
            vec.wait_ge(w_used, 4)
            vec.tensor_copy(mem_kv[:, 1, :], bank[5][:, :]).then_inc(gu_free, 1)
            ffn(0)
            split(U_WIN)
            split(U_WIN + 1)
            residual(0, U_WIN - 1, 0.5)
            norm(2, xT, 8, x_hi, x_lo, N, M_ORDER)
            for r in range(2, 6):
                split(U_WIN + r)
            vec.wait_ge(c_loaded, 16 * 12)
            vec.tensor_copy(ident_b[:], ident[:]).then_inc(mask_ready, 1)
            vec.tensor_copy(causal_b[:], causal[:]).then_inc(mask_ready, 1)
            head_norm(0, qs[:].unsqueeze(1), 1, MH, 0, 2, 1)
            split(U_WIN + 6)
            split(U_WIN + 7)
            key_logits(0)
            split(U_WIN + 8)
            split(U_WIN + 9)
            head_norm(1, qp[:], 2, MH, 0, 0, 3)
            split(U_WIN + 10)
            split(U_WIN + 11)
            key_logits(1)
            head_norm(2, ks[:].unsqueeze(1), 1, MH, 1, 2, 4)
            head_norm(3, kp[:], 2, MH, 1, 0, 6)
            split(U_WIN + 12)
            split(U_WIN + 13)
            own_keys(0)
            split(U_WIN + 14)
            split(U_WIN + 15)
            key_logits(2)
            head_norm(4, us[:, 256:512].unsqueeze(1), 1, CH, 2, None, 10)
            head_norm(5, up[:, :, 256:512], 2, CH, 2, None, 12)
            head_norm(6, mem_kv[:, :, 0:256], 2, CH, 3, None, 12)
            split(U_MIX)
            split(U_MIX + 1)
            key_logits(3)
            for what, k in steps(vec):
                if what == "L":
                    key_logits(k)
                elif what == "HA":
                    vec.wait_ge(sc_ready, k + 1)
                    if k:
                        vec.wait_ge(exp_done, 4 * k)
                    if k < MH // 2:
                        vec.tensor_reduce(mx[:, :, 0], banks[:, 0:2, 0:P], AX.X, ALU.max).then_inc(vec_step, 1)
                        chained[0] += 1
                        chain(vec.tensor_reduce(mx[:, :, 1], banks[:, 0:2, NP:2 * NP], AX.X, ALU.max))
                    else:
                        chain(vec.tensor_reduce(mx[:], banks[:, 0:2, :].rearrange("p h (t c) -> p h t c", t=2), AX.X, ALU.max))
                    vec.tensor_scalar(nb[:], mx[:], -SCALE, None, ALU.mult).then_inc(nb_ready, 1)
                elif what == "HB":
                    vec.wait_ge(exp_done, 4 * k + 4)
                    chain(vec.reciprocal(rc[:], sm[:]))
                    for t in range(2):
                        n = keys_of(k, t)
                        some = vec.tensor_tensor(prob[:, :, t, 0:n], prob[:, :, t, 0:n],
                                                 rc[:, :, t:t + 1].to_broadcast([P, 2, n]), ALU.mult)
                    some.then_inc(prob_ready, 1)
                elif what == "SA" and k == 1:
                    own_keys(1)
                elif what == "SB":
                    vec.wait_ge(rows_ready, (3, 6, 7)[k])
                    if k:
                        vec.wait_ge(sme_ready, k)
                    if k < 2:
                        blocks = rows[:, 0:PAST].rearrange("p (b c) -> p b c", b=BLOCKS)
                        chain(vec.tensor_reduce(stats[:, 0:4], blocks, AX.X, ALU.add))
                        chain(vec.tensor_reduce(stats[:, 4:5], stats[:, 0:4], AX.X, ALU.min))
                        chain(vec.scalar_tensor_tensor(out=stats[:, 5:9], in0=stats[:, 0:4], scalar=stats[:, 4:5],
                                                       in1=rank[:], op0=ALU.is_equal, op1=ALU.mult))
                        chain(vec.tensor_reduce(stats[:, 9:10], stats[:, 5:9], AX.X, ALU.max))
                        chain(vec.tensor_scalar(stats[:, 10:14], stats[:, 5:9], stats[:, 9:10], NEG, ALU.is_equal, ALU.mult))
                        chain(vec.tensor_tensor(blocks, blocks, stats[:, 10:14].unsqueeze(2).to_broadcast([32, BLOCKS, BLOCK]),
                                                ALU.add))
                    width = PAST + 1 if k < 2 else NP
                    chain(vec.tensor_reduce(stats[:, 14:15], rows[:, 0:width], AX.X, ALU.max))
                    vec.tensor_scalar(stats[:, 15:16], stats[:, 14:15], -SCALE, None, ALU.mult).then_inc(smn_ready, 1)
                elif what == "SC":
                    width = PAST + 1 if k < 2 else NP
                    vec.wait_ge(sme_ready, k + 1)
                    chain(vec.reciprocal(stats[:, 17:18], stats[:, 16:17]))
                    scaled = vec.tensor_scalar(rows[:, 0:width], rows[:, 0:width], stats[:, 17:18], None, ALU.mult)
                    if k < 2:
                        chain(scaled)
                        if k:
                            vec.wait_ge(p_psum, 1)
                        vec.tensor_scalar(p_own[:], ident[0:32, 0:32], rows[:, PAST:PAST + 1], None, ALU.mult)\
                            .then_inc(p_ready, 1)
                    else:
                        scaled.then_inc(p_ready, 1)
                elif what == "PV":
                    vec.wait_ge(yr_psum, PV_ORDER.index(k) + 1)
                    for two in range(2):
                        r = slice(HD * two, HD * two + HD)
                        if k < 2:
                            for b4 in range(4):
                                first = b4 * (P + MH) + two
                                some = vec.tensor_copy(tmp[r, 2:6, 4 * k + b4],
                                                       bank[5][r, first:first + 3 * 34 + 1:34])
                        else:
                            for hp in range(2):
                                first = 34 * hp + two
                                some = vec.tensor_copy(tmp[r, 6 + hp, 0:NS], bank[5][r, first:first + 7 * 68 + 1:68])
                        some.then_inc(ys_ready, 1)
            for m in range(KT):
                vec.wait_ge(cat_hi, m + 1)
                vec.tensor_tensor(x_lo[:, m, :], tmp[:, m, :], x_hi[:, m, :].bitcast(F32), ALU.subtract).then_inc(cat_lo, 1)
            for r in range(2, KT + 2):
                split(U_MIX + r)
            residual(1, U_FFN2 - 1, 1.0)
            norm(3, xT, 24, x_hi, x_lo, N, M_ORDER)
            vec.wait_ge(mid_stored, 16 * MID_STORES)
            ffn(1)
            residual(2, U_END - 1, 0.5)
            for g in range(0, 6, 2):
                y_rows(vec, g)

        @block.tensor
        def _(pe):
            def three(out, lhs, rhs, start, stop):
                pe.matmul(out, lhs[0], rhs[0], start=start, stop=False)
                pe.matmul(out, lhs[0], rhs[1], start=False, stop=False)
                return pe.matmul(out, lhs[1], rhs[0], start=False, stop=stop)

            def weights(slot, c0, c1):
                return w_hi[:, slot, c0:c1], w_lo[:, slot, c0:c1]

            def sum_squares(inst, cols, order, bk):
                for idx, m in enumerate(order):
                    pe.wait_ge(sq_ready, KT * inst + idx + 1)
                    mm = pe.matmul(bank[bk][:, 0:cols], ones[:], tmp[:, m, 0:cols], start=(idx == 0), stop=(idx == KT - 1))
                mm.then_inc(ss_ready, 1)

            def turn(out, in_, k=P):
                return pe.transpose(out, in_, ident[0:k, 0:k])

            def ffn(f):
                n0, inst = (U_FFN1, U_FFN2)[f], (1, 3)[f]
                pe.wait_ge(xlo_ready, KT * (inst + 1))
                with pe.Fori(0, HT // 2) as i:
                    for s in range(2):
                        pe.wait_ge(gu_free, i * 2 + (s + HT * f + 1))
                        for half in range(2):
                            j = 2 * s + half
                            pe.wait_ge(lo_ready, i * 4 + (n0 + j + 1))
                            for k in range(KT):
                                mm = three(bank[j][:, 0:N], weights((n0 + j) % RING, k * P, (k + 1) * P),
                                           (x_hi[:, k, :], x_lo[:, k, :]), k == 0, k == KT - 1)
                            mm.then_inc(w_used, 1)
                n0 += 2 * HT
                hidden = lambda k: tuple(h[:, ds(k, 1), :].rearrange("p a n -> p (a n)") for h in (h_hi, h_lo))
                for k in range(2):
                    outer(n0 + k, n0 + k, hidden(k), k == 0, False, f if k == 0 else None,
                          lambda k=k: pe.wait_ge(h_ready, HT * f + k + 1))
                with pe.Fori(0, 4) as i:
                    for j in range(4):
                        outer(n0 + 2 + j, i * 4 + (n0 + 2 + j), hidden(i * 4 + (2 + j)), False, False, None,
                              lambda j=j: pe.wait_ge(h_ready, i * 4 + (HT * f + 3 + j)))
                for k in range(HT - 4, HT):
                    outer(n0 + k, n0 + k, hidden(k), False, k == HT - 1, None, lambda k=k: pe.wait_ge(h_ready, HT * f + k + 1))

            def outer(n, unit, x, start, stop, first_of, ready):
                pe.wait_ge(lo_ready, unit + 1)
                ready()
                for idx, m in enumerate(M_ORDER):
                    if first_of is not None and m == 0:
                        pe.wait_ge(gu_free, 2 + HT * (first_of + 1))
                    mm = three(bank[m][:, 0:N], weights(n % RING, m * P, (m + 1) * P), x, start, stop)
                    if stop and idx < KT - 1:
                        mm.then_inc(out_done, 1)
                mm.then_inc(w_used, 1)

            def project(nb_, j):
                r = 4 * nb_ + j
                if j == 0 and nb_ >= 2:
                    pe.wait_ge(proj_evac, 3 * (nb_ - 1))
                pe.wait_ge(lo_ready, U_WIN + r + 1)
                for tt, c0 in enumerate((0, NS, NS + P)):
                    for kk in range(2):
                        k = 2 * j + kk
                        mm = three(bank[3 * (nb_ % 2) + tt][:, :], (x_hi[:, k, c0:c0 + P], x_lo[:, k, c0:c0 + P]),
                                   weights((U_WIN + r) % RING, kk * 512, kk * 512 + 512), k == 0, k == KT - 1)
                    if j == 3 and tt < 2:
                        mm.then_inc(proj_done, 1)
                mm.then_inc(w_used, 1)

            def queries(b):
                pe.wait_ge(nrm_ready, 1 if b < NS else 5)
                if b:
                    pe.wait_ge(qb_ready, b)
                if b < NS:
                    pe.matmul(bank[6][:, :], delta[:, b, 0:1].to_broadcast([NS, P]), qs[:], start=True, stop=True)\
                        .then_inc(qb_psum, 1)
                else:
                    for two in range(2):
                        mm = pe.matmul(bank[6][:, two * 256:two * 256 + 256],
                                       delta[:, 2 * (b - NS) + two, 0:1].to_broadcast([NS, P]), us[:, 256:512],
                                       start=True, stop=True)
                    mm.then_inc(qb_psum, 1)

            pe.wait_ge(id_loaded, 16)
            pe.wait_ge(g_loaded, 16 * 5)
            turn(bank[4][:, 0:34], g_rows[:], 34).then_inc(g_turned, 1)
            pe.wait_ge(m_loaded, 16)
            for g in range(4):
                for k in range(2):
                    for t in range(2):
                        mm = turn(bank[g][:, k * NP + t * P:k * NP + (t + 1) * P], m_rows[:, t, (2 * g + k) * P:(2 * g + k + 1) * P])
                mm.then_inc(m_turned, 1)
            pe.wait_ge(x_loaded, 32)
            for m in range(KT):
                bk = X_BANKS[m]
                if bk < 4:
                    pe.wait_ge(memT_ready, bk + 1)
                if bk == 4:
                    pe.wait_ge(gains_ready, 1)
                turn(bank[bk][:, 0:NS], x_rows[0:NS, 0, m * P:(m + 1) * P], NS)
                for t in range(2):
                    mm = turn(bank[bk][:, NS + t * P:NS + (t + 1) * P], x_rows[:, 1 + t, m * P:(m + 1) * P])
                mm.then_inc(x_turned, 1)
            pe.wait_ge(const_set, 4)
            pe.wait_ge(res_ready, KT)
            sum_squares(0, NP, range(KT), 6)
            pe.wait_ge(xlo_ready, KT)
            for j in range(4):
                pe.wait_ge(lo_ready, j + 1)
                for t in range(2):
                    for kk in range(2):
                        k = 2 * j + kk
                        mm = three(bank[4 + t][:, :], (m_hi[:, k, t * P:(t + 1) * P], m_lo[:, k, t * P:(t + 1) * P]),
                                   weights(j, kk * 512, kk * 512 + 512), k == 0, k == KT - 1)
                    if j == 3 and t == 0:
                        mm.then_inc(kvm_done, 1)
                mm.then_inc(w_used, 1)
                if j == 1:
                    sum_squares(1, N, range(KT), 7)
            ffn(0)
            sum_squares(2, N, M_ORDER, 4)
            pe.wait_ge(xlo_ready, 3 * KT)
            pe.wait_ge(c_loaded, 16 * 12)
            for nb_ in range(4):
                for j in range(4):
                    project(nb_, j)
                    if nb_ in (1, 2) and j in (1, 3):
                        queries(2 * (nb_ - 1) + j // 2)
            queries(4)
            pairs_done = 0
            for what, k in steps(pe):
                if what == "X":
                    pe.wait_ge(nrm_ready, 7)
                    pe.wait_ge(proj_evac, 12)
                    for g in range(6):
                        src, c0 = ((qp, 0), (qp, 256), (kp, 0), (kp, 256), (up, 256), (mem_kv, 0))[g]
                        if g >= 4:
                            pe.wait_ge(qkT_ready, g - 3)
                        for hh in range(2):
                            for t in range(2):
                                mm = turn(bank[g % 4][:, hh * NP + t * P:hh * NP + (t + 1) * P],
                                          src[:, t, c0 + hh * P:c0 + (hh + 1) * P])
                        mm.then_inc(qk_turned, 1)
                elif what == "POOL":
                    pe.wait_ge(ext_ready, 1)
                    for g in range(4):
                        out, r = bank[4 + g // 2], slice(HD * (g % 2), HD * (g % 2) + HD)
                        u0, u1 = (up[:, t, g * HD:(g + 1) * HD] for t in range(2))
                        pe.matmul(out[r, NS:NS + P], u0, band[:, g, 0:P], start=True, stop=True)
                        pe.matmul(out[r, NS + P:N], u1, band[:, g, P + EDGE:], start=True, stop=False)
                        pe.matmul(out[r, NS + P:NS + P + EDGE], u0, band[:, g, P:P + EDGE], start=False, stop=True)
                        mm = pe.matmul(out[r, 0:NS], ext[:, g * HD:(g + 1) * HD], samp[:, g, :], start=True, stop=True)
                        if g % 2:
                            mm.then_inc(pooled_psum, 1)
                    pe.wait_ge(poolw_loaded, 16 * 4)
                    for pr in range(2):
                        pe.wait_ge(pooled_ready, pr + 1)
                        pe.matmul(bank[4 + pr][:, 0:N], pool_wd[:, pr, :], sg[:, pr, :], start=True, stop=True).then_inc(pool_psum, 1)
                elif what == "HA":
                    if k == 0:
                        pe.wait_ge(qkT_ready, 6)
                        pe.wait_ge(mask_ready, 2)
                    else:
                        pe.wait_ge(exp_done, 4 * k)
                    q_, k_, hp = (qT, kT, k) if k < MH // 2 else (qmT, mkT, k - MH // 2)
                    masked = k < MH // 2
                    for t in range(2):
                        n = keys_of(k, t)
                        for h in range(2):
                            r = slice(HD * h, HD * h + HD)
                            mm = pe.matmul(bank[h][:, t * NP:t * NP + n], q_[r, hp, t * P:(t + 1) * P], k_[r, hp, 0:n],
                                           start=True, stop=not masked)
                        if masked:
                            c0 = t * (NP + P)
                            for h in range(2):
                                mm = pe.matmul(bank[h][:, c0:c0 + P], ident_b[:], causal_b[:], start=False, stop=True)
                    mm.then_inc(sc_ready, 1)
                elif what == "HB":
                    pairs_done = k + 1
                    pe.wait_ge(prob_ready, k + 1)
                    if k:
                        pe.wait_ge(probT_ready, k)
                    blocks = ((0, 0, 0), (1, 0, 1), (1, 1, 2)) if k < MH // 2 else ((0, 0, 0), (1, 0, 1), (0, 1, 2), (1, 1, 3))
                    for h in range(2):
                        for t, kt, at_ in blocks:
                            mm = turn(bank[2 + h][:, at_ * P:(at_ + 1) * P], prob[:, h, t, kt * P:(kt + 1) * P])
                    mm.then_inc(pT_psum, 1)
                    pe.wait_ge(probT_ready, k + 1)
                    if k:
                        pe.wait_ge(head_ready, k)
                    if k == 1:
                        pe.wait_ge(rows_ready, 3)
                    for kt in range(2):
                        for h in range(2):
                            head = 2 * k + h
                            v_ = vp[:, kt, head * HD:(head + 1) * HD] if k < MH // 2 else \
                                mem_kv[:, kt, 256 + (head - MH) * HD:256 + (head - MH + 1) * HD]
                            q0 = P if kt and k < MH // 2 else 0
                            mm = pe.matmul(bank[7][HD * h:HD * h + HD, q0:NP], v_, probT[:, h, 2 * P:2 * P + NP - q0] if kt
                                           else probT[:, h, 0:NP], start=(kt == 0), stop=(kt == 1))
                    mm.then_inc(pv_done, 1)
                elif what == "L":
                    if k + 1 < NS + 4:
                        queries(k + 1)
                elif what == "SA":
                    if k == 0:
                        pe.wait_ge(pool_ready, 2)
                    else:
                        pe.wait_ge(pcols_ready, 2 * k)
                    if k < 2:
                        pe.wait_ge(own_ready, k + 1)
                        if k:
                            pe.wait_ge(head_ready, pairs_done)
                        pe.matmul(bank[7][0:32, 256:257], own_e[:].rearrange("p b h -> p (b h)"), ones[0:NS, 0:1], start=True, stop=True)
                        pe.wait_ge(k_used, 4 * k + 4)
                        for t in range(PAGES):
                            mm = turn(bank[4 + t // 4][0:32, (t % 4) * P:(t % 4 + 1) * P],
                                      logits[:, t, :, :].rearrange("p b h -> p (b h)"))
                    else:
                        pe.wait_ge(k_used, NS + 4)
                        for t in range(2):
                            mm = turn(bank[4][0:32, t * P:(t + 1) * P], logits_m[:, t].rearrange("p b h -> p (b h)"))
                    mm.then_inc(lt_psum, 1)
                elif what == "SD":
                    pe.wait_ge(p_ready, k + 1)
                    for t in range(PAGES if k < 2 else 2):
                        mm = turn(bank[4][:, t * 32:(t + 1) * 32], rows[:, t * P:(t + 1) * P], 32)
                    if k < 2:
                        if pairs_done:
                            pe.wait_ge(head_ready, pairs_done)
                        mm = pe.matmul(bank[7][0:NS, 320:352], back[:, k, :], p_own[:], start=True, stop=True)
                    mm.then_inc(p_psum, 1)
                elif what == "PV":
                    pe.wait_ge(pcols_ready, (2, 4, 5)[k])
                    if k == 0:
                        pe.wait_ge(rows_ready, 6)
                    else:
                        pe.wait_ge(ys_ready, 2 * PV_ORDER.index(k))
                    if k < 2:
                        for b4 in range(4):
                            slot = kv_wait(pe, "v", 4 * k + b4)
                            for t in range(PAGES + 1):
                                for hp in range(4):
                                    out = bank[5][32 * hp:32 * hp + 32, b4 * P:(b4 + 1) * P]
                                    if t < PAGES:
                                        c0 = t * 512 + hp * P
                                        pe.matmul(out, p_cols[:, k, t, :], kv[:, slot, c0:c0 + P], start=(t == 0), stop=False)
                                    else:
                                        mm = pe.matmul(out, p_own8[:, k, :], vs[:, hp * P:(hp + 1) * P], start=False, stop=True)
                            mm.then_inc(v_used, 1)
                    else:
                        slot = kv_wait(pe, "mv", 0)
                        for b2 in range(4):
                            for t in range(2):
                                for two in range(2):
                                    for hp in range(2):
                                        part = 32 * (2 * two + hp)
                                        c0 = (2 * b2 + two) * 512 + t * 256 + hp * P
                                        mm = pe.matmul(bank[5][part:part + 32, b2 * P:(b2 + 1) * P], pm_cols[:, t, :],
                                                       kv[:, slot, c0:c0 + P], start=(t == 0), stop=(t == 1))
                        mm.then_inc(v_used, 1)
                    pe.wait_ge(yr_ready, PV_ORDER.index(k) + 1)
                    for b4 in range(4):
                        mm = turn(bank[5][:, b4 * P:(b4 + 1) * P], y_rows_s[:, b4 * P:(b4 + 1) * P])
                    mm.then_inc(yr_psum, 1)
            for k in range(KT):
                outer(U_MIX + k, U_MIX + k, (x_hi[:, k, :], x_lo[:, k, :]), k == 0, k == KT - 1, None,
                      lambda k=k: pe.wait_ge(cat_lo, k + 1))
            sum_squares(3, N, M_ORDER, 4)
            ffn(1)
            pe.wait_ge(res_ready, 4 * KT)
            for g in range(6):
                for q in range(4):
                    if g < 2:
                        mm = turn(bank[g][0:NS, q * P:(q + 1) * P], xT[:, 4 * g + q, 0:NS])
                    else:
                        t, m = (g - 2) // 2, 4 * ((g - 2) % 2) + q
                        mm = turn(bank[g][:, q * P:(q + 1) * P], xT[:, m, NS + t * P:NS + (t + 1) * P])
                mm.then_inc(y_turned, 1)


_INS = ["x_prompt", "x_sample", "mem_prompt", "cache_k", "cache_v", "cache_mem_k", "cache_mem_v", "state_pool", "page_table",
        "ffn1_norm", "ffn1_w_in", "ffn1_w_out", "mix_norm", "w_in", "pool_w", "pool_scale", "q_norm", "k_norm",
        "mem_norm", "mem_w_kv", "mem_q_norm", "mem_k_norm", "w_out", "ffn2_norm", "ffn2_w_in", "ffn2_w_out"]
_OUTS = [("y_prompt", (1, NP, D)), ("y_sample", (NS, 1, D)), ("k_out", (1, 1, NP, MH, HD)), ("v_out", (1, 1, NP, MH, HD)),
         ("mk_out", (1, 1, NP, CH, HD)), ("mv_out", (1, 1, NP, CH, HD)), ("buf_out", (1, 1, BUF, POOL)),
         ("ks_out", (1, NS, 1, MH, HD)), ("vs_out", (1, NS, 1, MH, HD)), ("state_out", (1, NS, BUF, POOL))]


def kernel(**inputs):
    import concourse.bacc as bacc
    from concourse.bass_utils import run_bass_kernel_spmd

    nc = bacc.Bacc("TRN2", target_bir_lowering=False, num_devices=1, dynamic_dma_scratch_size=1024)
    arrays, views = {}, {}
    given = {name: np.ascontiguousarray(inputs[name]) for name in _INS}
    for name, arr in list(given.items()) + list(shape_constants().items()):
        arrays[f"in_{name}"] = arr
        views[name] = nc.dram_tensor(f"in_{name}", arr.shape, mybir.dt.from_np(arr.dtype), kind="ExternalInput").ap()
    for name, shape in _OUTS:
        views[name] = nc.dram_tensor(f"out_{name}", shape, F32, kind="ExternalOutput").ap()
    layer(nc, views)
    r = run_bass_kernel_spmd(nc, [arrays], core_ids=[0])
    return tuple(r.results[0][f"out_{name}"] for name, _ in _OUTS)
```

```python
from contextlib import ExitStack

import concourse.bass as bass
from concourse import mybir
import numpy as np

F32 = mybir.dt.float32
F32R = mybir.dt.float32r
BF16 = mybir.dt.bfloat16
I32 = mybir.dt.int32
ALU = mybir.AluOpType
ACT = mybir.ActivationFunctionType
AX = mybir.AxisListType
ds = bass.ds

P = 128
D = 1024
KT = D // P
DFF = 2816
HT = DFF // P
NS = 8
NP = 256
N = NS + NP
POOL, MOBA, MEM = 256, 512, 256
HD = 64
MH, CH = MOBA // HD, MEM // HD
PAST, PAGE, BLOCK = 1024, 128, 256
PAGES = PAST // PAGE
BLOCKS = PAST // BLOCK
EPS = 1e-6
SCALE = HD ** -0.5
NEG = -1e30
WINDOWS = (2, 4, 8, 16)
BUF = 15
EDGE = 16
ROT, HALF_ROT, THETA = 16, 8, 500000.0

RING = 4
U_MEM = 0
U_FFN1 = U_MEM + 4
U_WIN = U_FFN1 + 3 * HT
U_MIX = U_WIN + 16
U_FFN2 = U_MIX + KT
U_END = U_FFN2 + 3 * HT
LEAD = 2
X_BANKS = (5, 6, 7, 0, 1, 2, 3, 4)
M_ORDER = (4, 5, 6, 7, 0, 1, 2, 3)
J_ORDER = (2, 3, 0, 1)
KV_SLOTS = 4
QB = 3
HELD = 6
KV_STREAM = ([("k", b) for b in range(NS)] + [("mk", 0)] + [("v", b) for b in range(4)] + [("mv", 0)] +
             [("v", b) for b in range(4, NS)])
KV_AT = {kb: n for n, kb in enumerate(KV_STREAM)}
GP_PAGES = (6,) * 4 + (7,) * 4


def shape_constants():
    c = {}
    c["ident"] = np.eye(P, dtype=np.float32)
    c["causal"] = np.where(np.arange(P)[None, :] <= np.arange(P)[:, None], 0.0, NEG).astype(np.float32)
    inv = np.power(np.float32(THETA), -np.arange(HALF_ROT, dtype=np.float32) * np.float32(2.0 / ROT)).astype(np.float32)
    pos = np.concatenate([np.arange(NP), np.full(P, PAST)]).astype(np.float32).reshape(3, P)
    ang = (pos.T[:, :, None] * inv[None, None, :]).astype(np.float32)
    c["rope"] = np.stack([np.cos(ang), np.sin(ang)], axis=1).astype(np.float32)
    band = np.zeros((P, 2, 4, NP), np.float32)
    samp = np.zeros((P, 4, NS), np.float32)
    for g, w in enumerate(WINDOWS):
        for t in range(NP):
            for s in range(max(0, t - w + 1), t + 1):
                band[s % P, s // P, g, t] += 1.0 / min(w, t + 1)
            band[t % P, t // P, g, t] -= 1.0
        for b in range(NS):
            samp[b, g, b] = 1.0 / w - 1.0
            for j in range(BUF - (w - 1), BUF):
                samp[NS + BUF * b + j, g, b] = 1.0 / w
    c["band"] = np.concatenate([band[:, 0, :, 0:P + EDGE], band[:, 1, :, P:NP]], axis=2)
    c["samp"] = samp
    delta = np.zeros((NS, NS, MH), np.float32)
    for b in range(NS):
        delta[b, b, :] = 1.0
    c["delta"] = delta
    back = np.zeros((32, 2, NS), np.float32)
    for r in range(32):
        for hf in range(2):
            back[r, hf, 4 * hf + r // MH] = 1.0
    c["back"] = back
    c["rank"] = np.tile(np.arange(1, BLOCKS + 1, dtype=np.float32), (32, 1))
    return c


def layer(nc, a):
    ctx = ExitStack()
    with ctx:
        cursor = [1152]

        def place(name, shape, dt=F32, at=None):
            size = 4 * int(np.prod(shape[1:]))
            if at is None:
                at = cursor[0]
                cursor[0] += -(-size // 64) * 64
            return nc.alloc_sbuf_tensor_at(name, list(shape), dt, offset=at)

        def sem(name):
            return ctx.enter_context(nc.semaphore(name))

        raw = place("raw", [P, RING, 1024])
        w_hi = place("w_hi", [P, RING, 1024], F32R)
        w_lo = place("w_lo", [P, RING, 1024], F32R)
        xT = place("xT", [P, KT, N])
        x_hi = place("x_hi", [P, KT, N], F32R)
        x_lo_at = cursor[0]
        x_lo = place("x_lo", [P, KT, N], F32R)
        rows = place("rows", [32, PAST + 8], at=x_lo_at)
        probT = place("probT", [P, 2, 2 * NP], at=x_lo_at + 4160)
        band = place("band", [P, 4, 2 * P + EDGE])
        tmp = place("tmp", [P, KT, N])
        mem_kv = place("mem_kv", [P, 2, 512])
        m_tmp = place("m_tmp", [P, KT, NP], at=cursor[0] + 4 * 3 * PAGES * 512)
        kv = place("kv", [P, KV_SLOTS, PAGES * 512])
        y_rows_s = place("y_rows_s", [P, 512], at=cursor[0])
        root = place("root", [P, N])
        rstd = place("rstd", [P, N])
        rot = place("rot", [P, 4, 2, MH * HALF_ROT], at=cursor[0])
        sg = place("sg", [P, 2, N])
        p_cols = place("p_cols", [P, 2, PAGES, 32], at=cursor[0])
        h_tmp = place("h_tmp", [P, 2, N])
        ident = place("ident", [P, P])
        causal = place("causal", [P, P])
        ident_b = place("ident_b", [P, P], BF16)
        causal_b = place("causal_b", [P, P], BF16)
        ones = place("ones", [P, P])
        gains = place("gains", [P, 34])
        rope = place("rope", [P, 2, 3, HALF_ROT])
        head_gain = place("head_gain", [P, 4, HD])
        eps_col = place("eps_col", [P, 1])
        dummy = place("dummy", [P, 4])
        page_ids = place("page_ids", [1, NS * PAGES], I32)
        samp = place("samp", [P, 4, NS])
        delta = place("delta", [NS, NS, MH])
        back = place("back", [32, 2, NS])
        rank = place("rank", [32, BLOCKS])
        own8 = place("own8", [NS, MH])
        own_e = place("own_e", [NS, 4, MH])
        logits = place("logits", [P, PAGES, NS, MH])
        logits_m = place("logits_m", [P, 2, NS, CH])
        pm_cols = place("pm_cols", [P, 2, 32])
        p_own = place("p_own", [32, 32])
        p_own8 = place("p_own8", [NS, 2, 32])
        stats = place("stats", [32, 24])
        qb = place("qb", [P, QB, 512])
        ss_h = place("ss_h", [P, 16])
        var_h = place("var_h", [P, 16])
        sd_h = place("sd_h", [P, 16])
        rs_h = place("rs_h", [P, 16])
        mx = place("mx", [P, 2, 2, 2])
        nb = place("nb", [P, 2, 2, 2])
        sm = place("sm", [P, 2, 2, 2])
        rc = place("rc", [P, 2, 2, 2])
        ext = place("ext", [P, POOL])
        pool_wd = place("pool_wd", [P, 2, P])
        region = cursor[0]
        h_hi = place("h_hi", [P, HT, N], F32R)
        h_lo = place("h_lo", [P, HT, N], F32R)
        end = cursor[0]
        at = [region]

        def over(name, shape, dt=F32):
            t = place(name, shape, dt, at=at[0])
            at[0] += -(-4 * int(np.prod(shape[1:])) // 64) * 64
            assert at[0] <= end, name
            return t

        x_rows = over("x_rows", [P, 3, D])
        m_rows = over("m_rows", [P, 2, D])
        memT = over("memT", [P, KT, NP])
        m_hi = over("m_hi", [P, KT, NP], F32R)
        m_lo = over("m_lo", [P, KT, NP], F32R)
        g_rows = over("g_rows", [34, P])
        at[0] = region
        qp = over("qp", [P, 2, 512])
        kp = over("kp", [P, 2, 512])
        vp = over("vp", [P, 2, 512])
        up = over("up", [P, 2, 512])
        qs = over("qs", [NS, 512])
        ks = over("ks", [NS, 512])
        vs = over("vs", [NS, 512])
        us = over("us", [NS, 512])
        qT = over("qT", [P, 4, NP])
        kT = over("kT", [P, 4, NP])
        qmT = over("qmT", [P, 2, NP])
        mkT = over("mkT", [P, 2, NP])
        prob_pair = [over("prob", [P, 2, 2, NP]), place("prob_odd", [P, 2, 2, NP], at=region)]
        sq_h = over("sq_h", [P, 2, 512])

        banks = ctx.enter_context(nc.psum_tensor("banks", [P, 8, 512], F32))
        bank = [banks[:, i, :] for i in range(8)]

        x_loaded, m_loaded, g_loaded = sem("x_loaded"), sem("m_loaded"), sem("g_loaded")
        id_loaded, c_loaded = sem("id_loaded"), sem("c_loaded")
        pg_loaded, poolw_loaded = sem("pg_loaded"), sem("poolw_loaded")
        raw_loaded = [sem(f"raw_loaded{i}") for i in range(RING)]
        kv_loaded = [sem(f"kv_loaded{i}") for i in range(KV_SLOTS)]
        hi_ready, lo_ready, w_used = sem("hi_ready"), sem("lo_ready"), sem("w_used")
        const_set = sem("const_set")
        g_turned, gains_ready = sem("g_turned"), sem("gains_ready")
        m_turned, memT_ready = sem("m_turned"), sem("memT_ready")
        x_turned, res_ready = sem("x_turned"), sem("res_ready")
        sq_ready, ss_ready, root_ready, rstd_ready = sem("sq_ready"), sem("ss_ready"), sem("root_ready"), sem("rstd_ready")
        xn_ready, xhi_ready, xlo_ready = sem("xn_ready"), sem("xhi_ready"), sem("xlo_ready")
        kvm_done, gu_free = sem("kvm_done"), sem("gu_free")
        silu_ready, hhi_ready, h_ready = sem("silu_ready"), sem("hhi_ready"), sem("h_ready")
        out_done = sem("out_done")
        proj_done, proj_evac = sem("proj_done"), sem("proj_evac")
        vec_step = sem("vec_step")
        var_ready, sqh_ready, sd_ready, nrm_ready = sem("var_ready"), sem("sqh_ready"), sem("sd_ready"), sem("nrm_ready")
        qb_psum, qb_ready, gp_done, k_used, v_used = sem("qb_psum"), sem("qb_ready"), sem("gp_done"), sem("k_used"), sem("v_used")
        qk_turned, qkT_ready = sem("qk_turned"), sem("qkT_ready")
        pooled_psum, pooled_ready, pool_psum, pool_ready = sem("pooled_psum"), sem("pooled_ready"), sem("pool_psum"), sem("pool_ready")
        ext_ready = sem("ext_ready")
        sc_ready, nb_ready, exp_done, prob_ready = sem("sc_ready"), sem("nb_ready"), sem("exp_done"), sem("prob_ready")
        pT_psum, probT_ready, pv_done, head_ready = sem("pT_psum"), sem("probT_ready"), sem("pv_done"), sem("head_ready")
        own_ready, lt_psum, rows_ready = sem("own_ready"), sem("lt_psum"), sem("rows_ready")
        yr_psum, yr_ready, mask_ready = sem("yr_psum"), sem("yr_ready"), sem("mask_ready")
        smn_ready, sme_ready, p_ready, p_psum, pcols_ready = (sem("smn_ready"), sem("sme_ready"), sem("p_ready"),
                                                              sem("p_psum"), sem("pcols_ready"))
        ys_ready = sem("ys_ready")
        cat_hi, cat_lo = sem("cat_hi"), sem("cat_lo")
        y_turned, y_ready = sem("y_turned"), [sem(f"y_ready{g}") for g in range(6)]
        mid_stored, stored = sem("mid_stored"), sem("stored")
        MID_STORES = 8

        def cols_view(w, k):
            return w[0].rearrange("(k p) c -> p k c", p=P)

        ffn_in = [cols_view(a["ffn1_w_in"], KT), cols_view(a["ffn2_w_in"], KT)]
        ffn_out = [cols_view(a["ffn1_w_out"], HT), cols_view(a["ffn2_w_out"], HT)]
        w_in, w_mix, w_mem = cols_view(a["w_in"], KT), cols_view(a["w_out"], KT), cols_view(a["mem_w_kv"], KT)

        def kv_level(n):
            total = 0
            for i in range(n % KV_SLOTS, n + 1, KV_SLOTS):
                total += 16 * (PAGES if KV_STREAM[i][0] in "kv" else 1)
            return total

        def kv_wait(eng, kind, b):
            n = KV_AT[(kind, b)]
            eng.wait_ge(kv_loaded[n % KV_SLOTS], kv_level(n))
            return n % KV_SLOTS

        V_ORDER = [0, 1, 2, 3, "mem", 4, 5, 6, 7]

        def raw_level(n, i):
            return 16 * (n // RING + 1) + 16 * i + (16 if n >= U_WIN + 12 else 0)

        Y_GROUPS = ((0, 1), (1, 1), (2, 1), (0, 0), (1, 0), (2, 0))

        def y_rows(eng, g):
            eng.wait_ge(y_turned, g + 1)
            rows_, half = Y_GROUPS[g]
            n = NS if rows_ == 0 else P
            dst, src = kv[0:n, g // 3, rows_ * 512:(rows_ + 1) * 512], bank[Y_BANKS[g]][0:n, :]
            if eng is act_engine[0]:
                eng.activation(dst, src, ACT.Copy).then_inc(y_ready[g], 1)
            else:
                eng.tensor_copy(dst, src).then_inc(y_ready[g], 1)

        Y_BANKS = (4, 5, 6, 7, 0, 1)
        act_engine = [None]
        QUERY_AT = (4, 6, 7, 9, 11, 13)
        TURN_BANKS = (0, 1, 2, 0, 2, 3)
        V_DONE = (4, 5, 9)
        ROWS_DONE = (3, 4, 7)
        PCOLS_DONE = (2, 3, 5)

        def keys_of(pair, t):
            return P if pair < MH // 2 and t == 0 else NP

        def steps(eng):
            order = [("L", 6), ("R", 0), ("POOL", 0), ("XM", 0), ("POOL", 1), ("SA", 0), ("L", 7), ("SB", 0), ("L", 8),
                     ("SC", 0), ("L", 9), ("L", 10), ("L", 11), ("SD", 0), ("R", 1, 0), ("SA", 1), ("SB", 1), ("V", 1),
                     ("SC", 1), ("R", 2, 2), ("SD", 1), ("SA", 2), ("SB", 2), ("R", 3, 3), ("Y", 0), ("V", "mem"),
                     ("SC", 2), ("Y", 1), ("SD", 2), ("R", 4, 4), ("R", 5, 5), ("R", 6, 6), ("V", 7), ("Y", 2)]
            for what, k, *between in order:
                if what != "R":
                    yield what, k
                    continue
                for part in {"tensor": ("HA", "HB", "V", "HX"), "vector": ("HB", "HA"), "scalar": ("HB", "HA", "HX")}[eng]:
                    if part == "V":
                        if between:
                            yield "V", between[0]
                        continue
                    p = k if part == "HA" else k - 1
                    if 0 <= p < 6:
                        yield part, p

        block = ctx.enter_context(nc.Block())

        @block.sync
        def _(sp):
            def load_unit(n0, j, i, src):
                n = n0 + j
                if not (isinstance(i, int) and n + 4 * i < RING):
                    sp.wait_ge(lo_ready, 4 * i + n - RING + 1)
                sp.dma_start(raw[:, n % RING, :].rearrange("p (k c) -> p k c", k=src.shape[1]), src)\
                    .then_inc(raw_loaded[n % RING], 16)

            def ffn_in_units(f, lo, hi):
                n0 = (U_FFN1, U_FFN2)[f]
                with sp.Fori(lo, hi) as i:
                    for j in range(4):
                        col = (j // 2) * P + (j % 2) * DFF
                        load_unit(n0, j, i, ffn_in[f][:, :, ds(i * (2 * P) + col, P)])

            def ffn_out_units(f):
                n0 = (U_FFN1, U_FFN2)[f] + 2 * HT
                for j in range(2):
                    load_unit(n0, j, 0, ffn_out[f][:, j:j + 1, :])
                with sp.Fori(0, 5) as i:
                    for j in range(4):
                        load_unit(n0 + 2, j, i, ffn_out[f][:, ds(i * 4 + (2 + j), 1), :])

            pages = {}

            def page_of(b, t):
                return sp.value_load(page_ids[0:1, b * PAGES + t:b * PAGES + t + 1], min_val=0,
                                     max_val=a["cache_k"].shape[1] - 1)

            def load_kv(n):
                kind, b = KV_STREAM[n]
                if n >= KV_SLOTS:
                    was, wb = KV_STREAM[n - KV_SLOTS]
                    if was in ("k", "mk"):
                        sp.wait_ge(k_used, wb + 1 if was == "k" else 12)
                    else:
                        sp.wait_ge(v_used, V_ORDER.index(wb if was == "v" else "mem") + 1)
                slot = n % KV_SLOTS
                if kind in "kv":
                    cache = a["cache_k"] if kind == "k" else a["cache_v"]
                    if kind == "k" and b < HELD:
                        pages[b] = [page_of(b, t) for t in range(PAGES)]
                    for t in range(PAGES):
                        page = pages[b][t] if b < HELD else page_of(b, t)
                        sp.dma_start(kv[:, slot, t * 512:(t + 1) * 512],
                                     cache[0, ds(page, 1)].rearrange("o p h d -> p (o h d)"))\
                            .then_inc(kv_loaded[slot], 16)
                else:
                    cache = a["cache_mem_k"] if kind == "mk" else a["cache_mem_v"]
                    sp.dma_start(kv[:, slot, :].rearrange("p (b t c) -> p b t c", b=NS, t=2),
                                 cache[0].rearrange("b (t p) h d -> p b t (h d)", p=P)).then_inc(kv_loaded[slot], 16)

            sp.dma_start(ident[:], a["ident"]).then_inc(id_loaded, 16)
            sp.dma_start(m_rows[:], a["mem_prompt"][0].rearrange("(t p) d -> p t d", p=P)).then_inc(m_loaded, 16)
            for j, name in enumerate(("ffn1_norm", "mix_norm", "mem_norm", "ffn2_norm")):
                sp.dma_start(g_rows[8 * j:8 * j + 8, :], a[name][0].rearrange("(k p) -> k p", p=P)).then_inc(g_loaded, 16)
            sp.dma_start(g_rows[32:34, :], a["pool_scale"][0].rearrange("(k p) -> k p", p=P)).then_inc(g_loaded, 16)
            sp.dma_start(x_rows[0:NS, 0, :], a["x_sample"][:, 0, :]).then_inc(x_loaded, 16)
            sp.dma_start(x_rows[:, 1:3, :], a["x_prompt"][0].rearrange("(t p) d -> p t d", p=P)).then_inc(x_loaded, 16)
            for j in range(4):
                load_unit(U_MEM, j, 0, w_mem[:, 2 * j:2 * j + 2, :])
            sp.dma_start(page_ids[:], a["page_table"].rearrange("b g -> (b g)").unsqueeze(0)).then_inc(pg_loaded, 16)
            for j, name in enumerate(("q_norm", "k_norm", "mem_q_norm", "mem_k_norm")):
                sp.dma_start(head_gain[:, j, :], a[name][0].partition_broadcast(P)).then_inc(c_loaded, 16)
            for dst, name in ((rope, "rope"), (samp, "samp"), (delta, "delta"), (back, "back"), (rank, "rank"),
                              (causal, "causal"), (band, "band")):
                sp.dma_start(dst[:], a[name]).then_inc(c_loaded, 16)
            sp.dma_start(ext[NS:P, :], a["state_pool"][0].rearrange("b j c -> (b j) c")).then_inc(c_loaded, 16)
            sp.wait_ge(const_set, 1)
            for g in range(4):
                lo = HD * (g % 2)
                sp.dma_start(pool_wd[lo:lo + HD, g // 2, lo:lo + HD], a["pool_w"][0, g]).then_inc(poolw_loaded, 16)
            sp.dma_start(a["state_out"][0, :, 0:BUF - 1, :], a["state_pool"][0, :, 1:BUF, :]).then_inc(stored, 16)
            sp.wait_ge(pg_loaded, 16)
            for s, (lo, hi) in enumerate(((0, 5), (5, 8), (8, 11))):
                ffn_in_units(0, lo, hi)
                load_kv(s)
            ffn_out_units(0)
            sp.wait_ge(xlo_ready, KT)
            load_kv(3)
            def load_projection(r):
                j = J_ORDER[r % 4]
                if r < 12:
                    c0 = POOL + MOBA * (r // 4)
                    load_unit(U_WIN, r, 0, w_in[:, 2 * j:2 * j + 2, c0:c0 + 512])
                    return
                sp.wait_ge(lo_ready, U_WIN + r - RING + 1)
                dst = raw[:, (U_WIN + r) % RING, :].rearrange("p (k c) -> p k c", k=2)
                last = POOL + 3 * MOBA
                sp.dma_start(dst[:, :, 0:256], w_in[:, 2 * j:2 * j + 2, 0:256]).then_inc(raw_loaded[(U_WIN + r) % RING], 16)
                sp.dma_start(dst[:, :, 256:512], w_in[:, 2 * j:2 * j + 2, last:last + 256])\
                    .then_inc(raw_loaded[(U_WIN + r) % RING], 16)

            for r in range(13):
                load_projection(r)
            load_kv(4)
            load_projection(13)
            load_projection(14)
            load_kv(5)
            load_projection(15)
            load_unit(U_MIX, 0, 0, w_mix[:, 0:1, :])
            load_kv(6)
            load_unit(U_MIX, 1, 0, w_mix[:, 1:2, :])
            for j in range(2, 4):
                load_unit(U_MIX, j, 0, w_mix[:, j:j + 1, :])
            for n in range(7, len(KV_STREAM)):
                load_kv(n)
            sp.wait_ge(nrm_ready, 7)
            sp.wait_ge(proj_evac, 12)
            sp.dma_start(a["k_out"][0, 0].rearrange("(t p) h d -> p t (h d)", p=P), kp[:]).then_inc(mid_stored, 16)
            sp.dma_start(a["v_out"][0, 0].rearrange("(t p) h d -> p t (h d)", p=P), vp[:]).then_inc(mid_stored, 16)
            sp.dma_start(a["mk_out"][0, 0].rearrange("(t p) h d -> p t (h d)", p=P), mem_kv[:, :, 0:256])\
                .then_inc(mid_stored, 16)
            sp.dma_start(a["mv_out"][0, 0].rearrange("(t p) h d -> p t (h d)", p=P), mem_kv[:, :, 256:512])\
                .then_inc(mid_stored, 16)
            sp.dma_start(a["buf_out"][0, 0], up[P - BUF:P, 1, 0:POOL]).then_inc(mid_stored, 16)
            sp.dma_start(a["ks_out"][0, :, 0].rearrange("b h d -> b (h d)"), ks[:]).then_inc(mid_stored, 16)
            sp.dma_start(a["vs_out"][0, :, 0].rearrange("b h d -> b (h d)"), vs[:]).then_inc(mid_stored, 16)
            sp.dma_start(a["state_out"][0, :, BUF - 1, :], us[:, 0:POOL]).then_inc(mid_stored, 16)
            for j in range(4, KT):
                load_unit(U_MIX, j, 0, w_mix[:, j:j + 1, :])
            ffn_in_units(1, 0, 11)
            ffn_out_units(1)
            for g, (rows_, half) in enumerate(Y_GROUPS):
                sp.wait_ge(y_ready[g], 1)
                c0 = half * 512
                dst = a["y_sample"][:, 0, c0:c0 + 512] if rows_ == 0 else a["y_prompt"][0, (rows_ - 1) * P:rows_ * P, c0:c0 + 512]
                sp.dma_start(dst, kv[0:dst.shape[0], g // 3, rows_ * 512:(rows_ + 1) * 512]).then_inc(stored, 16)
            sp.wait_ge(mid_stored, 16 * MID_STORES)
            sp.wait_ge(stored, 16 * 7)

        @block.gpsimd
        def _(pool):
            pool.memset(pool_wd[:], 0.0).then_inc(const_set, 1)
            pool.memset(ones[:], 1.0).then_inc(const_set, 1)
            pool.memset(eps_col[:], EPS).then_inc(const_set, 1)
            pool.memset(dummy[:], 1.0).then_inc(const_set, 1)

            def norm_lo(inst, src, hi, lo, cols, order):
                for idx, m in enumerate(order):
                    pool.wait_ge(xhi_ready, KT * inst + idx + 1)
                    pool.tensor_tensor(lo[:, m, :], src[:, m, 0:cols], hi[:, m, :].bitcast(F32), ALU.subtract)\
                        .then_inc(xlo_ready, 1)

            norm_lo(0, m_tmp, m_hi, m_lo, NP, range(KT))
            norm_lo(1, tmp, x_hi, x_lo, N, range(KT))
            norm_lo(2, tmp, x_hi, x_lo, N, M_ORDER)
            for b in range(NS + 4):
                pool.wait_ge(qb_ready, b + 1)
                if b < NS:
                    slot = kv_wait(pool, "k", b)
                    k_rows = kv[:, slot, 0:GP_PAGES[b] * 512].rearrange("p (t c) -> p t c", c=512)
                    pool.tensor_tensor(k_rows, k_rows, qb[:, b % QB, :].unsqueeze(1).to_broadcast([P, GP_PAGES[b], 512]),
                                       ALU.mult).then_inc(gp_done, 1)
                    if b == 6:
                        for n in (U_MIX, U_MIX + 1):
                            pool.wait_ge(hi_ready, n + 1)
                            pool.wait_ge(lo_ready, n)
                            pool.tensor_tensor(w_lo[:, n % RING, :], raw[:, n % RING, :], w_hi[:, n % RING, :].bitcast(F32),
                                               ALU.subtract).then_inc(lo_ready, 1)
                else:
                    g = b - NS
                    slot = kv_wait(pool, "mk", 0)
                    m_keys = kv[:, slot, g * 1024:(g + 1) * 1024].rearrange("p (b t c) -> p b t c", b=2, t=2)
                    q_two = qb[:, b % QB, :].rearrange("p (b c) -> p b c", b=2).unsqueeze(2).to_broadcast([P, 2, 2, 256])
                    pool.tensor_tensor(m_keys, m_keys, q_two, ALU.mult).then_inc(gp_done, 1)
            norm_lo(3, tmp, x_hi, x_lo, N, M_ORDER)

        @block.scalar
        def _(act):
            def split(n0, j=0, i=0):
                n = n0 + j
                act.wait_ge(raw_loaded[n % RING], raw_level(n, i))
                if not (isinstance(i, int) and n + 4 * i < RING):
                    act.wait_ge(w_used, 4 * i + n - RING + 1)
                act.activation(w_hi[:, n % RING, :], raw[:, n % RING, :], ACT.Copy).then_inc(hi_ready, 1)

            def norm_squares(inst, src, cols, order, ready, base):
                if inst > 1:
                    act.wait_ge(xlo_ready, KT * inst)
                for idx, m in enumerate(order):
                    act.wait_ge(ready, base + idx + 1)
                    act.activation(tmp[:, m, 0:cols], src[:, m, :], ACT.Square).then_inc(sq_ready, 1)

            def norm_root(inst, cols, bk):
                act.wait_ge(ss_ready, inst + 1)
                act.activation(root[:, 0:cols], bank[bk][:, 0:cols], ACT.Sqrt, bias=eps_col[:, 0:1],
                               scale=1.0 / D).then_inc(root_ready, 1)

            def norm_hi(inst, dst, src, cols, order):
                for idx, m in enumerate(order):
                    act.wait_ge(xn_ready, KT * inst + idx + 1)
                    act.activation(dst[:, m, :], src[:, m, 0:cols], ACT.Copy).then_inc(xhi_ready, 1)

            def silu(f, c, s):
                act.wait_ge(w_used, (U_FFN1, U_FFN2)[f] + 2 * c + 2)
                act.activation(sg[:, s, :], bank[2 * s][:, 0:N], ACT.Silu).then_inc(silu_ready, 1)

            def table(func, k):
                act.activation(dummy[:, k:k + 1], dummy[:, 3:4], func)

            def ffn(f):
                n0 = (U_FFN1, U_FFN2)[f]
                table(ACT.Silu, 0)
                with act.Fori(0, HT // 2) as i:
                    for s in range(2):
                        split(n0 + 2 + 2 * s, 0, i)
                        split(n0 + 3 + 2 * s, 0, i)
                        silu(f, i * 2 + s, s)
                with act.Fori(0, 5) as i:
                    for j in range(4):
                        split(n0 + 2 * HT + LEAD, j, i)

            def turned(groups):
                for g in groups:
                    dst = (qT, qT, kT, kT, qmT, mkT)[g]
                    act.wait_ge(qk_turned, g + 1)
                    half = 2 * (g % 2) if g < 4 else 0
                    act.activation(dst[:, half:half + 2, :].rearrange("p k c -> p (k c)"), bank[TURN_BANKS[g]][:, :],
                                   ACT.Copy).then_inc(qkT_ready, 1)

            def head_sd(inst, nrows, width):
                act.wait_ge(var_ready, inst + 1)
                act.activation(sd_h[0:nrows, 0:width], var_h[0:nrows, 0:width], ACT.Sqrt).then_inc(sd_ready, 1)

            def head_squares(inst, buf):
                if inst:
                    act.wait_ge(var_ready, inst)
                act.activation((sq_h if inst else tmp)[0:buf.shape[0], 0:buf.shape[1], 0:buf.shape[2]], buf, ACT.Square).then_inc(sqh_ready, 1)

            def evac(nb_, tts=range(3)):
                for tt in tts:
                    if tt < 2:
                        act.wait_ge(proj_done, 2 * nb_ + tt + 1)
                    else:
                        act.wait_ge(w_used, U_WIN + 4 * nb_ + 4)
                    src = bank[3 * (nb_ % 2) + tt]
                    if tt == 0:
                        act.activation((qs, ks, vs, us)[nb_][:], src[0:NS, :], ACT.Copy).then_inc(proj_evac, 1)
                    else:
                        act.activation((qp, kp, vp, up)[nb_][:, tt - 1, :], src[:, :], ACT.Copy).then_inc(proj_evac, 1)

            def queries(b):
                act.wait_ge(qb_psum, b + 1)
                if b >= QB:
                    act.wait_ge(k_used, b - QB + 1)
                act.activation(qb[:, b % QB, :], bank[6][:, :], ACT.Copy).then_inc(qb_ready, 1)

            act_engine[0] = act
            act.wait_ge(const_set, 4)
            table(ACT.Sqrt, 1)
            for g in range(4):
                act.wait_ge(m_turned, g + 1)
                act.activation(memT[:, 2 * g:2 * g + 2, :].rearrange("p k c -> p (k c)"), bank[g][:, :], ACT.Copy)\
                    .then_inc(memT_ready, 1)
            for k in range(KT):
                act.wait_ge(memT_ready, k // 2 + 1)
                act.activation(m_tmp[:, k, :], memT[:, k, :], ACT.Square).then_inc(sq_ready, 1)
            split(0)
            norm_squares(1, xT, N, range(KT), res_ready, 0)
            norm_root(0, NP, 6)
            norm_hi(0, m_hi, m_tmp, NP, range(KT))
            split(1)
            split(2)
            norm_root(1, N, 7)
            norm_hi(1, x_hi, tmp, N, range(KT))
            split(3)
            split(4)
            split(5)
            ffn(0)
            table(ACT.Sqrt, 1)
            act.wait_ge(gu_free, 2)
            act.wait_ge(xlo_ready, 2 * KT)
            head_squares(0, mem_kv[:, :, 0:256])
            head_sd(0, P, 2 * CH)
            split(U_WIN)
            split(U_WIN + 1)
            split(U_WIN + 2)
            norm_squares(2, xT, N, M_ORDER, res_ready, KT)
            norm_root(2, N, 4)
            norm_hi(2, x_hi, tmp, N, M_ORDER)
            split(U_WIN + 3)
            evac(0, [0])
            act.wait_ge(proj_evac, 1)
            head_squares(1, qs[:].unsqueeze(1))
            split(U_WIN + 4)
            head_sd(1, NS, MH)
            split(U_WIN + 5)
            split(U_WIN + 6)
            queries(0)
            split(U_WIN + 7)
            evac(0, [1, 2])
            queries(1)
            act.wait_ge(proj_evac, 3)
            head_squares(2, qp[:])
            split(U_WIN + 8)
            queries(2)
            head_sd(2, P, 2 * MH)
            split(U_WIN + 9)
            split(U_WIN + 10)
            queries(3)
            split(U_WIN + 11)
            evac(1)
            queries(4)
            act.wait_ge(proj_evac, 6)
            head_squares(3, ks[:].unsqueeze(1))
            head_sd(3, NS, MH)
            head_squares(4, kp[:])
            split(U_WIN + 12)
            head_sd(4, P, 2 * MH)
            queries(5)
            split(U_WIN + 13)
            split(U_WIN + 14)
            queries(6)
            split(U_WIN + 15)
            evac(2)
            split(U_MIX)
            queries(7)
            split(U_MIX + 1)
            evac(3, [0])
            act.wait_ge(proj_evac, 10)
            head_squares(5, us[:, 256:512].unsqueeze(1))
            act.activation(ext[0:NS, :], us[:, 0:POOL], ACT.Copy).then_inc(ext_ready, 1)
            evac(3, [1, 2])
            head_sd(5, NS, CH)
            turned(range(4))
            head_squares(6, up[:, :, 256:512])
            head_sd(6, P, 2 * CH)
            table(ACT.Exp, 2)
            for what, k in steps("scalar"):
                if what == "XM":
                    turned((4, 5))
                elif what == "POOL":
                    for pr in range(2) if k == 0 else ():
                        act.wait_ge(pooled_psum, pr + 1)
                        act.activation(sg[:, pr, :], bank[4 + pr][:, 0:N], ACT.Copy).then_inc(pooled_ready, 1)
                    for pr in range(2) if k == 1 else ():
                        act.wait_ge(pool_psum, pr + 1)
                        act.activation(tmp[:, pr, :], bank[4 + pr][:, 0:N], ACT.Copy, scale=gains[:, 32 + pr:33 + pr])\
                            .then_inc(pool_ready, 1)
                elif what == "HA":
                    act.wait_ge(nb_ready, k + 1)
                    if k >= 2:
                        act.wait_ge(pT_psum, k - 1)
                    prob = prob_pair[k % 2]
                    for h in range(2):
                        for t in range(2):
                            n = keys_of(k, t)
                            act.activation(prob[:, h, t, 0:n], bank[h][:, t * NP:t * NP + n], ACT.Exp, scale=SCALE,
                                           bias=nb[:, k % 2, h, t:t + 1], accum_out=sm[:, k % 2, h, t:t + 1]).then_inc(exp_done, 1)
                elif what == "HB":
                    act.wait_ge(pT_psum, k + 1)
                    if k:
                        act.wait_ge(pv_done, k)
                    n = 3 * P if k < MH // 2 else 4 * P
                    act.activation(probT[:, :, 0:n], banks[:, 2:4, 0:n], ACT.Copy).then_inc(probT_ready, 1)
                elif what == "HX":
                    act.wait_ge(pv_done, k + 1)
                    act.activation(tmp[:, 2 + k, NS:N], bank[7][:, 0:NP], ACT.Copy).then_inc(head_ready, 1)
                elif what == "L":
                    if k + 2 < NS + 4:
                        queries(k + 2)
                elif what == "SA":
                    act.wait_ge(lt_psum, k + 1)
                    if k:
                        act.wait_ge(p_psum, k)
                    if k != 1:
                        act.activation(rows[:, 0:512], bank[4][0:32, :], ACT.Copy).then_inc(rows_ready, 1)
                        act.activation(rows[:, 512:1024], bank[5 + k // 2][0:32, :], ACT.Copy).then_inc(rows_ready, 1)
                        act.activation(rows[:, 1024:1025], bank[7][0:32, 256:257], ACT.Copy).then_inc(rows_ready, 1)
                    else:
                        act.activation(rows[:, 0:NP], bank[4][0:32, 0:NP], ACT.Copy).then_inc(rows_ready, 1)
                elif what == "SC":
                    width = PAST + 1 if k != 1 else NP
                    act.wait_ge(smn_ready, k + 1)
                    act.activation(rows[:, 0:width], rows[:, 0:width], ACT.Exp, scale=SCALE, bias=stats[:, 15:16],
                                   accum_out=stats[:, 16:17]).then_inc(sme_ready, 1)
                elif what == "SD":
                    act.wait_ge(p_psum, k + 1)
                    if k != 1:
                        act.activation(p_cols[:, k // 2, :, :].rearrange("p t c -> p (t c)"), bank[4][:, 0:256], ACT.Copy)\
                            .then_inc(pcols_ready, 1)
                        act.activation(p_own8[:, k // 2, :], bank[7][0:NS, 320:352], ACT.Copy).then_inc(pcols_ready, 1)
                    else:
                        act.activation(pm_cols[:].rearrange("p t c -> p (t c)"), bank[4][:, 0:64], ACT.Copy)\
                            .then_inc(pcols_ready, 1)
                elif what == "Y":
                    act.wait_ge(v_used, V_DONE[k])
                    act.activation(y_rows_s[:], bank[5][:, :], ACT.Copy).then_inc(yr_ready, 1)
            act.wait_ge(ys_ready, 6)
            act.wait_ge(head_ready, 6)
            act.wait_ge(pool_ready, 2)
            for m in range(KT):
                act.activation(x_hi[:, m, :], tmp[:, m, :], ACT.Copy).then_inc(cat_hi, 1)
            table(ACT.Sqrt, 1)
            for r in range(2, KT + 2):
                split(U_MIX + r)
            norm_squares(3, xT, N, M_ORDER, res_ready, 2 * KT)
            norm_root(3, N, 4)
            norm_hi(3, x_hi, tmp, N, M_ORDER)
            ffn(1)
            for g in range(1, 6, 2):
                y_rows(act, g)


        @block.vector
        def _(vec):
            chained = [0]

            def chain(ins):
                chained[0] += 1
                ins.then_inc(vec_step, 1)
                vec.wait_ge(vec_step, chained[0])

            def split(n0, j=0, i=0):
                n = n0 + j
                vec.wait_ge(hi_ready, 4 * i + n + 1)
                vec.tensor_tensor(w_lo[:, n % RING, :], raw[:, n % RING, :], w_hi[:, n % RING, :].bitcast(F32),
                                  ALU.subtract).then_inc(lo_ready, 1)

            def norm(inst, src, g0, dst, cols, order):
                vec.wait_ge(root_ready, inst + 1)
                vec.reciprocal(rstd[:, 0:cols], root[:, 0:cols]).then_inc(rstd_ready, 1)
                vec.wait_ge(rstd_ready, inst + 1)
                for m in order:
                    vec.scalar_tensor_tensor(out=dst[:, m, 0:cols], in0=src[:, m, :], scalar=gains[:, g0 + m:g0 + m + 1],
                                             in1=rstd[:, 0:cols], op0=ALU.mult, op1=ALU.mult).then_inc(xn_ready, 1)

            def residual(inst, last, weight):
                for idx, m in enumerate(M_ORDER):
                    if idx < KT - 1:
                        vec.wait_ge(out_done, (KT - 1) * inst + idx + 1)
                    else:
                        vec.wait_ge(w_used, last + 1)
                    vec.scalar_tensor_tensor(out=xT[:, m, :], in0=bank[m][:, 0:N], scalar=weight, in1=xT[:, m, :],
                                             op0=ALU.mult, op1=ALU.add).then_inc(res_ready, 1)

            def ffn(f):
                n0 = (U_FFN1, U_FFN2)[f]
                with vec.Fori(0, HT // 2) as i:
                    for s in range(2):
                        split(n0 + 2 + 2 * s, 0, i)
                        split(n0 + 3 + 2 * s, 0, i)
                        c = i * 2 + s
                        vec.wait_ge(silu_ready, c + (HT * f + 1))
                        vec.tensor_tensor(h_tmp[:, s, :], sg[:, s, :], bank[2 * s + 1][:, 0:N], ALU.mult)\
                            .then_inc(gu_free, 1)
                        vec.wait_ge(gu_free, c + (HT * f + 3))
                        vec.tensor_copy(h_hi[:, ds(c, 1), :].rearrange("p a n -> p (a n)"), h_tmp[:, s, :]).then_inc(hhi_ready, 1)
                        vec.wait_ge(hhi_ready, c + (HT * f + 1))
                        vec.tensor_tensor(h_lo[:, ds(c, 1), :].rearrange("p a n -> p (a n)"), h_tmp[:, s, :],
                                          h_hi[:, ds(c, 1), :].rearrange("p a n -> p (a n)").bitcast(F32), ALU.subtract)\
                            .then_inc(h_ready, 1)
                with vec.Fori(0, 5) as i:
                    for j in range(4):
                        split(n0 + 2 * HT + LEAD, j, i)

            def heads_var(inst, nrows, nt, nh):
                vec.wait_ge(sqh_ready, inst + 1)
                if inst:
                    vec.wait_ge(sd_ready, inst)
                chain(vec.tensor_reduce(ss_h[0:nrows, 0:nt * nh].rearrange("p (t h) -> p t h", t=nt),
                                        (sq_h if inst else tmp)[0:nrows, 0:nt, 0:nh * HD].rearrange("p t (h d) -> p t h d", d=HD), AX.X, ALU.add))
                vec.tensor_scalar(var_h[0:nrows, 0:nt * nh], ss_h[0:nrows, 0:nt * nh], 1.0 / HD, EPS, ALU.mult, ALU.add)\
                    .then_inc(var_ready, 1)

            def heads_scale(inst, buf, nt, nh, gain, rope_at):
                nrows = buf.shape[0]
                vec.wait_ge(sd_ready, inst + 1)
                chain(vec.reciprocal(rs_h[0:nrows, 0:nt * nh], sd_h[0:nrows, 0:nt * nh]))
                heads = buf.rearrange("p t (h d) -> p t h d", d=HD)
                for step in range(2):
                    for t in range(nt):
                        r = rs_h[0:nrows, t * nh:(t + 1) * nh].unsqueeze(2).to_broadcast([nrows, nh, HD]) if step == 0 \
                            else head_gain[0:nrows, gain, :].unsqueeze(1).to_broadcast([nrows, nh, HD])
                        one = vec.tensor_tensor(heads[:, t], heads[:, t], r, ALU.mult)
                        if step and rope_at is None and t == nt - 1:
                            one.then_inc(nrm_ready, 1)
                        elif t < nt - 1:
                            one.then_inc(vec_step, 1)
                            chained[0] += 1
                        else:
                            chain(one)
                if rope_at is None:
                    return
                x1, x2 = heads[:, :, :, 0:HALF_ROT], heads[:, :, :, HALF_ROT:ROT]
                cs = [rope[0:nrows, q, rope_at:rope_at + nt, :].unsqueeze(2).to_broadcast([nrows, nt, nh, HALF_ROT])
                      for q in range(2)]
                r = [rot[0:nrows, q, 0:nt, :].rearrange("p t (h d) -> p t h d", h=nh) for q in range(4)]
                for q, (x, cos_sin) in enumerate(((x1, cs[0]), (x2, cs[1]), (x2, cs[0]), (x1, cs[1]))):
                    one = vec.tensor_tensor(r[q], x, cos_sin, ALU.mult)
                    if q < 3:
                        one.then_inc(vec_step, 1)
                        chained[0] += 1
                chain(one)
                vec.tensor_tensor(x1, r[0], r[1], ALU.subtract)
                vec.tensor_tensor(x2, r[2], r[3], ALU.add).then_inc(nrm_ready, 1)

            def own_keys(hf):
                if hf == 0:
                    chain(vec.tensor_tensor(y_rows_s[0:NS, :], qs[:], ks[:], ALU.mult))
                    chain(vec.tensor_reduce(own8[:], y_rows_s[0:NS, :].rearrange("p (h d) -> p h d", d=HD), AX.X, ALU.add))
                else:
                    vec.wait_ge(lt_psum, 1)
                vec.tensor_tensor(own_e[:], delta[:, 4 * hf:4 * hf + 4, :], own8[:].unsqueeze(1).to_broadcast([NS, 4, MH]),
                                  ALU.mult).then_inc(own_ready, 1)

            def key_logits(b):
                if b < NS:
                    slot = kv_wait(vec, "k", b)
                    vec.wait_ge(qb_ready, b + 1)
                    part = kv[:, slot, GP_PAGES[b] * 512:PAGES * 512].rearrange("p (t c) -> p t c", c=512)
                    chain(vec.tensor_tensor(part, part, qb[:, b % QB, :].unsqueeze(1)
                                            .to_broadcast([P, PAGES - GP_PAGES[b], 512]), ALU.mult))
                    vec.tensor_reduce(logits[:, GP_PAGES[b]:PAGES, b, :],
                                      part.rearrange("p t (h d) -> p t h d", d=HD), AX.X, ALU.add)
                    vec.wait_ge(gp_done, b + 1)
                    part = kv[:, slot, 0:GP_PAGES[b] * 512].rearrange("p (t h d) -> p t h d", d=HD, h=MH)
                    vec.tensor_reduce(logits[:, 0:GP_PAGES[b], b, :], part, AX.X, ALU.add).then_inc(k_used, 1)
                else:
                    g = b - NS
                    slot = KV_AT[("mk", 0)] % KV_SLOTS
                    vec.wait_ge(gp_done, b + 1)
                    m_keys = kv[:, slot, g * 1024:(g + 1) * 1024].rearrange("p (b t h d) -> p t b h d", b=2, t=2, h=CH)
                    for t in range(2):
                        red = vec.tensor_reduce(logits_m[:, t, 2 * g:2 * g + 2, :], m_keys[:, t], AX.X, ALU.add)
                    red.then_inc(k_used, 1)

            vec.wait_ge(g_turned, 1)
            vec.tensor_copy(gains[:], bank[4][:, 0:34]).then_inc(gains_ready, 1)
            for m in range(KT):
                vec.wait_ge(x_turned, m + 1)
                vec.tensor_copy(xT[:, m, :], bank[X_BANKS[m]][:, 0:N]).then_inc(res_ready, 1)
            split(0)
            vec.wait_ge(gains_ready, 1)
            norm(0, memT, 16, m_tmp, NP, range(KT))
            split(1)
            split(2)
            vec.wait_ge(xhi_ready, KT)
            norm(1, xT, 0, tmp, N, range(KT))
            split(3)
            split(4)
            split(5)
            vec.wait_ge(kvm_done, 1)
            vec.tensor_copy(mem_kv[:, 0, :], bank[4][:, :]).then_inc(gu_free, 1)
            vec.wait_ge(w_used, 4)
            vec.tensor_copy(mem_kv[:, 1, :], bank[5][:, :]).then_inc(gu_free, 1)
            ffn(0)
            vec.wait_ge(c_loaded, 16 * 12)
            vec.tensor_copy(ident_b[:], ident[:]).then_inc(mask_ready, 1)
            vec.tensor_copy(causal_b[:], causal[:]).then_inc(mask_ready, 1)
            heads_var(0, P, 2, CH)
            heads_scale(0, mem_kv[:, :, 0:256], 2, CH, 3, None)
            split(U_WIN)
            split(U_WIN + 1)
            residual(0, U_WIN - 1, 0.5)
            split(U_WIN + 2)
            norm(2, xT, 8, tmp, N, M_ORDER)
            split(U_WIN + 3)
            heads_var(1, NS, 1, MH)
            split(U_WIN + 4)
            heads_scale(1, qs[:].unsqueeze(1), 1, MH, 0, 2)
            for r in range(5, 8):
                split(U_WIN + r)
            key_logits(0)
            split(U_WIN + 8)
            heads_var(2, P, 2, MH)
            split(U_WIN + 9)
            heads_scale(2, qp[:], 2, MH, 0, 0)
            split(U_WIN + 10)
            key_logits(1)
            split(U_WIN + 11)
            heads_var(3, NS, 1, MH)
            key_logits(2)
            heads_scale(3, ks[:].unsqueeze(1), 1, MH, 1, 2)
            heads_var(4, P, 2, MH)
            split(U_WIN + 12)
            heads_scale(4, kp[:], 2, MH, 1, 0)
            split(U_WIN + 13)
            key_logits(3)
            own_keys(0)
            split(U_WIN + 14)
            split(U_WIN + 15)
            key_logits(4)
            key_logits(5)
            heads_var(5, NS, 1, CH)
            heads_scale(5, us[:, 256:512].unsqueeze(1), 1, CH, 2, None)
            heads_var(6, P, 2, CH)
            heads_scale(6, up[:, :, 256:512], 2, CH, 2, None)
            for what, k in steps("vector"):
                if what == "L":
                    key_logits(k)
                elif what == "HA":
                    vec.wait_ge(sc_ready, k + 1)
                    if k < MH // 2:
                        vec.tensor_reduce(mx[:, k % 2, :, 0], banks[:, 0:2, 0:P], AX.X, ALU.max).then_inc(vec_step, 1)
                        chained[0] += 1
                        chain(vec.tensor_reduce(mx[:, k % 2, :, 1], banks[:, 0:2, NP:2 * NP], AX.X, ALU.max))
                    else:
                        chain(vec.tensor_reduce(mx[:, k % 2], banks[:, 0:2, :].rearrange("p h (t c) -> p h t c", t=2), AX.X, ALU.max))
                    vec.tensor_scalar(nb[:, k % 2], mx[:, k % 2], -SCALE, None, ALU.mult).then_inc(nb_ready, 1)
                elif what == "HB":
                    vec.wait_ge(exp_done, 4 * k + 4)
                    prob = prob_pair[k % 2]
                    r = rc[:, k % 2]
                    chain(vec.reciprocal(r, sm[:, k % 2]))
                    for t in range(2):
                        n = keys_of(k, t)
                        some = vec.tensor_tensor(prob[:, :, t, 0:n], prob[:, :, t, 0:n],
                                                 r[:, :, t:t + 1].to_broadcast([P, 2, n]), ALU.mult)
                    some.then_inc(prob_ready, 1)
                elif what == "SA" and k == 2:
                    own_keys(1)
                elif what == "SB":
                    vec.wait_ge(rows_ready, ROWS_DONE[k])
                    if k:
                        vec.wait_ge(sme_ready, k)
                    if k != 1:
                        blocks = rows[:, 0:PAST].rearrange("p (b c) -> p b c", b=BLOCKS)
                        chain(vec.tensor_reduce(stats[:, 0:4], blocks, AX.X, ALU.add))
                        chain(vec.tensor_reduce(stats[:, 4:5], stats[:, 0:4], AX.X, ALU.min))
                        chain(vec.scalar_tensor_tensor(out=stats[:, 5:9], in0=stats[:, 0:4], scalar=stats[:, 4:5],
                                                       in1=rank[:], op0=ALU.is_equal, op1=ALU.mult))
                        chain(vec.tensor_reduce(stats[:, 9:10], stats[:, 5:9], AX.X, ALU.max))
                        chain(vec.tensor_scalar(stats[:, 10:14], stats[:, 5:9], stats[:, 9:10], NEG, ALU.is_equal, ALU.mult))
                        chain(vec.tensor_tensor(blocks, blocks, stats[:, 10:14].unsqueeze(2).to_broadcast([32, BLOCKS, BLOCK]),
                                                ALU.add))
                    width = PAST + 1 if k != 1 else NP
                    chain(vec.tensor_reduce(stats[:, 14:15], rows[:, 0:width], AX.X, ALU.max))
                    vec.tensor_scalar(stats[:, 15:16], stats[:, 14:15], -SCALE, None, ALU.mult).then_inc(smn_ready, 1)
                elif what == "SC":
                    width = PAST + 1 if k != 1 else NP
                    vec.wait_ge(sme_ready, k + 1)
                    chain(vec.reciprocal(stats[:, 17:18], stats[:, 16:17]))
                    scaled = vec.tensor_scalar(rows[:, 0:width], rows[:, 0:width], stats[:, 17:18], None, ALU.mult)
                    if k != 1:
                        chain(scaled)
                        if k:
                            vec.wait_ge(p_psum, 1)
                        vec.tensor_scalar(p_own[:], ident[0:32, 0:32], rows[:, PAST:PAST + 1], None, ALU.mult)\
                            .then_inc(p_ready, 1)
                    else:
                        scaled.then_inc(p_ready, 1)
                elif what == "Y":
                    vec.wait_ge(yr_psum, k + 1)
                    for two in range(2):
                        r = slice(HD * two, HD * two + HD)
                        if k != 1:
                            for b4 in range(4):
                                first = b4 * (P + MH) + two
                                some = vec.tensor_copy(tmp[r, 2:6, 2 * k + b4],
                                                       bank[5][r, first:first + 3 * 34 + 1:34])
                        else:
                            for hp in range(2):
                                first = 34 * hp + two
                                some = vec.tensor_copy(tmp[r, 6 + hp, 0:NS], bank[5][r, first:first + 7 * 68 + 1:68])
                        some.then_inc(ys_ready, 1)
            for m in range(KT):
                vec.wait_ge(cat_hi, m + 1)
                vec.tensor_tensor(x_lo[:, m, :], tmp[:, m, :], x_hi[:, m, :].bitcast(F32), ALU.subtract).then_inc(cat_lo, 1)
            vec.wait_ge(lo_ready, U_MIX + 2)
            for r in range(2, KT + 2):
                split(U_MIX + r)
            residual(1, U_FFN2 - 1, 1.0)
            norm(3, xT, 24, tmp, N, M_ORDER)
            vec.wait_ge(mid_stored, 16 * MID_STORES)
            ffn(1)
            residual(2, U_END - 1, 0.5)
            for g in range(0, 6, 2):
                y_rows(vec, g)

        @block.tensor
        def _(pe):
            def three(out, lhs, rhs, start, stop):
                pe.matmul(out, lhs[0], rhs[0], start=start, stop=False)
                pe.matmul(out, lhs[0], rhs[1], start=False, stop=False)
                return pe.matmul(out, lhs[1], rhs[0], start=False, stop=stop)

            def weights(slot, c0, c1):
                return w_hi[:, slot, c0:c1], w_lo[:, slot, c0:c1]

            def sum_squares(inst, cols, order, bk):
                for idx, m in enumerate(order):
                    pe.wait_ge(sq_ready, KT * inst + idx + 1)
                    mm = pe.matmul(bank[bk][:, 0:cols], ones[:], (tmp if inst else m_tmp)[:, m, 0:cols],
                                   start=(idx == 0), stop=(idx == KT - 1))
                mm.then_inc(ss_ready, 1)

            def turn(out, in_, k=P):
                return pe.transpose(out, in_, ident[0:k, 0:k])

            def ffn(f):
                n0, inst = (U_FFN1, U_FFN2)[f], (1, 3)[f]
                order = list((range(KT), M_ORDER)[f])
                with pe.Fori(0, HT // 2) as i:
                    for s in range(2):
                        pe.wait_ge(gu_free, i * 2 + (s + HT * f + 1))
                        for half in range(2):
                            j = 2 * s + half
                            pe.wait_ge(lo_ready, i * 4 + (n0 + j + 1))
                            for idx, k in enumerate(order):
                                if j == 0:
                                    pe.wait_ge(xlo_ready, KT * inst + idx + 1)
                                mm = three(bank[j][:, 0:N], weights((n0 + j) % RING, k * P, (k + 1) * P),
                                           (x_hi[:, k, :], x_lo[:, k, :]), idx == 0, idx == KT - 1)
                            mm.then_inc(w_used, 1)
                n0 += 2 * HT
                hidden = lambda k: tuple(h[:, ds(k, 1), :].rearrange("p a n -> p (a n)") for h in (h_hi, h_lo))
                for k in range(2):
                    outer(n0 + k, n0 + k, hidden(k), k == 0, False, f if k == 0 else None,
                          lambda k=k: pe.wait_ge(h_ready, HT * f + k + 1))
                with pe.Fori(0, 4) as i:
                    for j in range(4):
                        outer(n0 + 2 + j, i * 4 + (n0 + 2 + j), hidden(i * 4 + (2 + j)), False, False, None,
                              lambda j=j: pe.wait_ge(h_ready, i * 4 + (HT * f + 3 + j)))
                for k in range(HT - 4, HT):
                    outer(n0 + k, n0 + k, hidden(k), False, k == HT - 1, None, lambda k=k: pe.wait_ge(h_ready, HT * f + k + 1))

            def outer(n, unit, x, start, stop, first_of, ready):
                pe.wait_ge(lo_ready, unit + 1)
                ready()
                for idx, m in enumerate(M_ORDER):
                    if first_of is not None and m == 0:
                        pe.wait_ge(gu_free, 2 + HT * (first_of + 1))
                    mm = three(bank[m][:, 0:N], weights(n % RING, m * P, (m + 1) * P), x, start, stop)
                    if stop and idx < KT - 1:
                        mm.then_inc(out_done, 1)
                mm.then_inc(w_used, 1)

            def project(nb_, j, tts=range(3)):
                r = 4 * nb_ + j
                if j == 0 and nb_ >= 2:
                    pe.wait_ge(proj_evac, 3 * (nb_ - 1))
                pe.wait_ge(lo_ready, U_WIN + r + 1)
                for tt in tts:
                    c0 = (0, NS, NS + P)[tt]
                    for kk in range(2):
                        k = 2 * J_ORDER[j] + kk
                        if nb_ == 0 and tt == 0:
                            pe.wait_ge(xlo_ready, 2 * KT + 2 * j + kk + 1)
                        mm = three(bank[3 * (nb_ % 2) + tt][:, :], (x_hi[:, k, c0:c0 + P], x_lo[:, k, c0:c0 + P]),
                                   weights((U_WIN + r) % RING, kk * 512, kk * 512 + 512), j + kk == 0, j + kk == 4)
                    if j == 3 and tt < 2:
                        mm.then_inc(proj_done, 1)
                if 2 in tts:
                    mm.then_inc(w_used, 1)

            def turns(groups):
                pe.wait_ge(nrm_ready, 5 if groups[0] == 0 else 7)
                for g in groups:
                    if g == 0:
                        pe.wait_ge(proj_evac, 9)
                    if g == 3:
                        pe.wait_ge(qkT_ready, 1)
                    if g == 4:
                        pe.wait_ge(qkT_ready, 3)
                    if g == 5:
                        pe.wait_ge(proj_evac, 12)
                    src, c0 = ((qp, 0), (qp, 256), (kp, 0), (kp, 256), (up, 256), (mem_kv, 0))[g]
                    for hh in range(2):
                        for t in range(2):
                            mm = turn(bank[TURN_BANKS[g]][:, hh * NP + t * P:hh * NP + (t + 1) * P],
                                      src[:, t, c0 + hh * P:c0 + (hh + 1) * P])
                    mm.then_inc(qk_turned, 1)

            def queries(b):
                pe.wait_ge(nrm_ready, 2 if b < NS else 6)
                if b:
                    pe.wait_ge(qb_ready, b)
                if b < NS:
                    pe.matmul(bank[6][:, :], delta[:, b, 0:1].to_broadcast([NS, P]), qs[:], start=True, stop=True)\
                        .then_inc(qb_psum, 1)
                else:
                    for two in range(2):
                        mm = pe.matmul(bank[6][:, two * 256:two * 256 + 256],
                                       delta[:, 2 * (b - NS) + two, 0:1].to_broadcast([NS, P]), us[:, 256:512],
                                       start=True, stop=True)
                    mm.then_inc(qb_psum, 1)

            pe.wait_ge(id_loaded, 16)
            pe.wait_ge(g_loaded, 16 * 5)
            turn(bank[4][:, 0:34], g_rows[:], 34).then_inc(g_turned, 1)
            pe.wait_ge(m_loaded, 16)
            for g in range(4):
                for k in range(2):
                    for t in range(2):
                        mm = turn(bank[g][:, k * NP + t * P:k * NP + (t + 1) * P], m_rows[:, t, (2 * g + k) * P:(2 * g + k + 1) * P])
                mm.then_inc(m_turned, 1)
            pe.wait_ge(x_loaded, 32)
            for m in range(KT):
                bk = X_BANKS[m]
                if bk < 4:
                    pe.wait_ge(memT_ready, bk + 1)
                if bk == 4:
                    pe.wait_ge(gains_ready, 1)
                turn(bank[bk][:, 0:NS], x_rows[0:NS, 0, m * P:(m + 1) * P], NS)
                for t in range(2):
                    mm = turn(bank[bk][:, NS + t * P:NS + (t + 1) * P], x_rows[:, 1 + t, m * P:(m + 1) * P])
                mm.then_inc(x_turned, 1)
            pe.wait_ge(const_set, 4)
            pe.wait_ge(res_ready, KT)
            sum_squares(0, NP, range(KT), 6)
            sum_squares(1, N, range(KT), 7)
            for j in range(4):
                pe.wait_ge(lo_ready, j + 1)
                for t in range(2):
                    for kk in range(2):
                        k = 2 * j + kk
                        if t == 0:
                            pe.wait_ge(xlo_ready, k + 1)
                        mm = three(bank[4 + t][:, :], (m_hi[:, k, t * P:(t + 1) * P], m_lo[:, k, t * P:(t + 1) * P]),
                                   weights(j, kk * 512, kk * 512 + 512), k == 0, k == KT - 1)
                    if j == 3 and t == 0:
                        mm.then_inc(kvm_done, 1)
                mm.then_inc(w_used, 1)
            ffn(0)
            sum_squares(2, N, M_ORDER, 4)
            pe.wait_ge(c_loaded, 16 * 12)
            for j in range(4):
                project(0, j, [0])
            for j in range(4):
                project(0, j, [1, 2])
                if j == 2:
                    queries(0)
            queries(1)
            for nb_ in range(1, 4):
                for j in range(4):
                    project(nb_, j)
                    r = 4 * nb_ + j
                    if r in QUERY_AT:
                        queries(2 + QUERY_AT.index(r))
            turns((0, 1, 2, 3))
            pairs_done = own_turned = own_back = 0
            for what, k in steps("tensor"):
                if what == "XM":
                    turns((4, 5))
                elif what == "POOL" and k == 0:
                    pe.wait_ge(proj_evac, 12)
                    pe.wait_ge(ext_ready, 1)
                    for g in range(4):
                        out, r = bank[4 + g // 2], slice(HD * (g % 2), HD * (g % 2) + HD)
                        u0, u1 = (up[:, t, g * HD:(g + 1) * HD] for t in range(2))
                        pe.matmul(out[r, NS:NS + P], u0, band[:, g, 0:P], start=True, stop=True)
                        pe.matmul(out[r, NS + P:N], u1, band[:, g, P + EDGE:], start=True, stop=False)
                        pe.matmul(out[r, NS + P:NS + P + EDGE], u0, band[:, g, P:P + EDGE], start=False, stop=True)
                        mm = pe.matmul(out[r, 0:NS], ext[:, g * HD:(g + 1) * HD], samp[:, g, :], start=True, stop=True)
                        if g % 2:
                            mm.then_inc(pooled_psum, 1)
                elif what == "POOL":
                    pe.wait_ge(poolw_loaded, 16 * 4)
                    for pr in range(2):
                        pe.wait_ge(pooled_ready, pr + 1)
                        pe.matmul(bank[4 + pr][:, 0:N], pool_wd[:, pr, :], sg[:, pr, :], start=True, stop=True).then_inc(pool_psum, 1)
                elif what == "HA":
                    if k in (0, MH // 2):
                        pe.wait_ge(qkT_ready, 4 if k == 0 else 6)
                    if k == 0:
                        pe.wait_ge(mask_ready, 2)
                    else:
                        pe.wait_ge(exp_done, 4 * k)
                    q_, k_, hp = (qT, kT, k) if k < MH // 2 else (qmT, mkT, k - MH // 2)
                    masked = k < MH // 2
                    for t in range(2):
                        n = keys_of(k, t)
                        for h in range(2):
                            r = slice(HD * h, HD * h + HD)
                            mm = pe.matmul(bank[h][:, t * NP:t * NP + n], q_[r, hp, t * P:(t + 1) * P], k_[r, hp, 0:n],
                                           start=True, stop=not masked)
                        if masked:
                            c0 = t * (NP + P)
                            for h in range(2):
                                mm = pe.matmul(bank[h][:, c0:c0 + P], ident_b[:], causal_b[:], start=False, stop=True)
                    mm.then_inc(sc_ready, 1)
                elif what == "HB":
                    pe.wait_ge(prob_ready, k + 1)
                    if k:
                        pe.wait_ge(probT_ready, k)
                    else:
                        pe.wait_ge(qkT_ready, 6)
                    prob = prob_pair[k % 2]
                    blocks = ((0, 0, 0), (1, 0, 1), (1, 1, 2)) if k < MH // 2 else ((0, 0, 0), (1, 0, 1), (0, 1, 2), (1, 1, 3))
                    for h in range(2):
                        for t, kt, at_ in blocks:
                            mm = turn(bank[2 + h][:, at_ * P:(at_ + 1) * P], prob[:, h, t, kt * P:(kt + 1) * P])
                    mm.then_inc(pT_psum, 1)
                elif what == "HX":
                    pairs_done = k + 1
                    pe.wait_ge(probT_ready, k + 1)
                    if k:
                        pe.wait_ge(head_ready, k)
                    if own_turned:
                        pe.wait_ge(rows_ready, ROWS_DONE[own_turned - 1])
                    if own_back:
                        pe.wait_ge(pcols_ready, PCOLS_DONE[own_back - 1])
                    for kt in range(2):
                        for h in range(2):
                            head = 2 * k + h
                            v_ = vp[:, kt, head * HD:(head + 1) * HD] if k < MH // 2 else \
                                mem_kv[:, kt, 256 + (head - MH) * HD:256 + (head - MH + 1) * HD]
                            q0 = P if kt and k < MH // 2 else 0
                            mm = pe.matmul(bank[7][HD * h:HD * h + HD, q0:NP], v_, probT[:, h, 2 * P:2 * P + NP - q0] if kt
                                           else probT[:, h, 0:NP], start=(kt == 0), stop=(kt == 1))
                    mm.then_inc(pv_done, 1)
                elif what == "L":
                    if k + 2 < NS + 4:
                        queries(k + 2)
                elif what == "SA":
                    if k == 0:
                        pe.wait_ge(pool_ready, 2)
                    else:
                        pe.wait_ge(pcols_ready, PCOLS_DONE[k - 1])
                    if k != 1:
                        pe.wait_ge(own_ready, k // 2 + 1)
                        if pairs_done:
                            pe.wait_ge(head_ready, pairs_done)
                        pe.matmul(bank[7][0:32, 256:257], own_e[:].rearrange("p b h -> p (b h)"), ones[0:NS, 0:1], start=True, stop=True)
                        pe.wait_ge(k_used, 2 * k + 4)
                        own_turned = k + 1
                        if k:
                            pe.wait_ge(qb_ready, NS + 4)
                        for t in range(PAGES):
                            mm = turn(bank[4 if t < 4 else 5 + k // 2][0:32, (t % 4) * P:(t % 4 + 1) * P],
                                      logits[:, t, 2 * k:2 * k + 4, :].rearrange("p b h -> p (b h)"))
                    else:
                        pe.wait_ge(k_used, NS + 4)
                        for t in range(2):
                            mm = turn(bank[4][0:32, t * P:(t + 1) * P], logits_m[:, t].rearrange("p b h -> p (b h)"))
                    mm.then_inc(lt_psum, 1)
                elif what == "SD":
                    pe.wait_ge(p_ready, k + 1)
                    for t in range(PAGES if k != 1 else 2):
                        mm = turn(bank[4][:, t * 32:(t + 1) * 32], rows[:, t * P:(t + 1) * P], 32)
                    if k != 1:
                        if pairs_done:
                            pe.wait_ge(head_ready, pairs_done)
                        own_back = k + 1
                        mm = pe.matmul(bank[7][0:NS, 320:352], back[:, k // 2, :], p_own[:], start=True, stop=True)
                    mm.then_inc(p_psum, 1)
                elif what == "V":
                    if k == 0:
                        pe.wait_ge(rows_ready, 3)
                    if k == "mem":
                        pe.wait_ge(pcols_ready, PCOLS_DONE[1])
                        pe.wait_ge(ys_ready, 2)
                        slot = kv_wait(pe, "mv", 0)
                        for b2 in range(4):
                            for t in range(2):
                                for two in range(2):
                                    for hp in range(2):
                                        part = 32 * (2 * two + hp)
                                        c0 = (2 * b2 + two) * 512 + t * 256 + hp * P
                                        mm = pe.matmul(bank[5][part:part + 32, b2 * P:(b2 + 1) * P], pm_cols[:, t, :],
                                                       kv[:, slot, c0:c0 + P], start=(t == 0), stop=(t == 1))
                    else:
                        half, b4 = k // 4, k % 4
                        pe.wait_ge(pcols_ready, PCOLS_DONE[2 * half])
                        if k == 4:
                            pe.wait_ge(ys_ready, 4)
                        slot = kv_wait(pe, "v", k)
                        for t in range(PAGES + 1):
                            for hp in range(4):
                                out = bank[5][32 * hp:32 * hp + 32, b4 * P:(b4 + 1) * P]
                                if t < PAGES:
                                    c0 = t * 512 + hp * P
                                    pe.matmul(out, p_cols[:, half, t, :], kv[:, slot, c0:c0 + P], start=(t == 0), stop=False)
                                else:
                                    mm = pe.matmul(out, p_own8[:, half, :], vs[:, hp * P:(hp + 1) * P], start=False, stop=True)
                    mm.then_inc(v_used, 1)
                elif what == "Y":
                    pe.wait_ge(yr_ready, k + 1)
                    for b4 in range(4):
                        mm = turn(bank[5][:, b4 * P:(b4 + 1) * P], y_rows_s[:, b4 * P:(b4 + 1) * P])
                    mm.then_inc(yr_psum, 1)
            for k in range(KT):
                outer(U_MIX + k, U_MIX + k, (x_hi[:, k, :], x_lo[:, k, :]), k == 0, k == KT - 1, None,
                      lambda k=k: pe.wait_ge(cat_lo, k + 1))
            sum_squares(3, N, M_ORDER, 4)
            ffn(1)
            for g, (rows_, half) in enumerate(Y_GROUPS):
                pe.wait_ge(res_ready, 3 * KT + (4 if half else KT))
                c0, n = (0, NS, NS + P)[rows_], NS if rows_ == 0 else P
                for q in range(4):
                    mm = turn(bank[Y_BANKS[g]][0:n, q * P:(q + 1) * P], xT[:, 4 * half + q, c0:c0 + n])
                mm.then_inc(y_turned, 1)


_INS = ["x_prompt", "x_sample", "mem_prompt", "cache_k", "cache_v", "cache_mem_k", "cache_mem_v", "state_pool", "page_table",
        "ffn1_norm", "ffn1_w_in", "ffn1_w_out", "mix_norm", "w_in", "pool_w", "pool_scale", "q_norm", "k_norm",
        "mem_norm", "mem_w_kv", "mem_q_norm", "mem_k_norm", "w_out", "ffn2_norm", "ffn2_w_in", "ffn2_w_out"]
_OUTS = [("y_prompt", (1, NP, D)), ("y_sample", (NS, 1, D)), ("k_out", (1, 1, NP, MH, HD)), ("v_out", (1, 1, NP, MH, HD)),
         ("mk_out", (1, 1, NP, CH, HD)), ("mv_out", (1, 1, NP, CH, HD)), ("buf_out", (1, 1, BUF, POOL)),
         ("ks_out", (1, NS, 1, MH, HD)), ("vs_out", (1, NS, 1, MH, HD)), ("state_out", (1, NS, BUF, POOL))]


def kernel(**inputs):
    import concourse.bacc as bacc
    from concourse.bass_utils import run_bass_kernel_spmd

    nc = bacc.Bacc("TRN2", target_bir_lowering=False, num_devices=1, dynamic_dma_scratch_size=1024)
    arrays, views = {}, {}
    given = {name: np.ascontiguousarray(inputs[name]) for name in _INS}
    for name, arr in list(given.items()) + list(shape_constants().items()):
        arrays[f"in_{name}"] = arr
        views[name] = nc.dram_tensor(f"in_{name}", arr.shape, mybir.dt.from_np(arr.dtype), kind="ExternalInput").ap()
    for name, shape in _OUTS:
        views[name] = nc.dram_tensor(f"out_{name}", shape, F32, kind="ExternalOutput").ap()
    layer(nc, views)
    r = run_bass_kernel_spmd(nc, [arrays], core_ids=[0])
    return tuple(r.results[0][f"out_{name}"] for name, _ in _OUTS)
```
